# Optimizing a Trainium2 kernel written in Bass

```python
import math
import jax, jax.numpy as jnp
from jax import lax
import numpy as np

D_MODEL = 1024
BATCH = 1
SEQ = 1024
DEPTH = 1

BRANCH_WIDTH = D_MODEL // 2
N_BRANCH = 3
HG_HEADS = 4
HG_HEAD_DIM = BRANCH_WIDTH // HG_HEADS
HG_CHUNK = 16
S5_GROUP_CH = 16
S5_GROUPS = BRANCH_WIDTH // S5_GROUP_CH
S5_STATE = 64
RG_BLOCKS = 4
RG_BLOCK_W = BRANCH_WIDTH // RG_BLOCKS
RG_CONV = 4
RG_C = 8.0
IN_COLS = 4 * BRANCH_WIDTH + BRANCH_WIDTH + 2 * BRANCH_WIDTH + N_BRANCH * D_MODEL
N_EXPERTS = 64
N_EXPERT_GROUPS = 8
TOPK_GROUPS = 4
TOP_K = 8
EXPERT_HIDDEN = D_MODEL // 4
ROUTED_SCALE = 2.5
MOE_BLOCK = 128
DN_ALPHA = (2 * DEPTH) ** 0.25
DN_BETA = (8 * DEPTH) ** -0.25
LN_EPS = 1e-5
RMS_EPS = 1e-6

kernel_name = 'hybrid_hgrn2_s5_rglru_moe_deepnorm'

def _layernorm(x, g, b):
    xf = x.astype(jnp.float32)
    mu = jnp.mean(xf, axis=-1, keepdims=True)
    var = jnp.mean(jnp.square(xf - mu), axis=-1, keepdims=True)
    y = (xf - mu) * lax.rsqrt(var + LN_EPS) * g.astype(jnp.float32) + b.astype(jnp.float32)
    return y.astype(x.dtype)

def _lin_combine(left, right):
    a_l, b_l = left
    a_r, b_r = right
    return a_l * a_r, a_r * b_l + b_r

def _hgrn2(q, f_pre, v, g, lb, norm_w):
    Bn, S, _ = q.shape
    nc = S // HG_CHUNK
    f32 = jnp.float32

    def heads(t):
        return t.reshape(Bn, nc, HG_CHUNK, HG_HEADS, HG_HEAD_DIM).transpose(0, 3, 1, 2, 4)

    lbf = lb.astype(f32)
    f = lbf + (1.0 - lbf) * jax.nn.sigmoid(f_pre.astype(f32))
    qh = heads(jax.nn.silu(q.astype(f32)))
    kh = heads(1.0 - f)
    vh = heads(v.astype(f32))
    bcum = jnp.cumsum(heads(jnp.log(f)), axis=3)
    causal = jnp.tril(jnp.ones((HG_CHUNK, HG_CHUNK), dtype=bool))
    diff = bcum[:, :, :, :, None, :] - bcum[:, :, :, None, :, :]
    decay = jnp.exp(jnp.where(causal[:, :, None], diff, -jnp.inf))
    scores = jnp.sum(qh[:, :, :, :, None, :] * kh[:, :, :, None, :, :] * decay, axis=-1)
    o_intra = jnp.einsum('bhnts,bhnsv->bhntv', scores, vh)
    b_last = bcum[:, :, :, -1, :]
    kv = jnp.einsum('bhnsd,bhnsv->bhndv', kh * jnp.exp(b_last[:, :, :, None, :] - bcum), vh)

    def step(state, inp):
        dec, upd = inp
        return dec[..., None] * state + upd, state

    init = jnp.zeros((Bn, HG_HEADS, HG_HEAD_DIM, HG_HEAD_DIM), f32)
    _, s_prev = lax.scan(step, init, (jnp.moveaxis(jnp.exp(b_last), 2, 0), jnp.moveaxis(kv, 2, 0)))
    s_prev = jnp.moveaxis(s_prev, 0, 2)
    o = o_intra + jnp.einsum('bhntd,bhndv->bhntv', qh * jnp.exp(bcum), s_prev)
    o = o.transpose(0, 2, 3, 1, 4).reshape(Bn, S, HG_HEADS, HG_HEAD_DIM)
    o = o * lax.rsqrt(jnp.mean(jnp.square(o), axis=-1, keepdims=True) + RMS_EPS)
    o = o.reshape(Bn, S, BRANCH_WIDTH) * norm_w.astype(f32) * jax.nn.silu(g.astype(f32))
    return o.astype(q.dtype)

def _s5(u, a_re, a_im, b_re, b_im, c_re, c_im, d, log_dt, glu_w, glu_b):
    Bn, S, _ = u.shape
    f32 = jnp.float32
    uf = u.astype(f32).reshape(Bn, S, S5_GROUPS, S5_GROUP_CH)
    A = lax.complex(a_re.astype(f32), a_im.astype(f32))
    dt = jnp.exp(log_dt.astype(f32))[:, None]
    A_bar = jnp.exp(A * dt)
    B_bar = ((A_bar - 1.0) / A)[..., None] * lax.complex(b_re.astype(f32), b_im.astype(f32))
    Cm = lax.complex(c_re.astype(f32), c_im.astype(f32))
    bu = jnp.einsum('bsgc,gpc->bsgp', uf.astype(jnp.complex64), B_bar)
    a = jnp.broadcast_to(A_bar[None, None], (1, S, S5_GROUPS, S5_STATE))
    _, h = lax.associative_scan(_lin_combine, (a, bu), axis=1)
    y = jnp.einsum('bsgp,gcp->bsgc', h, Cm).real + d.astype(f32).reshape(S5_GROUPS, S5_GROUP_CH) * uf
    y = jax.nn.gelu(y.reshape(Bn, S, BRANCH_WIDTH))
    y = y * jax.nn.sigmoid(jnp.einsum('bsc,ce->bse', y, glu_w.astype(f32)) + glu_b.astype(f32))
    return y.astype(u.dtype)

def _rglru(xg, xr, conv_w, conv_b, wa, ba, wx, bx, lam):
    Bn, S, _ = xr.shape
    f32 = jnp.float32
    xc = lax.conv_general_dilated(
        xr.astype(f32), conv_w.astype(f32)[:, None, :], window_strides=(1,),
        padding=[(RG_CONV - 1, 0)], dimension_numbers=('NWC', 'WIO', 'NWC'),
        feature_group_count=BRANCH_WIDTH) + conv_b.astype(f32)
    xb = xc.reshape(Bn, S, RG_BLOCKS, RG_BLOCK_W)
    r = jax.nn.sigmoid(jnp.einsum('bshi,hij->bshj', xb, wa.astype(f32)).reshape(Bn, S, BRANCH_WIDTH) + ba.astype(f32))
    i = jax.nn.sigmoid(jnp.einsum('bshi,hij->bshj', xb, wx.astype(f32)).reshape(Bn, S, BRANCH_WIDTH) + bx.astype(f32))
    log_a = -RG_C * r * jax.nn.softplus(-lam.astype(f32))
    a = jnp.exp(log_a)
    b = jnp.sqrt(-jnp.expm1(2.0 * log_a)) * (i * xc)
    _, h = lax.associative_scan(_lin_combine, (a, b), axis=1)
    return (h * jax.nn.gelu(xg.astype(f32))).astype(xr.dtype)

def _swiglu(x, w1, w3, w2):
    return (jax.nn.silu(x @ w1) * (x @ w3)) @ w2

def _moe(x2d, router_w, router_bias, w1, w3, w2, sw1, sw3, sw2):
    N, D = x2d.shape
    f32 = jnp.float32
    scores = jax.nn.sigmoid(x2d.astype(f32) @ router_w.astype(f32))
    biased = scores + router_bias.astype(f32)
    per_group = N_EXPERTS // N_EXPERT_GROUPS
    grp_score = jnp.sum(lax.top_k(biased.reshape(N, N_EXPERT_GROUPS, per_group), 2)[0], axis=-1)
    _, grp_idx = lax.top_k(grp_score, TOPK_GROUPS)
    grp_mask = jnp.any(grp_idx[:, :, None] == jnp.arange(N_EXPERT_GROUPS)[None, None, :], axis=1)
    masked = jnp.where(jnp.repeat(grp_mask, per_group, axis=1), biased, -jnp.inf)
    _, top_idx = lax.top_k(masked, TOP_K)
    w = jnp.take_along_axis(scores, top_idx, axis=1)
    w = w / jnp.sum(w, axis=-1, keepdims=True) * ROUTED_SCALE

    nk = N * TOP_K
    e_flat = top_idx.reshape(-1)
    tok_flat = jnp.arange(nk, dtype=jnp.int32) // TOP_K
    w_flat = w.reshape(-1)
    order = jnp.argsort(e_flat)
    e_sorted = e_flat[order]
    counts = jnp.zeros((N_EXPERTS,), jnp.int32).at[e_flat].add(1)
    start = jnp.cumsum(counts) - counts
    padded = (counts + MOE_BLOCK - 1) // MOE_BLOCK * MOE_BLOCK
    pad_end = jnp.cumsum(padded)
    pad_start = pad_end - padded
    dest = pad_start[e_sorted] + (jnp.arange(nk, dtype=jnp.int32) - start[e_sorted])
    n_blocks = (nk + N_EXPERTS * (MOE_BLOCK - 1) + MOE_BLOCK - 1) // MOE_BLOCK
    n_rows = n_blocks * MOE_BLOCK
    row_tok = jnp.full((n_rows,), N, jnp.int32).at[dest].set(tok_flat[order])
    row_w = jnp.zeros((n_rows,), f32).at[dest].set(w_flat[order])
    block_start = jnp.arange(n_blocks, dtype=jnp.int32) * MOE_BLOCK
    block_exp = jnp.minimum(jnp.searchsorted(pad_end, block_start, side='right'), N_EXPERTS - 1)
    x_pad = jnp.concatenate([x2d, jnp.zeros((1, D), x2d.dtype)], axis=0)

    def block_fn(acc, inp):
        rows, wts, e = inp
        xb = x_pad[rows]
        yb = _swiglu(xb, w1[e], w3[e], w2[e]) * wts[:, None].astype(x2d.dtype)
        return acc.at[rows].add(yb), None

    acc0 = jnp.zeros((N + 1, D), x2d.dtype)
    routed, _ = lax.scan(block_fn, acc0, (row_tok.reshape(n_blocks, MOE_BLOCK),
                                          row_w.reshape(n_blocks, MOE_BLOCK), block_exp))
    return routed[:N] + _swiglu(x2d, sw1, sw3, sw2)

def setup_inputs(seed: int = 0) -> dict:
    key = jax.random.key(seed)
    ks = jax.random.split(key, 36)
    L, D, W = DEPTH, D_MODEL, BRANCH_WIDTH
    G, P, CH = S5_GROUPS, S5_STATE, S5_GROUP_CH
    E, H = N_EXPERTS, EXPERT_HIDDEN

    def nrm(i, shape, s):
        return s * jax.random.normal(ks[i], shape, jnp.float32)

    def uni(i, shape, lo, hi):
        return jax.random.uniform(ks[i], shape, jnp.float32, lo, hi)

    a0 = uni(21, (L, W), 0.9, 0.999)
    s = a0 ** (1.0 / RG_C)
    return {
        'x': nrm(0, (BATCH, SEQ, D), 1.0),
        'w_in': nrm(1, (L, D, IN_COLS), D ** -0.5),
        'b_gate': nrm(2, (L, N_BRANCH * D), 0.02),
        'hgrn_lb_logits': nrm(3, (L, W), 0.5),
        'hgrn_norm_w': 1.0 + nrm(4, (L, W), 0.02),
        's5_a_re': -0.5 + nrm(5, (L, G, P), 0.01),
        's5_a_im': math.pi * jnp.arange(P, dtype=jnp.float32) + nrm(6, (L, G, P), 0.01),
        's5_b_re': nrm(7, (L, G, P, CH), (2 * CH) ** -0.5),
        's5_b_im': nrm(8, (L, G, P, CH), (2 * CH) ** -0.5),
        's5_c_re': nrm(9, (L, G, CH, P), (2 * P) ** -0.5),
        's5_c_im': nrm(10, (L, G, CH, P), (2 * P) ** -0.5),
        's5_d': nrm(11, (L, W), 0.5),
        's5_log_dt': uni(12, (L, G), math.log(1e-3), math.log(1e-1)),
        's5_glu_w': nrm(13, (L, W, W), W ** -0.5),
        's5_glu_b': nrm(14, (L, W), 0.02),
        'rg_conv_w': nrm(15, (L, RG_CONV, W), RG_CONV ** -0.5),
        'rg_conv_b': nrm(16, (L, W), 0.02),
        'rg_wa': nrm(17, (L, RG_BLOCKS, RG_BLOCK_W, RG_BLOCK_W), RG_BLOCK_W ** -0.5),
        'rg_ba': nrm(18, (L, W), 0.02),
        'rg_wx': nrm(19, (L, RG_BLOCKS, RG_BLOCK_W, RG_BLOCK_W), RG_BLOCK_W ** -0.5),
        'rg_bx': nrm(20, (L, W), 0.02),
        'rg_lambda': jnp.log(s) - jnp.log1p(-s),
        'w_branch': nrm(22, (L, N_BRANCH, W, D), DN_BETA * W ** -0.5),
        'w_out': nrm(23, (L, D, D), DN_BETA * D ** -0.5),
        'ln1_g': 1.0 + nrm(24, (L, D), 0.02),
        'ln1_b': nrm(25, (L, D), 0.02),
        'router_w': nrm(26, (L, D, E), D ** -0.5),
        'router_bias': nrm(27, (L, E), 0.01),
        'exp_w1': nrm(28, (L, E, D, H), D ** -0.5),
        'exp_w3': nrm(29, (L, E, D, H), D ** -0.5),
        'exp_w2': nrm(30, (L, E, H, D), DN_BETA * H ** -0.5),
        'sh_w1': nrm(31, (L, D, H), D ** -0.5),
        'sh_w3': nrm(32, (L, D, H), D ** -0.5),
        'sh_w2': nrm(33, (L, H, D), DN_BETA * H ** -0.5),
        'ln2_g': 1.0 + nrm(34, (L, D), 0.02),
        'ln2_b': nrm(35, (L, D), 0.02),
    }

def reference(x, w_in, b_gate, hgrn_lb_logits, hgrn_norm_w, s5_a_re, s5_a_im, s5_b_re, s5_b_im,
              s5_c_re, s5_c_im, s5_d, s5_log_dt, s5_glu_w, s5_glu_b, rg_conv_w, rg_conv_b,
              rg_wa, rg_ba, rg_wx, rg_bx, rg_lambda, w_branch, w_out, ln1_g, ln1_b,
              router_w, router_bias, exp_w1, exp_w3, exp_w2, sh_w1, sh_w3, sh_w2, ln2_g, ln2_b):
    Bn, S, D = x.shape
    sm = jax.nn.softmax(hgrn_lb_logits.astype(jnp.float32), axis=0)
    lower_bounds = jnp.cumsum(sm, axis=0) - sm[0:1]
    splits = np.cumsum([BRANCH_WIDTH] * 7).tolist()
    for l in range(DEPTH):
        proj = jnp.einsum('bsd,dc->bsc', x, w_in[l])
        hq, hf, hi, hg, su, rg_g, rg_x, gate_pre = jnp.split(proj, splits, axis=-1)
        y_a = _hgrn2(hq, hf, hi, hg, lower_bounds[l], hgrn_norm_w[l])
        y_b = _s5(su, s5_a_re[l], s5_a_im[l], s5_b_re[l], s5_b_im[l], s5_c_re[l], s5_c_im[l],
                  s5_d[l], s5_log_dt[l], s5_glu_w[l], s5_glu_b[l])
        y_c = _rglru(rg_g, rg_x, rg_conv_w[l], rg_conv_b[l], rg_wa[l], rg_ba[l], rg_wx[l], rg_bx[l],
                     rg_lambda[l])
        ys = jnp.stack([y_a, y_b, y_c], axis=2)
        branch = jnp.einsum('bskc,kcd->bskd', ys, w_branch[l])
        gates = jax.nn.sigmoid(gate_pre.reshape(Bn, S, N_BRANCH, D) + b_gate[l].reshape(N_BRANCH, D))
        mix = jnp.einsum('bsd,de->bse', jnp.sum(gates * branch, axis=2), w_out[l])
        x = _layernorm(DN_ALPHA * x + mix, ln1_g[l], ln1_b[l])
        ffn = _moe(x.reshape(Bn * S, D), router_w[l], router_bias[l], exp_w1[l], exp_w3[l], exp_w2[l],
                   sh_w1[l], sh_w3[l], sh_w2[l]).reshape(Bn, S, D)
        x = _layernorm(DN_ALPHA * x + ffn, ln2_g[l], ln2_b[l])
    return x


_drawn_inputs = setup_inputs


def setup_inputs(seed=0):
    import zlib

    import numpy as np

    out = dict(_drawn_inputs(seed))
    spreads = {}
    factors = {'b_gate': 5.186,
     'hgrn_norm_w': 4.189,
     's5_a_re': 64.0,
     's5_a_im': 27.64,
     's5_b_re': 48.232,
     's5_b_im': 30.664,
     's5_c_re': 30.688,
     's5_c_im': 36.48,
     's5_log_dt': 32.12,
     's5_glu_w': 2.855,
     's5_glu_b': 43.228,
     'rg_ba': 39.164,
     'rg_bx': 29.303,
     'ln2_g': 8.124,
     'ln2_b': 8.39}
    for name, (base, spread) in spreads.items():
        noise = np.random.default_rng([zlib.crc32(name.encode()), seed]).standard_normal(out[name].shape)
        drawn = base * np.exp(spread * noise) if base else spread * noise
        out[name] = __import__('jax').numpy.asarray(drawn.astype(out[name].dtype))
    for name, factor in factors.items():
        out[name] = (out[name] * factor).astype(out[name].dtype)
    return out
```

```python
from contextlib import ExitStack

import numpy as np

import concourse.bass as bass
from concourse import mybir

F32 = mybir.dt.float32
BF16 = mybir.dt.bfloat16
I32 = mybir.dt.int32
ALU = mybir.AluOpType
ACT = mybir.ActivationFunctionType
AX = mybir.AxisListType.X

P = 128
D = 1024
T = 1024
KD = D // P
W = 512
WT = W // P
HALF = 512
C = 128
NCH = T // C
LEVELS = [1, 2, 4, 8, 16, 32, 64]
G, NS, CH = 32, 64, 16
GP = G // 2
HP = GP // 2
SC = 8
NM = T // SC
E, TOPK, NG = 64, 8, 8
EH = 256
NW = KD * 2 * EH + 2 * D
SHB = T // P
NBMAX = SHB + T * TOPK // P + E
NBT = NBMAX + 4
TRASH = P
NROW = T + TRASH
ALPHA = 2.0 ** 0.25
LN_EPS, RMS_EPS = 1e-5, 1e-6
BIG = 1e30
PI = float(np.pi)
PI_IN = float(np.nextafter(np.float32(np.pi), np.float32(0)))
TP1 = 6.28125
TP2 = float(np.array(int(np.float32(2 * np.pi - TP1).view(np.int32)) & ~0xFFF, np.int32).view(np.float32))
TP3 = float(np.float32(2 * np.pi - TP1 - TP2))

CV = {}
_o = 0
for _n, _k in (("lb", 4), ("nw", 4), ("glub", 4), ("convw", 16), ("convb", 4), ("ba", 4), ("bx", 4), ("lam", 4), ("bgate", 24)):
    CV[_n] = _o
    _o += _k
NCV = _o
RV = {"ln1g": 0, "ln1b": D, "ln2g": 2 * D, "ln2b": 3 * D, "rb": 4 * D}
NRV = 4 * D + E

(DT, TH, RE, SN, CS, ARE, AIM, NR, NI, QR, QI, DEN, T0, T1, CR, CI, U2R, U2I, U4R, U4I) = range(20)
RJ, UR, UI, PR, PIM, PRR, PIR = 20, 29, 38, 47, 56, 65, 73
NPT = 81

U_P1, U_SU, U_H0, U_HL, U_GB, U_GA, U_WO, U_RT = 0, 4, 6, 8, 22, 30, 38, 42
T_Q, T_F, T_V, T_G, T_SU, T_RG, T_RX, T_GATE = 0, 4, 8, 12, 16, 20, 24, 28


ONE = 1


class Chain:

    def __init__(self, eng, sem):
        self.eng, self.sem, self.base, self.n = eng, sem, 0, 0

    def add(self, ins):
        self.n += 1
        ins.then_inc(self.sem, 1)

    def wait(self):
        self.eng.wait_ge(self.sem, self.base + self.n)

    def link(self, ins):
        self.add(ins)
        self.wait()

    def enter(self, i, per):
        self.start, self.per = self.base + self.n, per
        self.base, self.n = i * per + self.start, 0

    def leave(self, count):
        assert self.n == self.per, (self.n, self.per)
        self.base, self.n = self.start + self.per * count, 0


def build(nc, a, out, dbg=None):
    ctx = ExitStack()
    with ctx:
        def sem(name):
            return ctx.enter_context(nc.semaphore(name))

        def sbx(stack, name, shape, dt=F32):
            return stack.enter_context(nc.sbuf_tensor(name, shape, dt))

        def sb(name, shape, dt=F32):
            return sbx(ctx, name, shape, dt)

        ps = [ctx.enter_context(nc.psum_tensor(f"ps{i}", [P, HALF], F32)) for i in range(8)]
        PB4 = ps[4:8]

        x1d = nc.dram_tensor("x1_rows", [NROW, D], F32, kind="Internal").ap()
        accd = nc.dram_tensor("ffn_rows", [NROW, D], F32, kind="Internal").ap()
        slotd = nc.dram_tensor("slot_table", [P * NBT, 2], I32, kind="Internal").ap()
        blockd = nc.dram_tensor("block_table", [2 * P, 2], I32, kind="Internal").ap()

        ident = sb("ident", [P, P])
        ones = sb("ones", [P, P])
        avg = sb("avg", [P, P])
        before = sb("before", [P, P])
        mask = sb("mask", [P, len(LEVELS), C // 2], BF16)
        diag = sb("diag", [P, C], BF16)
        chan = sb("chan", [P, NCV])
        sp4 = sb("sp4", [P, WT, 8])
        lb1 = sb("lb1", [P, 2, WT])
        eps = sb("eps", [P, 2])

        lay_a = ExitStack()
        ring = sbx(lay_a, "ring", [P, 6, KD, P])
        bring = sbx(lay_a, "bring", [P, 2, WT, P])
        xT = sbx(lay_a, "xT", [P, KD, T])
        u_tok = sbx(lay_a, "u_tok", [P, G, SC, CH])
        yC = sbx(lay_a, "yC", [P, WT, T])
        N4 = sbx(lay_a, "N4", [P, 4, T])
        rgt = N4
        fN, qN, gN, vN = (N4[:, n] for n in range(4))
        yB = u_tok[:, :, :, :].rearrange("p g s c -> p (g s c)").rearrange("p (c t) -> p c t", c=WT)
        yT = yB

        lay_1 = ExitStack()
        rgx = sbx(lay_1, "rgx", [P, WT, T])
        s5p = sbx(lay_1, "s5p", [P, 3 * GP])
        s5w = sbx(lay_1, "s5w", [P, 4, GP, CH])
        s5d = sbx(lay_1, "s5d", [P, W])
        pt = sbx(lay_1, "pt", [P, NPT, GP])
        pti = sbx(lay_1, "pti", [P, GP], I32)
        Bb = sbx(lay_1, "Bb", [P, 2, GP, CH])
        OutR = sbx(lay_1, "OutR", [P, HP, 9, CH])
        OutI = sbx(lay_1, "OutI", [P, HP, 9, CH])
        InR = sbx(lay_1, "InR", [P, HP, SC, CH])
        InI = sbx(lay_1, "InI", [P, HP, SC, CH])
        InT = sbx(lay_1, "InT", [P, 2, HP, P])
        ER = sbx(lay_1, "ER", [P, HP, NM])
        EI = sbx(lay_1, "EI", [P, HP, NM])
        R8 = sbx(lay_1, "R8", [P, HP, NM])
        Hs = sbx(lay_1, "Hs", [P, 2, HP, NM])
        TU = sbx(lay_1, "TU", [P, 4 * HP, P])
        Tg, uT = TU[:, 0:2 * HP, :], TU[:, 2 * HP:4 * HP, :]
        glut = TU[:, :, :].rearrange("p a b -> p (a b)").rearrange("p (j t) -> p j t", j=WT)
        xc = uT.rearrange("p (s a) m -> p s (a m)", s=2)
        Ksb = Hs[:, :, :, :].rearrange("p a b m -> p (a b) m")
        WR, WI = (InR[:, :, :, :].rearrange("p g s c -> p g (s c)"), InI[:, :, :, :].rearrange("p g s c -> p g (s c)"))
        ytok = rgx[:, :, :].rearrange("p a b -> p (a b)").rearrange("p (s w) -> p s w", s=SC)
        lay_1.close()

        lay_2 = ExitStack()
        mixT = sbx(lay_2, "mixT", [P, KD, T])
        yA = sbx(lay_2, "yA", [P, WT, T])
        sig = sbx(lay_2, "sig", [P, 2, HALF])
        lay_3 = ExitStack()
        Fd = sbx(lay_3, "Fd", [P, T])
        qs = sbx(lay_3, "qs", [P, T])
        kk = sbx(lay_3, "kk", [P, T])
        Gd = sbx(lay_3, "Gd", [P, T])
        qF = sbx(lay_3, "qF", [P, T])
        kG = sbx(lay_3, "kG", [P, T])
        St = sbx(lay_3, "St", [P, T])
        tmp = sbx(lay_3, "tmp", [P, T])
        vtok = sbx(lay_3, "vtok", [P, NCH, P])
        kGt = tmp[:, :].rearrange("p (n d) -> p n d", n=NCH)
        Sall = kG[:, :].rearrange("p (n d) -> p n d", n=NCH)
        lay_3.close()
        lay_4 = ExitStack()
        wout = sbx(lay_4, "wout", [P, KD, D])
        xr, x1 = N4[:, 0], N4[:, 1:3]
        x1T = N4[:, 3].rearrange("p (k t) -> p k t", k=KD)
        ln1 = sbx(lay_4, "ln1", [P, 2, D])
        bst = sbx(lay_4, "bst", [P, 2, 6])
        mv = sbx(lay_4, "mv", [P, 4])
        rwt = sbx(lay_4, "rwt", [P, KD, E])
        lay_4.close()
        lay_2.close()
        lay_a.close()

        lay_m = ExitStack()
        wts = sbx(lay_m, "wts", [P, 3, NW])
        lay_pad = sbx(lay_m, "under_tail", [P, 34 * 1024 // 4])
        slt = sbx(lay_m, "slt", [P, NBT, 2], I32)
        sc = sbx(lay_m, "sc", [P, KD, E])
        bi = sbx(lay_m, "bi", [P, KD, E])
        top2 = sbx(lay_m, "top2", [P, KD, NG, 8])
        gs = sbx(lay_m, "gs", [P, KD, NG])
        gr = sbx(lay_m, "gr", [P, 3, KD, NG])
        ma = sbx(lay_m, "ma", [P, KD, E])
        mr = sbx(lay_m, "mr", [P, KD, E])
        m8 = sbx(lay_m, "m8", [P, KD, 8])
        sel = sbx(lay_m, "sel", [P, KD, E])
        wt = sbx(lay_m, "wt", [P, KD, E])
        key = sbx(lay_m, "key", [P, KD, E])
        eq = sbx(lay_m, "eq", [P, KD, E])
        k8 = sbx(lay_m, "k8", [P, KD, 8])
        w8 = sbx(lay_m, "w8", [P, 8, KD])
        den = sbx(lay_m, "den", [P, KD])
        i8 = sbx(lay_m, "i8", [P, 3, KD, 8], I32)
        tokw = sbx(lay_m, "tokw", [P, KD, 8, 2], I32)
        ec = sbx(lay_m, "ec", [P, 6, E + 1])
        eci = sbx(lay_m, "eci", [P, 3, E + 1], I32)
        bno = sbx(lay_m, "bno", [P, 2])
        bcmp = sbx(lay_m, "bcmp", [P, 2, E + 1])
        bof = sbx(lay_m, "bof", [P, 2, 2])
        boi = sbx(lay_m, "boi", [P, 2, 2], I32)
        btab = sbx(lay_m, "btab", [1, 2 * P, 2], I32)
        rb = sbx(lay_m, "rb", [P, E])
        xg = sbx(lay_m, "xg", [P, 2, D])
        xgT = sbx(lay_m, "xgT", [P, 2, KD, P])
        si = sbx(lay_m, "si", [P, 2, EH])
        hm = sbx(lay_m, "hm", [P, 2, EH])
        hTs = sbx(lay_m, "hTs", [P, 2, P])
        yo = sbx(lay_m, "yo", [P, 2, D])
        ix = sbx(lay_m, "ix", [P, 2], I32)
        sx = sbx(lay_m, "sx", [P, 2], I32)
        wx = sbx(lay_m, "wx", [P, 2])
        ln2 = sbx(lay_m, "ln2", [P, 2, D])
        sltf = slt[:, :, :].bitcast(F32)
        fr = wts[:, :, :].rearrange("p a b -> p (a b)")[:, 0:4 * D].rearrange("p (n d) -> p n d", n=4)
        fst = sbx(lay_m, "fst", [P, 2, 6])
        fmv = sbx(lay_m, "fmv", [P, 4])
        lay_m.close()

        s_x = sem("x_loaded")
        s_par = sem("params_loaded")
        s_s5par = sem("s5_params_loaded")
        s_const = sem("constants_built")
        s_pool = sem("pool_chain")
        s_dve = sem("dve_chain")
        s_act = sem("act_chain")
        a_go = sem("act_waited")
        p_go = sem("pool_waited")
        w_full = [sem(f"w_full{i}") for i in range(6)]
        b_full = [sem(f"bw_full{i}") for i in range(2)]
        k_full = [sem(f"bank_full{i}") for i in range(4)]
        k_free = [sem(f"bank_free{i}") for i in range(4)]
        s_sp = sem("rg_rate_exp")
        s_rate = sem("rg_rate_ready")
        s_conv = sem("rg_conv_done")
        s_rgmm = sem("rg_gate_products")
        s_rgact = sem("rg_gates_done")
        s_rgsq = sem("rg_sqrt_done")
        s_rgy = sem("rg_tile_done")
        s_trig = sem("s5_trig_in")
        s_trigo = sem("s5_trig_out")
        s_tab = sem("s5_tables")
        s_pe5 = sem("s5_pe_steps")
        s_ev5 = sem("s5_evacuated")
        s_toep = sem("s5_toeplitz_placed")
        s_H = sem("s5_states_ready")
        s_y5 = sem("s5_y_tokens")
        s_gelu5 = sem("s5_gelu_done")
        s_glua = sem("s5_glu_gate")
        s_yB = sem("yB_done")
        h_q = sem("head_q_ready")
        h_k = sem("head_k_F_ready")
        h_F = sem("head_F_level")
        h_G = sem("head_G_level")
        h_qF = sem("head_qF_ready")
        h_kG = sem("head_kG_ready")
        h_lvl = sem("level_products")
        h_lfree = sem("level_bank_free")
        h_pe = sem("head_pe_steps")
        h_ev = sem("head_act_evacs")
        h_S = sem("states_ready")
        h_o = sem("head_output_done")
        g_sig = sem("gate_sigmoid")
        g_mix = sem("gate_mixed")
        s_wo = sem("w_out_loaded")
        s_ln1 = sem("ln1_router_loaded")
        s_xr = sem("x_rows_loaded")
        s_xrf = sem("x_rows_used")
        s_var = sem("variance_ready")
        s_std = sem("deviation_ready")
        s_x1 = sem("x1_tile_ready")
        s_x1s = [sem(f"x1_tile_stored{i}") for i in range(2)]
        s_xtr = sem("x1_tile_turned")
        s_x1T = sem("x1T_ready")
        s_lg = sem("logits_ready")
        s_z = sem("zero_rows_ready")
        s_zd = sem("zero_rows_stored")
        s_xa = sem("residual_rows_ready")
        s_xas = sem("residual_rows_stored")
        s_sc_ = sem("scores_done")
        s_sel = sem("selection_ready")
        s_pos = sem("positions_counted")
        s_tw = sem("token_numbers")
        s_slt0 = sem("slot_table_default")
        s_slt1 = sem("slot_default_stored")
        s_adr = sem("slot_addresses")
        s_scat = sem("slots_scattered")
        s_slt = sem("slot_table_loaded")
        s_bt0 = sem("block_table_ready")
        s_bt1 = sem("block_table_stored")
        s_bt = sem("block_table_loaded")
        s_rb = sem("router_bias_loaded")
        w_in = [sem(f"expert_slot_full{i}") for i in range(3)]
        s_we = sem("expert_weights")
        e_g = [sem(f"rows_gathered{i}") for i in range(2)]
        e_T = sem("rows_turned")
        e_Te = sem("rowsT_ready")
        e_H = sem("hidden_products")
        e_si = sem("silu_ready")
        e_hm = sem("hidden_ready")
        e_hT = sem("hidden_turned")
        e_hTe = sem("hiddenT_ready")
        e_Y = sem("output_products")
        e_wx = sem("row_weight_ready")
        e_ya = sem("output_half_act")
        e_yd = sem("output_half_dve")
        e_sc = sem("rows_adding")
        e_add = sem("rows_added")
        f_in = [sem(f"ffn_rows_loaded{i}") for i in range(4)]
        f_var = sem("ffn_variance")
        f_std = sem("ffn_deviation")
        f_y = sem("out_tile_ready")
        f_out = [sem(f"out_tile_stored{i}") for i in range(4)]

        def counts(eng):
            eng.wait_ge(s_bt, 16)
            return eng.value_load(eci[0:1, 2, 0:1], min_val=1, max_val=NBMAX // 2)

        def tail_sp(sp):
            sp.dma_start(ln1[:], a["ln1"]).then_inc(s_ln1, 16)
            sp.dma_start(rwt[:], a["router_w"]).then_inc(s_ln1, 16)
            sp.wait_ge(s_z, 1)
            zr = sig[:, :, :].rearrange("p a b -> p (a b)")
            sp.dma_start(x1d[T:NROW, :], zr).then_inc(s_zd, 16)
            sp.dma_start(accd[T:NROW, :], zr).then_inc(s_zd, 16)

            def weights(slot, o):
                src = a["experts"][o] if isinstance(o, int) else a["experts"][bass.ds(o, 1)].rearrange("o p n -> (o p) n")
                sp.dma_start(wts[:, slot], src).then_inc(w_in[slot], 16)

            for t in range(KD):
                if t:
                    sp.wait_ge(s_xrf, t)
                sp.dma_start(xr, a["x"][t * P:(t + 1) * P, :]).then_inc(s_xr, 16)
                if t:
                    store_x1(sp, t - 1)
                if t == 0:
                    for o in range(3):
                        weights(o, o)
            store_x1(sp, KD - 1)
            for k in range(2):
                sp.wait_ge(s_x1s[k], 8 * KD)
            sp.wait_ge(s_lg, KD)
            sp.dma_start(rb[:], a["rb"]).then_inc(s_rb, 16)
            sp.wait_ge(s_slt0, 3)
            sp.dma_start(slotd.rearrange("(p b) w -> p b w", b=NBT), slt[:]).then_inc(s_slt1, 16)
            sp.wait_ge(s_bt0, 1)
            sp.dma_start(blockd.rearrange("(k p) w -> p k w", k=2), boi[:]).then_inc(s_bt1, 16)
            sp.wait_ge(s_bt1, 16)
            sp.dma_start(btab[:], blockd.rearrange("(o b) w -> o b w", o=1)).then_inc(s_bt, 16)
            sp.wait_ge(s_scat, 16 * KD * TOPK)
            sp.dma_start(slt[:], slotd.rearrange("(p b) w -> p b w", b=NBT)).then_inc(s_slt, 16)
            sp.dma_start(ln2[:], a["ln2"]).then_inc(s_ln1, 16)
            sp.wait_ge(s_xas, 16 * KD)

            def next_weights(slot, o):
                end = sp.value_load(eci[0:1, 1, o - 3:o - 2] if isinstance(o, int) else eci[0:1, 1, bass.ds(o - 3, 1)],
                                    min_val=0, max_val=NBMAX)
                sp.wait_ge(e_Y, end + ONE)
                weights(slot, o)

            def announce(slot, n):
                sp.wait_ge(w_in[slot], n)
                sp.sem_inc(s_we, 1)

            announce(0, 16)
            announce(1, 16)
            with sp.Fori(1, 21) as i:
                for k in range(3):
                    next_weights(k, i * 3 + k)
                    announce((k + 2) % 3, i * 16 + (0 if k == 0 else 16))
            for o in (63, 64):
                next_weights(o % 3, o)
                announce((o - 1) % 3, ((o - 1) // 3 + 1) * 16)
            announce(64 % 3, (64 // 3 + 1) * 16)
            n = counts(sp)
            sp.wait_ge(e_sc, n * 32)
            for t in range(KD):
                if t >= 4:
                    sp.wait_ge(f_out[t % 4], 16)
                sp.dma_start(fr[:, t % 4], accd[t * P:(t + 1) * P, :]).then_inc(f_in[t % 4], 16)
                if t >= 2:
                    store_out(sp, t - 2)
            store_out(sp, KD - 2)
            store_out(sp, KD - 1)
            for k in range(4):
                sp.wait_ge(f_out[k], 32)

        def store_x1(sp, t):
            sp.wait_ge(s_x1, t + 1)
            sp.dma_start(x1d[t * P:(t + 1) * P, :], x1[:, t % 2]).then_inc(s_x1s[t % 2], 16)
            sp.wait_ge(s_xa, t + 1)
            sp.dma_start(accd[t * P:(t + 1) * P, :], sig[:, :, :].rearrange("p a b -> p (a b)")).then_inc(s_xas, 16)

        def store_out(sp, t):
            sp.wait_ge(f_y, t + 1)
            sp.dma_start(out[t * P:(t + 1) * P, :], fr[:, t % 4]).then_inc(f_out[t % 4], 16)

        def tail_pool(pool, ch):
            g = nc.gpsimd
            pool.wait_ge(g_mix, 48 + ONE)
            g.memset(sig[:], 0.0).then_inc(s_z, 1)
            pool.wait_ge(s_lg, KD)
            g.iota(slt[:, 0:SHB, 0:1], pattern=[[P, SHB], [0, 1]], base=0, channel_multiplier=1).then_inc(s_slt0, 1)
            g.iota(slt[:, SHB:NBT, 0:1], pattern=[[0, NBT - SHB], [0, 1]], base=T, channel_multiplier=1).then_inc(s_slt0, 1)
            ch.add(g.memset(sltf[:, SHB:NBT, 1:2], 0.0))
            ch.wait()
            g.memset(sltf[:, 0:SHB, 1:2], 1.0).then_inc(s_slt0, 1)
            g.iota(bno[:, :], pattern=[[P, 2]], base=0, channel_multiplier=1, allow_small_or_imprecise_dtypes=True).then_inc(s_tw, 1)
            g.iota(tokw[:, :, :, 0:1], pattern=[[P, KD], [0, 8], [0, 1]], base=0, channel_multiplier=1).then_inc(s_tw, 1)
            pool.wait_ge(s_tw, 2)
            pool.wait_ge(s_slt1, 16)
            pool.wait_ge(s_adr, 1)
            for t in range(KD):
                for j in range(TOPK):
                    g.indirect_dma_start(out=slotd, out_offset=bass.IndirectOffsetOnAxis(ap=i8[:, 2, t, j:j + 1], axis=0),
                                         in_=tokw[:, t, j, :], in_offset=None).then_inc(s_scat, 16)
            pool.wait_ge(s_slt, 16)
            for k in range(2):
                pool.wait_ge(s_x1s[k], 8 * KD)
            pool.wait_ge(s_zd, 32)
            pool.wait_ge(s_xas, 16 * KD)

            def gather(k, c):
                pool.sem_inc(p_go, 1)
                ch.link(g.tensor_copy(ix[:, k:k + 1], slt[:, c, 0:1] if isinstance(c, int)
                                      else slt[:, bass.ds(c, 1), 0:1].rearrange("p o w -> p (o w)")))
                pool.sem_inc(p_go, 1)
                g.indirect_dma_start(out=xg[:, k, :], out_offset=None, in_=x1d,
                                     in_offset=bass.IndirectOffsetOnAxis(ap=ix[:, k:k + 1], axis=0)).then_inc(e_g[k], 16)

            gather(0, 0)
            gather(1, 1)
            pool.wait_ge(e_T, 1)
            pool.wait_ge(e_g[0], 16)
            gather(0, 2)
            n = counts(pool)
            with pool.Fori(0, n) as i:
                ch.enter(i, 4)
                for u in range(2):
                    b = i * 2 + u
                    pool.wait_ge(e_T, i * 2 + (u + 2))
                    pool.wait_ge(e_g[1 - u], i * 16 + (16 + 16 * u))
                    gather(1 - u, i * 2 + (u + 3))
                    ch.link(g.tensor_copy(sx[:, u:u + 1], slt[:, bass.ds(b, 1), 0:1].rearrange("p o w -> p (o w)")))
                    pool.wait_ge(e_ya, i * 2 + (u + 1) + ONE)
                    pool.wait_ge(e_yd, i * 2 + (u + 1) + ONE)
                    pool.sem_inc(p_go, 1)
                    g.indirect_dma_start(out=accd, out_offset=bass.IndirectOffsetOnAxis(ap=sx[:, u:u + 1], axis=0),
                                         in_=yo[:, u, :], in_offset=None, compute_op=ALU.add).then_inc(e_sc, 16)
                    pool.wait_ge(e_sc, i * 32 + 16 * (u + 1))
                    pool.sem_inc(e_add, 1)
                ch.base = 0

        def tail_pe(pe):
            mm, tr = nc.tensor.matmul, nc.tensor.transpose
            pe.wait_ge(s_wo, 16)
            pe.wait_ge(g_mix, 48 + ONE)
            pe.wait_ge(s_ln1, 32)
            for t in range(KD + 2):
                if t < KD:
                    for h in range(2):
                        b = 2 * (t % 2) + h
                        pe.wait_ge(k_free[b], U_WO + t // 2)
                        for k in range(KD):
                            ins = mm(ps[b][:], mixT[:, k, t * P:(t + 1) * P], wout[:, k, h * HALF:(h + 1) * HALF],
                                     start=k == 0, stop=k == KD - 1)
                        ins.then_inc(k_full[b], 1)
                if 1 <= t <= KD:
                    pe.wait_ge(s_x1, t)
                    pe.wait_ge(s_x1T, t - 1)
                    for k in range(KD):
                        ins = tr(ps[4 + k // 4][:, (k % 4) * P:(k % 4 + 1) * P], x1[:, (t - 1) % 2, k * P:(k + 1) * P], ident[:])
                    ins.then_inc(s_xtr, 1)
                if t >= 2 or t == KD + 1:
                    pass
                if t >= 1 and t <= KD:
                    pe.wait_ge(s_x1T, t)
                    for k in range(KD):
                        ins = mm(ps[6][:, (t - 1) * E:t * E], x1T[:, k, :], rwt[:, k, :], start=k == 0, stop=k == KD - 1)
                    ins.then_inc(s_lg, 1)
            pe.wait_ge(s_sel, 1)
            for t in range(KD):
                o = ps[4][:, t * E:(t + 1) * E]
                ins = mm(o, before[:], sel[:, t], start=True, stop=t == 0)
                for t2 in range(t):
                    ins = mm(o, ones[:], sel[:, t2], start=False, stop=t2 == t - 1)
            for t in range(KD):
                ins = mm(ps[5][:, 0:E], ones[:], sel[:, t], start=t == 0, stop=t == KD - 1)
            ins.then_inc(s_pos, 1)

            n = counts(pe)

            def turn(k, c16, c):
                pe.wait_ge(e_g[k], c16)
                pe.wait_ge(e_Te, c)
                for q in range(KD):
                    ins = tr(ps[q // 4][:, (q % 4) * P:(q % 4 + 1) * P], xg[:, k, q * P:(q + 1) * P], ident[:])
                ins.then_inc(e_T, 1)

            def block_weights(c):
                o = pe.value_load(btab[0:1, bass.ds(c, 1), 0:1] if not isinstance(c, int) else btab[0:1, c:c + 1, 0:1], min_val=0, max_val=E)
                s = pe.value_load(btab[0:1, bass.ds(c, 1), 1:2] if not isinstance(c, int) else btab[0:1, c:c + 1, 1:2], min_val=0, max_val=2)
                pe.wait_ge(s_we, o + 1)
                return s

            def hidden(k, s, te, free):
                pe.wait_ge(e_Te, te)
                if free is not None:
                    pe.wait_ge(e_hm, free + ONE)
                for q in range(KD):
                    ins = mm(ps[2 + k][:], xgT[:, k, q, :], wts[:, bass.ds(s, 1), q * 2 * EH:(q + 1) * 2 * EH].rearrange("p o n -> p (o n)"),
                             start=q == 0, stop=q == KD - 1)
                ins.then_inc(e_H, 1)

            turn(0, 16, 0)
            turn(1, 16, 1)
            hidden(0, block_weights(0), 1, None)
            with pe.Fori(0, n) as i:
                for u in range(2):
                    pe.wait_ge(e_hm, i * 2 + (u + 1) + ONE)
                    pe.wait_ge(e_hTe, i * 2 + u + ONE)
                    for q in range(2):
                        ins = tr(ps[4][:, q * P:(q + 1) * P], hm[:, u, q * P:(q + 1) * P], ident[:])
                    ins.then_inc(e_hT, 1)
                    hidden(1 - u, block_weights(i * 2 + (u + 1)), i * 2 + (u + 2), i * 2 + u)
                    turn(u, i * 16 + 32, i * 2 + (u + 2))
                    s = block_weights(i * 2 + u)
                    pe.wait_ge(e_hTe, i * 2 + (u + 1) + ONE)
                    pe.wait_ge(e_ya, i * 2 + u + ONE)
                    pe.wait_ge(e_yd, i * 2 + u + ONE)
                    for h in range(2):
                        for q in range(2):
                            c0 = KD * 2 * EH + q * D + h * HALF
                            ins = mm(ps[6 + h][:], hTs[:, q, :], wts[:, bass.ds(s, 1), c0:c0 + HALF].rearrange("p o n -> p (o n)"),
                                     start=q == 0, stop=q == 1)
                    ins.then_inc(e_Y, 1)

        def tail_act(act):
            A = nc.scalar.activation
            for t in range(KD + 1):
                if t < KD:
                    act.wait_ge(s_var, t + 1)
                    A(mv[:, 2:3], mv[:, 1:2], ACT.Sqrt, bias=eps[:, 0:1]).then_inc(s_std, 1)
                if t >= 1:
                    act.wait_ge(s_x1, t)
                    act.wait_ge(s_zd, 32)
                    if t >= 2:
                        act.wait_ge(s_xas, 16 * (t - 1))
                    A(sig[:, :, :].rearrange("p a b -> p (a b)"), x1[:, (t - 1) % 2], ACT.Copy, scale=ALPHA).then_inc(s_xa, 1)
                    act.wait_ge(s_xtr, t)
                    act.wait_ge(s_lg, t - 1)
                    for b in range(2):
                        ins = A(x1T[:, 4 * b:4 * b + 4, :].rearrange("p a b -> p (a b)"), ps[4 + b][:], ACT.Copy)
                    ins.then_inc(s_x1T, 1)
            act.wait_ge(s_lg, KD)
            A(sc[:].rearrange("p a b -> p (a b)"), ps[6][:], ACT.Sigmoid).then_inc(s_sc_, 1)
            n = counts(act)

            def rowsT(k, t, free):
                act.wait_ge(e_T, t)
                if free is not None:
                    act.wait_ge(e_H, free)
                for b in range(2):
                    ins = A(xgT[:, k, 4 * b:4 * b + 4, :].rearrange("p a b -> p (a b)"), ps[b][:], ACT.Copy)
                ins.then_inc(e_Te, 1)

            def silu(k, h, free):
                act.wait_ge(e_H, h)
                if free is not None:
                    act.wait_ge(e_hm, free + ONE)
                A(si[:, k, :], ps[2 + k][:, 0:EH], ACT.Silu).then_inc(e_si, 1)

            rowsT(0, 1, None)
            rowsT(1, 2, None)
            silu(0, 1, None)
            with act.Fori(0, n) as i:
                for u in range(2):
                    silu(1 - u, i * 2 + (u + 2), i * 2 + u)
                    rowsT(u, i * 2 + (u + 3), i * 2 + (u + 1))
                    act.wait_ge(e_Y, i * 2 + (u + 1) + ONE)
                    act.wait_ge(e_wx, i * 2 + (u + 1))
                    act.wait_ge(e_add, i * 2 + (u + 1))
                    A(yo[:, u, 0:HALF], ps[6][:], ACT.Copy, scale=wx[:, u:u + 1]).then_inc(e_ya, 1)
            for t in range(KD):
                act.wait_ge(f_var, t + 1)
                A(fmv[:, 2:3], fmv[:, 1:2], ACT.Sqrt, bias=eps[:, 0:1]).then_inc(f_std, 1)

        def tail_dve(dve, ch):
            V = nc.vector
            tt, ts, stt = V.tensor_tensor, V.tensor_scalar, V.scalar_tensor_tensor
            L, N = ch.link, ch.add
            bc = lambda x, shape: x.broadcast_to(shape)

            def layernorm(x, st, m, gb, var, std, done, t):
                for h in range(2):
                    N(V.bn_stats(st[:, h, :], x[:, h * HALF:(h + 1) * HALF]))
                ch.wait()
                V.bn_aggr(m[:, 0:2], st[:, :, :].rearrange("p a b -> p (a b)")).then_inc(var, 1)
                dve.wait_ge(std, t + 1)
                L(V.reciprocal(m[:, 3:4], m[:, 2:3]))
                L(ts(x, x, m[:, 0:1], m[:, 3:4], ALU.subtract, ALU.mult))
                L(tt(x, x, gb[:, 0], ALU.mult))
                tt(x, x, gb[:, 1], ALU.add).then_inc(done, 1)

            dve.wait_ge(s_ln1, 32)
            for t in range(KD):
                dve.wait_ge(s_xr, 16 * (t + 1))
                if t >= 2:
                    dve.wait_ge(s_x1s[t % 2], 16 * (t // 2))
                    dve.wait_ge(s_xtr, t - 1)
                    dve.wait_ge(s_xa, t - 1)
                x = x1[:, t % 2]
                for h in range(2):
                    b = 2 * (t % 2) + h
                    dve.wait_ge(k_full[b], U_WO + t // 2 + 1)
                    cols = slice(h * HALF, (h + 1) * HALF)
                    stt(x[:, cols], xr[:, cols], ALPHA, ps[b][:], ALU.mult, ALU.add).then_inc(k_free[b], 1)
                    dve.wait_ge(k_free[b], U_WO + t // 2 + 1)
                dve.sem_inc(s_xrf, 1)
                layernorm(x, bst, mv, ln1, s_var, s_std, s_x1, t)
            dve.wait_ge(s_sc_, 1)
            dve.wait_ge(s_rb, 16)
            L(tt(bi[:], sc[:], bc(rb[:].unsqueeze(1), [P, KD, E]), ALU.add))
            for t in range(KD):
                for q in range(NG):
                    N(V.max(top2[:, t, q, :], bi[:, t, q * 8:(q + 1) * 8]))
            ch.wait()
            L(tt(gs[:], top2[:, :, :, 0], top2[:, :, :, 1], ALU.add))
            L(V.memset(gr[:, 0], 0.0))
            for q in range(NG):
                v = gs[:, :, q:q + 1]
                if q < NG - 1:
                    n = NG - 1 - q
                    L(tt(gr[:, 1, :, q + 1:], bc(v, [P, KD, n]), gs[:, :, q + 1:], ALU.is_ge))
                if q > 0:
                    L(tt(gr[:, 1, :, 0:q], bc(v, [P, KD, q]), gs[:, :, 0:q], ALU.is_gt))
                L(V.memset(gr[:, 1, :, q:q + 1], 0.0))
                L(tt(gr[:, 0], gr[:, 0], gr[:, 1], ALU.add))
            L(ts(gr[:, 1], gr[:, 0], 4.0, None, ALU.is_lt))
            L(ts(gr[:, 2], gr[:, 1], BIG, -BIG, ALU.mult, ALU.add))
            for t in range(KD):
                v4 = lambda x: x[:, t].rearrange("p (q e) -> p q e", q=NG)
                N(tt(v4(ma), v4(bi), bc(gr[:, 1, t].unsqueeze(2), [P, NG, 8]), ALU.mult))
            ch.wait()
            for t in range(KD):
                v4 = lambda x: x[:, t].rearrange("p (q e) -> p q e", q=NG)
                N(tt(v4(ma), v4(ma), bc(gr[:, 2, t].unsqueeze(2), [P, NG, 8]), ALU.add))
            ch.wait()
            for t in range(KD):
                N(V.max(m8[:, t, :], ma[:, t, :]))
            ch.wait()
            for t in range(KD):
                N(V.match_replace(out=mr[:, t, :], in_to_replace=m8[:, t, :], in_values=ma[:, t, :], imm_value=-3 * BIG))
            ch.wait()
            ts(sel[:], mr[:], -2 * BIG, None, ALU.is_lt).then_inc(s_sel, 1)
            dve.wait_ge(s_sel, 1)
            L(tt(wt[:], sc[:], sel[:], ALU.mult))
            L(V.tensor_reduce(den[:], wt[:], AX, ALU.add))
            L(V.reciprocal(den[:], den[:]))
            L(ts(den[:], den[:], 2.5, None, ALU.mult))
            L(tt(wt[:], wt[:], bc(den[:].unsqueeze(2), [P, KD, E]), ALU.mult))
            dve.wait_ge(s_pos, 1)
            cI, cF, nb, end, beg = eci[:, 0, 0:E], ec[:, 0, 0:E], ec[:, 1, 0:E], ec[:, 2], ec[:, 3, 0:E]
            L(ts(cI, ps[5][:, 0:E], float(P - 1), None, ALU.add))
            L(ts(cI, cI, 7, None, ALU.logical_shift_right))
            L(ts(nb, cI, 1.0, None, ALU.max))
            L(V.memset(end[:, 0:1], float(SHB)))
            L(V.tensor_tensor_scan(end[:, 1:E + 1], ones[:, 0:E], nb, float(SHB), ALU.mult, ALU.add))
            L(tt(beg, end[:, 1:E + 1], nb, ALU.subtract))
            L(V.tensor_copy(eci[:, 1, :], end))
            dve.wait_ge(s_tw, 2)
            for k in range(2):
                N(ts(bcmp[:, k], end, bno[:, k:k + 1], None, ALU.is_le))
            ch.wait()
            L(V.tensor_reduce(bof[:, :, 0:1].rearrange("p k o -> p (k o)"), bcmp[:], AX, ALU.add))
            L(ts(bof[:, :, 0], bof[:, :, 0], float(E), None, ALU.min))
            L(V.tensor_copy(boi[:, :, 0], bof[:, :, 0]))
            L(ts(bof[:, :, 1], bof[:, :, 0], 171.0, None, ALU.mult))
            L(V.tensor_copy(boi[:, :, 1], bof[:, :, 1]))
            L(ts(boi[:, :, 1], boi[:, :, 1], 9, None, ALU.logical_shift_right))
            L(stt(bof[:, :, 1], boi[:, :, 1], -3.0, bof[:, :, 0], ALU.mult, ALU.add))
            L(V.tensor_copy(boi[:, :, 1], bof[:, :, 1]))
            L(ts(eci[:, 2, 0:1], end[:, E:E + 1], 1.0, None, ALU.add))
            ts(eci[:, 2, 0:1], eci[:, 2, 0:1], 1, None, ALU.logical_shift_right).then_inc(s_bt0, 1)
            L(ts(beg, beg, float(P), 1.0, ALU.mult, ALU.add))
            L(tt(key[:], ps[4][:].rearrange("p (t e) -> p t e", t=KD), bc(beg.unsqueeze(1), [P, KD, E]), ALU.add))
            L(tt(key[:], key[:], sel[:], ALU.mult))
            for t in range(KD):
                N(V.max(k8[:, t, :], key[:, t, :]))
            ch.wait()
            for j in range(TOPK):
                L(tt(eq[:], key[:], bc(k8[:, :, j:j + 1], [P, KD, E]), ALU.is_equal))
                L(tt(eq[:], eq[:], wt[:], ALU.mult))
                L(V.tensor_reduce(w8[:, j, :], eq[:], AX, ALU.add))
            L(V.tensor_copy(tokw[:, :, :, 1].bitcast(F32), w8[:].rearrange("p j t -> p t j")))
            L(ts(i8[:, 0], k8[:], -1.0, None, ALU.add))
            L(ts(i8[:, 1], i8[:, 0], P - 1, None, ALU.bitwise_and))
            L(ts(i8[:, 0], i8[:, 0], 7, None, ALU.logical_shift_right))
            stt(i8[:, 2], i8[:, 1], float(NBT), i8[:, 0], ALU.mult, ALU.add).then_inc(s_adr, 1)
            n = counts(dve)

            def hid(k, h, free):
                dve.wait_ge(e_si, h)
                if free is not None:
                    dve.wait_ge(e_hT, free + ONE)
                tt(hm[:, k, :], si[:, k, :], ps[2 + k][:, EH:2 * EH], ALU.mult).then_inc(e_hm, 1)

            dve.wait_ge(s_slt, 16)
            hid(0, 1, None)
            with dve.Fori(0, n) as i:
                for u in range(2):
                    dve.wait_ge(e_ya, i * 2 + u + ONE)
                    dve.wait_ge(e_yd, i * 2 + u + ONE)
                    V.tensor_copy(wx[:, u:u + 1], sltf[:, bass.ds(i * 2 + u, 1), 1:2].rearrange("p o w -> p (o w)")).then_inc(e_wx, 1)
                    dve.wait_ge(e_hT, i * 2 + (u + 1) + ONE)
                    dve.wait_ge(e_Y, i * 2 + u + ONE)
                    V.tensor_copy(hTs[:].rearrange("p a b -> p (a b)"), ps[4][:, 0:2 * P]).then_inc(e_hTe, 1)
                    hid(1 - u, i * 2 + (u + 2), i * 2 + u)
                    dve.wait_ge(e_Y, i * 2 + (u + 1) + ONE)
                    dve.wait_ge(e_wx, i * 2 + (u + 1))
                    dve.wait_ge(e_add, i * 2 + (u + 1))
                    ts(yo[:, u, HALF:D], ps[7][:], wx[:, u:u + 1], None, ALU.mult).then_inc(e_yd, 1)
            dve.wait_ge(s_ln1, 48)
            for t in range(KD):
                dve.wait_ge(f_in[t % 4], 16 * (t // 4 + 1))
                layernorm(fr[:, t % 4], fst, fmv, ln2, f_var, f_std, f_y, t)

        def dyn(ap, i):
            if isinstance(i, int):
                return ap[:, i]
            x = ap[:, bass.ds(i, 1)]
            return x.rearrange("p o n -> p (o n)") if len(x.shape) == 3 else x.rearrange("p o a b -> p (o a) b")

        block = ctx.enter_context(nc.Block())

        @block.sync
        def _(sp):
            sp.dma_start(xT[:], a["xT"]).then_inc(s_x, 16)

            def load_w(slot, tile, bank, n):
                if n is not None:
                    sp.wait_ge(k_full[bank], n)
                src = a["w_in"][tile] if isinstance(tile, int) else a["w_in"][bass.ds(tile, 1)].rearrange("o p k c -> (o p) k c")
                sp.dma_start(ring[:, slot], src).then_inc(w_full[slot], 16)

            def load_b(slot, tile, n):
                if n is not None:
                    sp.wait_ge(k_full[3], n)
                src = a["w_branch"][tile] if isinstance(tile, int) else a["w_branch"][bass.ds(tile, 1)].rearrange("o p k c -> (o p) k c")
                sp.dma_start(bring[:, slot], src).then_inc(b_full[slot], 16)

            def load_gate(s, i, branch, n):
                load_w(4 + s, i * 2 + (T_GATE + KD * branch + s), 1, n)
                load_b(s, i * 2 + (KD * branch + s), n)

            for s in range(4):
                load_w(s, T_RX + s, None, None)
            sp.dma_start(chan[:], a["chan"]).then_inc(s_par, 16)
            sp.dma_start(s5p[:], a["s5p"]).then_inc(s_s5par, 16)
            sp.dma_start(s5w[:], a["s5w"]).then_inc(s_s5par, 16)
            sp.dma_start(s5d[:], a["s5d"]).then_inc(s_s5par, 16)
            sp.dma_start(ring[:, 4], a["rg_w"]).then_inc(w_full[4], 16)
            for s in range(4):
                load_w(s, T_RG + s, 2 * (s % 2) + 1, s // 2 + 1)
            for s in range(4):
                load_w(s, T_SU + s, 2 * (s % 2) + 1, s // 2 + 3)
            for s, t in enumerate((T_F, T_Q, T_G, T_V)):
                load_w(s, t, 3, U_SU + 2)
            for half in range(2):
                sp.wait_ge(s_ev5, 3 * half + 3)
                for s in range(SC):
                    sp.dma_start(Tg[s * CH:(s + 1) * CH, :, s * CH:P], Ksb[0:CH, :, 0:P - s * CH]).then_inc(s_toep, 16)
                if half == 0:
                    sp.wait_ge(s_rgmm, WT)
                    sp.dma_start(ring[:, 4:6].rearrange("p a k c -> p (a k c)"), a["glu_w"]).then_inc(w_full[5], 16)
            sp.wait_ge(s_pe5, 18)
            for s in range(2):
                load_gate(s, 0, 2, None)
            for s, t in enumerate((T_F, T_Q, T_G, T_V)):
                load_w(s, t + 1, 2 * (s % 2) + 1, U_H0 + s // 2 + 1)
            with sp.Fori(1, WT - 1) as i:
                for s, t in enumerate((T_F, T_Q, T_G, T_V)):
                    load_w(s, i + (t + 1), 2 * (s % 2) + 1, i * 4 + (U_HL - 3 + s // 2))
                for s in range(2):
                    load_gate(s, i, 2, i * 4 + (U_HL - 1 + s))
            for s in range(2):
                load_gate(s, WT - 1, 2, (WT - 1) * 4 + (U_HL - 1 + s))
            for branch, u in ((1, U_GB), (0, U_GA)):
                with sp.Fori(0, 4) as i:
                    for s in range(2):
                        load_gate(s, i, branch, i * 2 + (u + s - 1))
            sp.wait_ge(h_o, WT + ONE)
            sp.dma_start(wout[:], a["w_out"]).then_inc(s_wo, 16)
            tail_sp(sp)

        @block.gpsimd
        def _(pool):
            ch = Chain(pool, s_pool)
            pool.sem_inc(h_kG, ONE)
            pool.sem_inc(e_add, 2)
            g = nc.gpsimd
            ch.add(g.memset(ident[:], 0.0))
            ch.add(g.memset(before[:], 1.0))
            ch.add(g.memset(ones[:], 1.0))
            ch.add(g.memset(avg[:], 1.0 / P))
            ch.add(g.memset(mask[:], 1.0))
            ch.add(g.memset(eps[:, 0:1], LN_EPS))
            ch.add(g.memset(eps[:, 1:2], RMS_EPS))
            ch.link(g.memset(Tg, 0.0))
            ch.add(g.affine_select(out=ident[:], in_=ident[:], compare_op=ALU.not_equal, fill=1.0, base=0,
                                   pattern=[[-1, P]], channel_multiplier=1))
            ch.add(g.affine_select(out=before[:], in_=before[:], compare_op=ALU.is_gt, fill=0.0, base=0,
                                   pattern=[[1, P]], channel_multiplier=-1))
            for n, h in enumerate(LEVELS):
                m = mask[:, n].rearrange("p (b j) -> p b j", j=h)
                nb = C // (2 * h)
                ch.wait()
                ch.link(g.affine_select(out=m, in_=m, compare_op=ALU.is_ge, fill=0.0, base=0,
                                        pattern=[[-2 * h, nb], [0, h]], channel_multiplier=1))
                ch.add(g.affine_select(out=m, in_=m, compare_op=ALU.is_ge, fill=0.0, base=h - 1,
                                       pattern=[[2 * h, nb], [0, h]], channel_multiplier=-1))
            ch.wait()
            g.tensor_copy(diag[:], ident[:]).then_inc(s_const, 1)

            def head(i):
                pool.wait_ge(h_kG, i * 7 + ONE)
                pool.wait_ge(h_pe, i * 5 + ONE)
                pool.sem_inc(p_go, 1)
                ch.link(g.memset(Gd[:], 1.0))
                for n, h in enumerate(LEVELS):
                    Gv, Fv = (x[:, :].rearrange("p (b j) -> p b j", j=2 * h) for x in (Gd, Fd))
                    nb = T // (2 * h)
                    pool.wait_ge(h_F, i * 7 + (n + 1))
                    g.tensor_tensor(Gv[:, :, 0:h], Gv[:, :, 0:h], Fv[:, :, 2 * h - 1:2 * h].broadcast_to([P, nb, h]),
                                    ALU.mult).then_inc(h_G, 1)
                    pool.wait_ge(h_G, i * 7 + (n + 1))
                    pool.wait_ge(h_lvl, i * 8 + (n + 2))
                    if 0 < n < len(LEVELS) - 1:
                        kv, Gw, Kw = (x[:, :].rearrange("p (b j) -> p b j", j=4 * h)[:, :, 0:2 * h] for x in (kk, Gd, kG))
                        g.tensor_tensor(Kw, kv, Gw, ALU.mult).then_inc(h_kG, 1)
                    else:
                        g.tensor_tensor(kG[:], kk[:], Gd[:], ALU.mult).then_inc(h_kG, 1)
                    pool.wait_ge(h_kG, i * 7 + (n + 1) + ONE)

            pool.wait_ge(s_yB, WT)
            with pool.Fori(0, WT - 1) as i:
                ch.enter(i, 1)
                head(i)
                ch.leave(WT - 1)
            head(WT - 1)
            tail_pool(pool, ch)

        NORMAL = ("V f0 L0 f1 L1 q0 L2 q1 L3 g0 L4 g1 L5 v0 L6 v1 L7 G00 G01 KT B00 KV B01 G10 O G11 M B10 B11").split()
        LAST = "V L0 G00 L1 G01 L2 B00 L3 B01 L4 G10 L5 G11 L6 B10 L7 B11 KT KV O M".split()

        def use(step, last):
            kind, h = step[0], int(step[-1])
            if kind in "fq":
                return (0 if kind == "f" else 2) + h, 0
            if kind in "gv":
                return (0 if kind == "g" else 2) + h, 1
            return (0 if kind == "G" else 2) + h, (0 if last else 2) + int(step[1])

        @block.tensor
        def _(pe):
            mm, tr = nc.tensor.matmul, nc.tensor.transpose
            for one in (h_pe, e_hT, e_Y):
                pe.sem_inc(one, ONE)

            def claim(b, n):
                pe.wait_ge(k_free[b], n)

            def project(slot, nw, h, b, n):
                if h == 0:
                    pe.wait_ge(w_full[slot], nw)
                claim(b, n)
                for k in range(KD):
                    ins = mm(ps[b][:], ring[:, slot, k, :], xT[:, k, h * HALF:(h + 1) * HALF], start=k == 0, stop=k == KD - 1)
                ins.then_inc(k_full[b], 1)

            pe.wait_ge(s_x, 16)
            for t in range(8):
                for h in range(2):
                    project(t % 4, 16 * (t // 4 + 1), h, 2 * (t % 2) + h, U_P1 + t // 2)

            pe.wait_ge(s_const, 1)
            rgw = ring[:, 4].rearrange("p (a j) c -> p a j c", a=2)
            for j in range(WT):
                for s in (2 * j, 2 * j + 1):
                    if s == 0:
                        for q in range(4):
                            pe.wait_ge(w_full[q], 48)
                    claim(s % 4, U_SU + s // 4)
                    for k in range(KD):
                        ins = mm(ps[s % 4][:], xT[:, k, s::SC], ring[:, 0:4, k, :], start=k == 0, stop=k == KD - 1)
                    ins.then_inc(k_full[s % 4], 1)
                pe.wait_ge(s_conv, j + 1)
                if j:
                    pe.wait_ge(s_rgact, 2 * j)
                else:
                    pe.wait_ge(w_full[4], 16)
                for m in range(2):
                    for h in range(2):
                        ins = mm(ps[4 + 2 * m + h][:], rgw[:, m, j, :], xc[:, j % 2, h * HALF:(h + 1) * HALF], start=True, stop=True)
                ins.then_inc(s_rgmm, 1)
            def by_rows(q):
                return PB4[2 * (q % 2) + q // 8][:, (q // 2 % 4) * P:(q // 2 % 4 + 1) * P]

            def s5_half(half):
                lo = 2 * HP * half
                if half:
                    pe.wait_ge(s_y5, 1)
                else:
                    pe.wait_ge(s_rgact, 2 * WT)
                    for q in range(4):
                        pe.wait_ge(k_free[q], U_SU + 2)
                for q in range(2 * HP):
                    ins = tr(PB4[q // 4][:, (q % 4) * P:(q % 4 + 1) * P], u_tok[:, lo + q].rearrange("p s c -> p (s c)"), ident[:])
                ins.then_inc(s_pe5, 1)
                yield
                pe.wait_ge(s_ev5, 3 * half + 1)
                pe.wait_ge(s_tab, half + 1)
                for part, src in ((0, InR), (1, InI)):
                    for q in range(HP):
                        ins = tr(PB4[2 * part + q // 4][:, (q % 4) * P:(q % 4 + 1) * P], src[:, q].rearrange("p s c -> p (s c)"), ident[:])
                ins.then_inc(s_pe5, 1)
                yield
                pe.wait_ge(s_ev5, 3 * half + 2)
                for q in range(2 * HP):
                    r = slice(NS * (q % 2), NS * (q % 2) + NS)
                    o = by_rows(q)[0:CH]
                    mm(o, Bb[r, 0, HP * half + q // 2, :], OutR[r, q // 2, 0:SC, :], start=True, stop=False)
                    ins = mm(o, Bb[r, 1, HP * half + q // 2, :], OutI[r, q // 2, 0:SC, :], start=False, stop=True)
                ins.then_inc(s_pe5, 1)
                yield
                pe.wait_ge(s_ev5, 3 * half + 3)
                for part in range(2):
                    for q in range(2 * HP):
                        o = PB4[2 * part + q // 8][NS * (q % 2):NS * (q % 2) + NS, (q // 2 % 4) * P:(q // 2 % 4 + 1) * P]
                        ins = mm(o, InT[:, part, q // 2, NS * (q % 2):NS * (q % 2) + NS], uT[:, q, :], start=True, stop=True)
                ins.then_inc(s_pe5, 1)
                yield
                pe.wait_ge(s_H, half + 1)
                pe.wait_ge(s_toep, 16 * SC * (half + 1))
                for q in range(2 * HP):
                    r = slice(NS * (q % 2), NS * (q % 2) + NS)
                    o = by_rows(q)
                    mm(o, uT[:, q, :], Tg[:, q, :], start=True, stop=False)
                    mm(o, Hs[r, 0, q // 2, :], OutR[r, q // 2, 1:SC + 1, :], start=False, stop=False)
                    ins = mm(o, Hs[r, 1, q // 2, :], OutI[r, q // 2, 1:SC + 1, :], start=False, stop=True)
                ins.then_inc(s_pe5, 1)
                yield

            first = s5_half(0)
            next(first)
            for s in range(4):
                for h in range(2):
                    project(s, 64, h, 2 * (s % 2) + h, U_H0 + s // 2)
                if s < 3:
                    next(first)
            next(first)
            for _ in s5_half(1):
                pass
            for cj in range(WT):
                pe.wait_ge(s_gelu5, 2)
                if cj >= 2:
                    pe.wait_ge(s_ev5, 6 + cj - 1)
                else:
                    pe.wait_ge(s_y5, 2)
                for s in range(SC):
                    ins = tr(PB4[2 * (cj % 2) + s // 4][:, (s % 4) * P:(s % 4 + 1) * P], ytok[:, s, cj * P:(cj + 1) * P], ident[:])
                ins.then_inc(s_pe5, 1)
            glu = ring[:, 4:6].rearrange("p a k c -> p (a k c)").rearrange("p (k n) -> p k n", k=WT)
            pe.wait_ge(w_full[5], 16)
            pe.wait_ge(s_ev5, 10)
            for e in range(WT):
                if e >= 2:
                    pe.wait_ge(s_glua, e - 1)
                for h in range(2):
                    for k in range(WT):
                        ins = mm(PB4[2 * (e % 2) + h][:], glu[:, k, e * P:(e + 1) * P], yT[:, k, h * HALF:(h + 1) * HALF],
                                 start=k == 0, stop=k == WT - 1)
                ins.then_inc(s_pe5, 1)

            def gate(s, h, n, nw):
                if h == 0:
                    pe.wait_ge(w_full[4 + s], nw)
                claim(h, n)
                for k in range(KD):
                    ins = mm(ps[h][:], ring[:, 4 + s, k, :], xT[:, k, h * HALF:(h + 1) * HALF], start=k == 0, stop=k == KD - 1)
                ins.then_inc(k_full[h], 1)

            def branch(s, h, y, n, nb):
                if h == 0:
                    pe.wait_ge(b_full[s], nb)
                claim(2 + h, n)
                for k in range(WT):
                    ins = mm(ps[2 + h][:], bring[:, s, k, :], y[:, k, h * HALF:(h + 1) * HALF], start=k == 0, stop=k == WT - 1)
                ins.then_inc(k_full[2 + h], 1)

            def head(i, sched, last):
                for step in sched:
                    if step == "V":
                        pe.wait_ge(k_free[3], i * 4 + U_HL)
                        pe.wait_ge(h_ev, i * 4 + ONE)
                        for n in range(NCH):
                            ins = tr(ps[4 + n // 4][:, (n % 4) * P:(n % 4 + 1) * P], vN[:, n * P:(n + 1) * P], ident[:])
                        ins.then_inc(h_pe, 1)
                    elif step[0] == "L":
                        l = int(step[1])
                        if l == 0:
                            pe.wait_ge(h_ev, i * 4 + 1 + ONE)
                            pe.wait_ge(h_k, i + 1)
                            pe.wait_ge(h_q, i + 1)
                            for n in range(NCH):
                                ins = mm(ps[4 + n // 4][:, (n % 4) * P:(n % 4 + 1) * P], kk[:, n * P:(n + 1) * P], qs[:, n * P:(n + 1) * P],
                                         start=True, stop=True)
                        else:
                            pe.wait_ge(h_lfree, i * 8 + max(1, l - 1))
                            pe.wait_ge(h_qF, i * 8 + l + ONE)
                            if l > 1:
                                pe.wait_ge(h_kG, i * 7 + (l - 1) + ONE)
                            left = kk if l == 1 else kG
                            qc = qF[:, ((l - 1) % 2) * HALF:((l - 1) % 2 + 1) * HALF]
                            for n in range(NCH):
                                ins = mm(ps[4 + l % 2][:, n * 64:(n + 1) * 64], left[:, n * P:(n + 1) * P], qc[:, n * 64:(n + 1) * 64],
                                         start=True, stop=True)
                        ins.then_inc(h_lvl, 1)
                    elif step == "KT":
                        pe.wait_ge(h_lfree, i * 8 + 8)
                        pe.wait_ge(h_kG, i * 7 + 7 + ONE)
                        for n in range(NCH):
                            ins = tr(ps[4 + n // 4][:, (n % 4) * P:(n % 4 + 1) * P], kG[:, n * P:(n + 1) * P], ident[:])
                        ins.then_inc(h_pe, 1)
                    elif step == "KV":
                        pe.wait_ge(h_ev, i * 4 + 2 + ONE)
                        for n in range(NCH - 1):
                            ins = mm(ps[4 + n // 4][:, (n % 4) * P:(n % 4 + 1) * P], kGt[:, n, :], vtok[:, n, :], start=True, stop=True)
                        ins.then_inc(h_pe, 1)
                    elif step == "O":
                        pe.wait_ge(h_S, i + 1)
                        pe.wait_ge(h_qF, i * 8 + 8 + ONE)
                        pe.wait_ge(h_o, i + ONE)
                        for n in range(NCH):
                            o = ps[6 + n // 4][:, (n % 4) * P:(n % 4 + 1) * P]
                            ins = mm(o, vtok[:, n, :], St[:, n * P:(n + 1) * P], start=True, stop=n == 0)
                            if n:
                                ins = mm(o, Sall[:, n, :], qF[:, n * P:(n + 1) * P], start=False, stop=True)
                        ins.then_inc(h_pe, 1)
                    elif step == "M":
                        pe.wait_ge(h_ev, i * 4 + 3 + ONE)
                        for h in range(2):
                            ins = mm(ps[4 + h][:], avg[:], tmp[:, h * HALF:(h + 1) * HALF], start=True, stop=True)
                        ins.then_inc(h_pe, 1)
                    else:
                        b, k = use(step, last)
                        n = i * 4 + (U_HL + k)
                        if step[0] == "G":
                            gate(int(step[1]), int(step[2]), n, i * 16 + 32)
                        elif step[0] == "B":
                            branch(int(step[1]), int(step[2]), yC, n, i * 16 + 16)
                        else:
                            slot, h = "fqgv".index(step[0]), int(step[1])
                            project(slot, i * 16 + 80, h, b, n)

            pe.wait_ge(s_glua, WT)
            with pe.Fori(0, WT - 1) as i:
                head(i, NORMAL, False)
            head(WT - 1, LAST, True)
            for m, (y, u) in enumerate(((yB, U_GB), (yA, U_GA))):
                if m:
                    pe.wait_ge(h_o, WT + ONE)
                else:
                    pe.wait_ge(s_yB, WT)
                with pe.Fori(0, 4) as i:
                    for s in range(2):
                        for h in range(2):
                            gate(s, h, i * 2 + (u + s), i * 16 + 16 * (6 + 4 * m))
                        for h in range(2):
                            branch(s, h, y, i * 2 + (u + s), i * 16 + 16 * (5 + 4 * m))
            tail_pe(pe)

        @block.scalar
        def _(act):
            A = nc.scalar.activation
            ch = Chain(act, s_act)
            for one in (h_ev, e_ya):
                act.sem_inc(one, ONE)

            def evac(out, b, n, func=ACT.Copy, own=None, **kw):
                act.wait_ge(k_full[b], n + 1)
                if not isinstance(n, int):
                    act.sem_inc(a_go, 1)
                return A(out, ps[b][:], func, **kw).then_inc(k_free[b], 1)

            act.wait_ge(s_sp, 1)
            A(sp4[:, :, 1], sp4[:, :, 0], ACT.Exp, scale=-1.0).then_inc(s_rate, 1)
            act.wait_ge(s_s5par, 48)
            A(pt[:, DT], s5p[:, 2 * GP:3 * GP], ACT.Exp).then_inc(s_trigo, 1)
            for t in range(4):
                for h in range(2):
                    evac(rgx[:, t, h * HALF:(h + 1) * HALF], 2 * (t % 2) + h, U_P1 + t // 2)
            act.wait_ge(s_trig, 1)
            A(pt[:, SN], pt[:, SN], ACT.Sin)
            A(pt[:, CS], pt[:, CS], ACT.Sin)
            for j in range(1, 9):
                ins = A(pt[:, RJ + j], pt[:, RE], ACT.Exp, scale=float(j))
            ins.then_inc(s_trigo, 1)
            for t in range(4, 8):
                for h in range(2):
                    evac(yC[:, t - 4, h * HALF:(h + 1) * HALF], 2 * (t % 2) + h, U_P1 + t // 2, ACT.Gelu_apprx_tanh)
            for j in range(WT):
                for s in (2 * j, 2 * j + 1):
                    act.wait_ge(k_full[s % 4], U_SU + s // 4 + 1)
                    A(u_tok[:, :, s, :], ps[s % 4][:].rearrange("p (g c) -> p g c", g=G), ACT.Copy).then_inc(k_free[s % 4], 1)
                act.wait_ge(s_rgmm, j + 1)
                act.wait_ge(s_rgy, j)
                for h in range(2):
                    ins = A(rgt[:, 0, h * HALF:(h + 1) * HALF], PB4[h][:], ACT.Sigmoid, bias=chan[:, CV["ba"] + j:CV["ba"] + j + 1])
                ins.then_inc(s_rgact, 1)
                for h in range(2):
                    ins = A(rgt[:, 1, h * HALF:(h + 1) * HALF], PB4[2 + h][:], ACT.Sigmoid, bias=chan[:, CV["bx"] + j:CV["bx"] + j + 1])
                ins.then_inc(s_rgact, 1)
                act.wait_ge(s_rgact, 2 * j + 2)
                A(rgt[:, 2], rgt[:, 0], ACT.Tanh, scale=sp4[:, j, 7:8]).then_inc(s_rgsq, 1)
                act.wait_ge(s_rgsq, 2 * j + 1)
                A(rgt[:, 3], rgt[:, 2], ACT.Sqrt).then_inc(s_rgsq, 1)

            def s5_half(half):
                act.wait_ge(s_pe5, 5 * half + 1)
                act.wait_ge(s_rgy, WT)
                for q in range(4):
                    ins = A(uT[:, 4 * q:4 * q + 4, :].rearrange("p a b -> p (a b)"), PB4[q][:], ACT.Copy)
                ins.then_inc(s_ev5, 1)
                yield
                act.wait_ge(s_pe5, 5 * half + 2)
                for q in range(4):
                    ins = A(InT[:, q // 2, 4 * (q % 2):4 * (q % 2) + 4, :].rearrange("p a b -> p (a b)"), PB4[q][:], ACT.Copy)
                ins.then_inc(s_ev5, 1)
                yield
                act.wait_ge(s_pe5, 5 * half + 3)
                for q in range(4):
                    ins = A(Ksb[0:CH].rearrange("p (h a e) b -> p h e a b", h=2, e=2)[:, q % 2, q // 2],
                            PB4[q][0:CH, :].rearrange("p (a b) -> p a b", a=4), ACT.Copy)
                ins.then_inc(s_ev5, 1)
                yield

            first = s5_half(0)

            def gelu5(half):
                for q in range(2):
                    g0 = 2 * HP * half + 8 * q
                    ins = A(ytok[:, :, g0 * CH:(g0 + 8) * CH].rearrange("p s (g c) -> p g s c", g=8), u_tok[:, g0:g0 + 8], ACT.Gelu_apprx_tanh)
                ins.then_inc(s_gelu5, 1)

            def head_evac(s, h, b, n, i):
                if i is not None:
                    act.wait_ge(*((h_F, i * 7 + 1), (h_q, i * 2 + 2), (h_q, i * 2 + 2), (h_pe, i * 5 + 1 + ONE))[s])
                evac((fN, qN, gN, vN)[s][:, h * HALF:(h + 1) * HALF], b, n, ACT.Sigmoid if s == 0 else ACT.Copy)

            next(first)
            for s in range(4):
                for h in range(2):
                    head_evac(s, h, 2 * (s % 2) + h, U_H0 + s // 2, None)
                if s < 2:
                    next(first)
            act.wait_ge(s_y5, 1)
            gelu5(0)
            for _ in s5_half(1):
                pass
            act.wait_ge(s_y5, 2)
            gelu5(1)
            for cj in range(WT):
                act.wait_ge(s_pe5, 10 + cj + 1)
                yv = yT[:, cj, :].rearrange("p (m s) -> p s m", s=SC)
                for b in range(2):
                    ins = A(yv[:, 4 * b:4 * b + 4, :], PB4[2 * (cj % 2) + b][:].rearrange("p (s m) -> p s m", s=4), ACT.Copy)
                ins.then_inc(s_ev5, 1)
            for e in range(WT):
                act.wait_ge(s_pe5, 14 + e + 1)
                for h in range(2):
                    ins = A(glut[:, e, h * HALF:(h + 1) * HALF], PB4[2 * (e % 2) + h][:], ACT.Sigmoid,
                            bias=chan[:, CV["glub"] + e:CV["glub"] + e + 1])
                ins.then_inc(s_glua, 1)

            def gate(s, h, n, tile, branch):
                j, before = tile
                act.wait_ge(g_mix, before * 2 + ONE)
                evac(sig[:, h, :], h, n, ACT.Sigmoid, bias=chan[:, bass.ds(j + (CV["bgate"] + KD * branch), 1)]
                     if not isinstance(j, int) else chan[:, CV["bgate"] + KD * branch + j:CV["bgate"] + KD * branch + j + 1])

            def head(i, sched, last):
                for step in sched:
                    if step == "V":
                        act.wait_ge(k_free[2], i * 4 + U_HL)
                        act.wait_ge(k_free[3], i * 4 + U_HL)
                        act.wait_ge(k_free[1], i * 4 + U_HL)
                        act.wait_ge(k_free[0], i * 4 + U_HL)
                        act.wait_ge(h_qF, i * 8 + ONE)
                        act.sem_inc(a_go, 1)
                        A(qs[:], qN, ACT.Silu).then_inc(h_q, 1)
                        A(dyn(yA, i), gN, ACT.Silu).then_inc(h_q, 1)
                        act.wait_ge(h_pe, i * 5 + 1 + ONE)
                        for b in range(2):
                            ins = A(vtok[:, 4 * b:4 * b + 4, :].rearrange("p a b -> p (a b)"), ps[4 + b][:], ACT.Copy)
                        ins.then_inc(h_ev, 1)
                    elif step == "KT":
                        act.wait_ge(h_pe, i * 5 + 2 + ONE)
                        act.wait_ge(h_qF, i * 8 + 8 + ONE)
                        for b in range(2):
                            ins = A(tmp[:, b * HALF:(b + 1) * HALF], ps[4 + b][:], ACT.Copy)
                        ins.then_inc(h_ev, 1)
                    elif step == "O":
                        act.wait_ge(h_pe, i * 5 + 4 + ONE)
                        for b in range(2):
                            ins = A(tmp[:, b * HALF:(b + 1) * HALF], ps[6 + b][:], ACT.Square)
                        ins.then_inc(h_ev, 1)
                    elif step == "M":
                        act.wait_ge(h_pe, i * 5 + 5 + ONE)
                        for b in range(2):
                            ins = A(St[:, b * HALF:(b + 1) * HALF], ps[4 + b][:], ACT.Sqrt, bias=eps[:, 1:2])
                        ins.then_inc(h_ev, 1)
                    elif step[0] in "fqgv":
                        b, k = use(step, last)
                        head_evac("fqgv".index(step[0]), int(step[1]), b, i * 4 + (U_HL + k), i)
                    elif step[0] == "G":
                        b, k = use(step, last)
                        t = i * 2 + int(step[1])
                        gate(int(step[1]), int(step[2]), i * 4 + (U_HL + k), (t, t), 2)

            act.wait_ge(s_yB, WT)
            with act.Fori(0, WT - 1) as i:
                head(i, NORMAL, False)
            head(WT - 1, LAST, True)
            for m, (br, u) in enumerate(((1, U_GB), (0, U_GA))):
                with act.Fori(0, 4) as i:
                    for s in range(2):
                        for h in range(2):
                            gate(s, h, i * 2 + (u + s), (i * 2 + s, i * 2 + (s + KD + KD * m)), br)
            tail_act(act)

        @block.vector
        def _(dve):
            V = nc.vector
            tt, ts, stt = V.tensor_tensor, V.tensor_scalar, V.scalar_tensor_tensor
            ch = Chain(dve, s_dve)
            for one in (h_o, h_qF, g_mix, e_yd, e_hTe, e_hm):
                dve.sem_inc(one, ONE)
            L = ch.link
            N = ch.add

            dve.wait_ge(s_par, 16)
            lam = chan[:, CV["lam"]:CV["lam"] + WT]
            L(ts(sp4[:, :, 0], lam, -1.0, None, ALU.mult))
            N(ts(sp4[:, :, 7], sp4[:, :, 0], 0.0, None, ALU.max))
            tt(sp4[:, :, 0], sp4[:, :, 0], lam, ALU.max).then_inc(s_sp, 1)
            dve.wait_ge(s_rate, 1)
            z, w, w2, acc = (sp4[:, :, n] for n in (1, 2, 3, 4))
            L(ts(w, z, 2.0, None, ALU.add))
            L(V.reciprocal(w2, w))
            L(tt(w, z, w2, ALU.mult))
            L(tt(w2, w, w, ALU.mult))
            L(ts(acc, w2, 1.0 / 17, 1.0 / 15, ALU.mult, ALU.add))
            for n in (13, 11, 9, 7, 5, 3, 1):
                L(tt(acc, acc, w2, ALU.mult))
                L(ts(acc, acc, 1.0 / n, None, ALU.add))
            L(tt(acc, acc, w, ALU.mult))
            L(stt(acc, acc, 2.0, sp4[:, :, 7], ALU.mult, ALU.add))
            L(ts(sp4[:, :, 7], acc, 4.0, None, ALU.mult))
            lbl = chan[:, CV["lb"]:CV["lb"] + WT]
            L(tt(lb1[:, 0], lbl, lbl, ALU.subtract))
            L(ts(lb1[:, 0], lb1[:, 0], 1.0, None, ALU.add))
            L(tt(lb1[:, 0], lb1[:, 0], lb1[:, 0], ALU.subtract))
            L(ts(lb1[:, 1], lb1[:, 0], -1.0, 1.0, ALU.mult, ALU.add))

            p = lambda n: pt[:, n]
            dve.wait_ge(s_trigo, 1)
            are, aim = s5p[:, 0:GP], s5p[:, GP:2 * GP]
            N(tt(p(RE), are, p(DT), ALU.mult))
            L(tt(p(TH), aim, p(DT), ALU.mult))
            L(ts(p(T0), p(TH), float(1 / (2 * np.pi)), None, ALU.mult))
            L(V.tensor_copy(pti[:], p(T0)))
            L(V.tensor_copy(p(T0), pti[:]))
            L(stt(p(TH), p(T0), -TP1, p(TH), ALU.mult, ALU.add))
            L(stt(p(TH), p(T0), -TP2, p(TH), ALU.mult, ALU.add))
            L(stt(p(TH), p(T0), -TP3, p(TH), ALU.mult, ALU.add))
            L(ts(p(SN), p(TH), PI_IN, -PI_IN, ALU.min, ALU.max))
            L(ts(p(CS), p(SN), -1.0, None, ALU.mult))
            L(tt(p(CS), p(CS), p(SN), ALU.max))
            ts(p(CS), p(CS), -1.0, PI / 2, ALU.mult, ALU.add).then_inc(s_trig, 1)
            N(V.memset(p(UR), 1.0))
            N(V.memset(p(UI), 0.0))
            N(V.memset(p(RJ), 1.0))
            dve.wait_ge(s_trigo, 2)
            N(V.tensor_copy(p(UR + 1), p(CS)))
            L(V.tensor_copy(p(UI + 1), p(SN)))

            def bc(x, shape):
                return x.broadcast_to(shape)

            def cmul(outr, outi, ar, ai, br, bi, t, shape=None, first=None):
                N(tt(outr, ar, br, ALU.mult))
                L(tt(t, ai, bi, ALU.mult))
                L(tt(outr, outr, t, ALU.subtract))
                N(tt(outi, ar, bi, ALU.mult))
                L(tt(t, ai, br, ALU.mult))
                L(tt(outi, outi, t, ALU.add))

            scr = Hs[:, :, :, :].rearrange("p a b m -> p (a b m)")

            def pwr(dst, src, n, by):
                b3 = [P, n, GP]
                fr, fi = (bc(pt[:, x + by:x + by + 1, :], b3) for x in (UR, UI))
                cmul(pt[:, UR + dst:UR + dst + n], pt[:, UI + dst:UI + dst + n], pt[:, UR + src:UR + src + n],
                     pt[:, UI + src:UI + src + n], fr, fi, scr[:, 0:n * GP].rearrange("p (n g) -> p n g", n=n))

            pwr(2, 1, 1, 1)
            pwr(3, 1, 2, 2)
            pwr(5, 1, 4, 4)
            N(tt(pt[:, PR:PR + 9], pt[:, RJ:RJ + 9], pt[:, UR:UR + 9], ALU.mult))
            L(tt(pt[:, PIM:PIM + 9], pt[:, RJ:RJ + 9], pt[:, UI:UI + 9], ALU.mult))
            for s in range(SC):
                N(V.tensor_copy(p(PRR + s), p(PR + SC - 1 - s)))
                N(V.tensor_copy(p(PIR + s), p(PIM + SC - 1 - s)))
            N(ts(p(NR), p(PR + 1), -1.0, None, ALU.add))
            N(tt(p(T0), are, are, ALU.mult))
            L(tt(p(T1), aim, aim, ALU.mult))
            L(tt(p(DEN), p(T0), p(T1), ALU.add))
            N(V.reciprocal(p(DEN), p(DEN)))
            N(tt(p(QR), p(NR), are, ALU.mult))
            N(tt(p(T0), p(PIM + 1), aim, ALU.mult))
            N(tt(p(QI), p(PIM + 1), are, ALU.mult))
            L(tt(p(T1), p(NR), aim, ALU.mult))
            N(tt(p(QR), p(QR), p(T0), ALU.add))
            L(tt(p(QI), p(QI), p(T1), ALU.subtract))
            N(tt(p(QR), p(QR), p(DEN), ALU.mult))
            L(tt(p(QI), p(QI), p(DEN), ALU.mult))
            sh = [P, GP, CH]
            qr, qi = (bc(p(x).unsqueeze(2), sh) for x in (QR, QI))
            cmul(Bb[:, 0], Bb[:, 1], s5w[:, 0], s5w[:, 1], qr, qi, scr[:, 0:GP * CH].rearrange("p (g c) -> p g c", g=GP))

            def tables(half):
                gs = slice(HP * half, HP * half + HP)

                def view(x, n):
                    return pt[:, x:x + n, gs].rearrange("p j g -> p g j")

                sh = [P, HP, 9, CH]
                pr, pi = (bc(view(x, 9).unsqueeze(3), sh) for x in (PR, PIM))
                cr, ci = (bc(s5w[:, x, gs].unsqueeze(2), sh) for x in (2, 3))
                t = scr[:, 0:HP * 9 * CH].rearrange("p (g j c) -> p g j c", g=HP, j=9)
                for g in range(HP):
                    q = slice(g, g + 1)
                    N(tt(OutR[:, g], cr[:, g], pr[:, g], ALU.mult))
                    N(tt(t[:, g], ci[:, g], pi[:, g], ALU.mult))
                ch.wait()
                L(tt(OutR[:], OutR[:], t, ALU.subtract))
                for g in range(HP):
                    N(tt(OutI[:, g], cr[:, g], pi[:, g], ALU.mult))
                    N(tt(t[:, g], ci[:, g], pr[:, g], ALU.mult))
                ch.wait()
                L(stt(OutI[:].rearrange("p g j c -> p (g j c)"), OutI[:].rearrange("p g j c -> p (g j c)"), -1.0,
                      t.rearrange("p g j c -> p (g j c)"), ALU.mult, ALU.subtract))
                sh = [P, HP, SC, CH]
                pr, pi = (bc(view(x, SC).unsqueeze(3), sh) for x in (PRR, PIR))
                br, bi = (bc(Bb[:, x, gs].unsqueeze(2), sh) for x in (0, 1))
                t = scr[:, 0:HP * P].rearrange("p (g s c) -> p g s c", g=HP, s=SC)
                for o, (x0, x1), op in ((InR, (pr, pi), ALU.subtract), (InI, (pi, pr), ALU.add)):
                    for g in range(HP):
                        N(tt(o[:, g], br[:, g], x0[:, g], ALU.mult))
                        N(tt(t[:, g], bi[:, g], x1[:, g], ALU.mult))
                    ch.wait()
                    ins = tt(o[:], o[:], t, op)
                    L(ins) if o is InR else ins.then_inc(s_tab, 1)
                dve.wait_ge(s_tab, half + 1)
                N(V.memset(ER[:, :, 0:1], 1.0))
                N(V.memset(EI[:, :, 0:1], 0.0))
                L(V.tensor_copy(pt[:, CR:CR + 1, gs], pt[:, UR + 8:UR + 9, gs]))
                L(V.tensor_copy(pt[:, CI:CI + 1, gs], pt[:, UI + 8:UI + 9, gs]))
                n = 1
                while n < NM:
                    sh = [P, HP, n]
                    cr, ci = (bc(pt[:, x, gs].unsqueeze(2), sh) for x in (CR, CI))
                    cmul(ER[:, :, n:2 * n], EI[:, :, n:2 * n], ER[:, :, 0:n], EI[:, :, 0:n], cr, ci,
                         R8[:].rearrange("p g m -> p (g m)")[:, 0:HP * n].rearrange("p (g m) -> p g m", g=HP))
                    if 2 * n < NM:
                        a_, b_, c_ = (pt[:, x, gs] for x in (T0, CR, CI))
                        N(tt(pt[:, T1, gs], b_, c_, ALU.mult))
                        L(tt(a_, c_, c_, ALU.mult))
                        L(tt(b_, b_, b_, ALU.mult))
                        L(tt(b_, b_, a_, ALU.subtract))
                        L(ts(c_, pt[:, T1, gs], 2.0, None, ALU.mult))
                    n *= 2
                L(V.tensor_copy(R8[:], bc(pt[:, RJ + 8, gs].unsqueeze(2), [P, HP, NM])))
                L(V.memset(R8[:, :, 0:1], 0.0))

            tables(0)

            def conv(j):
                dve.wait_ge(k_free[2 * (j % 2) + 1], U_P1 + j // 2 + 1)
                dve.wait_ge(k_free[2 * (j % 2)], U_P1 + j // 2 + 1)
                if j >= 2:
                    dve.wait_ge(s_rgmm, j - 1)
                o = xc[:, j % 2]
                tap = lambda k: chan[:, CV["convw"] + 4 * k + j:CV["convw"] + 4 * k + j + 1]
                L(ts(o, rgx[:, j], tap(3), chan[:, CV["convb"] + j:CV["convb"] + j + 1], ALU.mult, ALU.add))
                for k in (2, 1, 0):
                    d = 3 - k
                    ins = stt(o[:, d:T], rgx[:, j, 0:T - d], tap(k), o[:, d:T], ALU.mult, ALU.add)
                    L(ins) if k else ins.then_inc(s_conv, 1)

            def recur(j):
                i_, s_, q_, r_ = rgt[:, 1], rgt[:, 2], rgt[:, 3], rgt[:, 0]
                dve.wait_ge(s_rgact, 2 * j + 2)
                dve.wait_ge(s_conv, j + 1)
                L(tt(i_, i_, xc[:, j % 2], ALU.mult))
                dve.wait_ge(s_rgsq, 2 * j + 2)
                L(ts(s_, s_, 1.0, None, ALU.add))
                L(V.reciprocal(r_, s_))
                L(stt(q_, q_, 2.0, r_, ALU.mult, ALU.mult))
                L(tt(i_, i_, q_, ALU.mult))
                L(ts(r_, r_, 2.0, -1.0, ALU.mult, ALU.add))
                L(V.tensor_tensor_scan(s_, r_, i_, 0.0, ALU.mult, ALU.add))
                dve.wait_ge(k_free[2 * (j % 2) + 1], U_P1 + 2 + j // 2 + 1)
                dve.wait_ge(k_free[2 * (j % 2)], U_P1 + 2 + j // 2 + 1)
                tt(yC[:, j], s_, yC[:, j], ALU.mult).then_inc(s_rgy, 1)
                dve.wait_ge(s_rgy, j + 1)

            conv(0)
            conv(1)
            for j in range(WT):
                recur(j)
                if j + 2 < WT:
                    conv(j + 2)

            def s5_half(half):
                dve.wait_ge(s_pe5, 5 * half + 4)
                for b in range(2):
                    gs = slice(4 * b, 4 * b + 4)
                    ir, ii = (PB4[2 * x + b][:].rearrange("p (g m) -> p g m", g=4)[:, :, 0:NM - 1] for x in range(2))
                    er, ei = ER[:, gs, 1:NM], EI[:, gs, 1:NM]
                    wr, wi = (x[:, gs, 1:NM] for x in (WR, WI))
                    if half == 0 or True:
                        dve.wait_ge(s_toep, 16 * SC * (half + 1))
                    t = Hs[:, 0, gs, 1:NM]
                    N(tt(wr, er, ir, ALU.mult))
                    L(tt(t, ei, ii, ALU.mult))
                    L(tt(wr, wr, t, ALU.add))
                    N(tt(wi, er, ii, ALU.mult))
                    L(tt(t, ei, ir, ALU.mult))
                    L(tt(wi, wi, t, ALU.subtract))
                N(V.memset(WR[:, :, 0:1], 0.0))
                L(V.memset(WI[:, :, 0:1], 0.0))
                r8 = R8[:].rearrange("p g m -> p (g m)")
                for w_ in (WR, WI):
                    f = w_.rearrange("p g m -> p (g m)")
                    L(V.tensor_tensor_scan(f, r8, f, 0.0, ALU.mult, ALU.add))
                hr, hi = Hs[:, 0], Hs[:, 1]
                N(tt(hr, ER[:], WR, ALU.mult))
                L(tt(R8[:], EI[:], WI, ALU.mult))
                L(tt(hr, hr, R8[:], ALU.subtract))
                N(tt(hi, ER[:], WI, ALU.mult))
                L(tt(R8[:], EI[:], WR, ALU.mult))
                tt(hi, hi, R8[:], ALU.add).then_inc(s_H, 1)
                g0 = 2 * HP * half
                d = s5d[:, :].rearrange("p (g c) -> p g c", g=G)
                L(tt(u_tok[:, g0:g0 + 2 * HP], u_tok[:, g0:g0 + 2 * HP], bc(d[:, g0:g0 + 2 * HP].unsqueeze(2), [P, 2 * HP, SC, CH]), ALU.mult))
                dve.wait_ge(s_pe5, 5 * half + 5)
                for b in range(4):
                    o = u_tok[:, g0:g0 + 2 * HP].rearrange("p (h a e) s c -> p h e a (s c)", h=2, e=2)[:, b % 2, b // 2]
                    ins = tt(o, o, PB4[b][:].rearrange("p (a n) -> p a n", a=4), ALU.add)
                    if b < 3:
                        N(ins)
                ins.then_inc(s_y5, 1)

            s5_half(0)
            tables(1)
            s5_half(1)
            dve.wait_ge(s_pe5, 18)
            for e in range(WT):
                dve.wait_ge(s_glua, e + 1)
                tt(yB[:, e], glut[:, e], yT[:, e], ALU.mult).then_inc(s_yB, 1)

            def mixin(s, h, n, tile, first):
                j, before = tile
                dve.wait_ge(g_mix, before * 2 + ONE)
                dve.wait_ge(k_full[2 + h], n + 1)
                dve.wait_ge(k_free[h], n + 1)
                o = mixT[:, :, h * HALF:(h + 1) * HALF]
                o = o[:, j] if isinstance(j, int) else o[:, bass.ds(j, 1)].rearrange("p o n -> p (o n)")
                if first:
                    tt(o, sig[:, h], ps[2 + h][:], ALU.mult).then_inc(g_mix, 1)
                    dve.wait_ge(g_mix, before * 2 + (h + 1) + ONE)
                    dve.sem_inc(k_free[2 + h], 1)
                else:
                    tt(sig[:, h], sig[:, h], ps[2 + h][:], ALU.mult).then_inc(k_free[2 + h], 1)
                    dve.wait_ge(k_free[2 + h], n + 1)
                    tt(o, o, sig[:, h], ALU.add).then_inc(g_mix, 1)

            odd = lambda x, h: x[:, :].rearrange("p (b j) -> p b j", j=2 * h)[:, :, h:2 * h]

            def head(i, sched, last):
                K = i * 8
                for step in sched:
                    if step == "V":
                        dve.wait_ge(k_free[0], i * 4 + U_HL)
                        dve.wait_ge(k_free[1], i * 4 + U_HL)
                        dve.wait_ge(h_kG, i * 7 + ONE)
                        dve.wait_ge(h_o, i + ONE)
                        sc = (lb1[:, 1], lb1[:, 0])
                        sc = [x[:, i:i + 1] if isinstance(i, int) else x[:, bass.ds(i, 1)] for x in sc]
                        ts(Fd[:], fN, sc[0], sc[1], ALU.mult, ALU.add).then_inc(h_F, 1)
                        dve.wait_ge(h_F, i * 7 + 1)
                        ts(kk[:], Fd[:], -1.0, 1.0, ALU.mult, ALU.add).then_inc(h_k, 1)
                        dve.wait_ge(h_q, i * 2 + 1)
                        tt(qF[:, 0:HALF].rearrange("p (b j) -> p b j", j=1), odd(qs, 1), odd(Fd, 1), ALU.mult).then_inc(h_qF, 1)
                        dve.wait_ge(h_qF, K + 1 + ONE)
                    elif step[0] == "L":
                        l = int(step[1])
                        if l < 7:
                            h = LEVELS[l]
                            Fv = Fd[:, :].rearrange("p (b j) -> p b j", j=2 * h)
                            dve.wait_ge(h_G, i * 7 + (l + 1))
                            ins = tt(Fv[:, :, h:], Fv[:, :, h:], bc(Fv[:, :, h - 1:h], [P, T // (2 * h), h]), ALU.mult)
                            if l < 6:
                                ins.then_inc(h_F, 1)
                                dve.wait_ge(h_F, i * 7 + (l + 2))
                                h2 = 2 * h
                                if l > 0:
                                    dve.wait_ge(h_lvl, K + (l + 1))
                                qc = qF[:, ((l + 1) % 2) * HALF:((l + 1) % 2 + 1) * HALF].rearrange("p (b j) -> p b j", j=h2)
                                tt(qc, odd(qs, h2), odd(Fd, h2), ALU.mult).then_inc(h_qF, 1)
                            else:
                                L(ins)
                        dve.wait_ge(h_lvl, K + (l + 1))
                        if l == 0:
                            for b in range(2):
                                v = lambda x: x.rearrange("p (n t) -> p n t", n=4)
                                ins = tt(v(St[:, b * HALF:(b + 1) * HALF]), v(ps[4 + b][:]), bc(diag[:, :].unsqueeze(1), [P, 4, C]), ALU.mult)
                                if b == 0:
                                    N(ins)
                            ins.then_inc(h_lfree, 1)
                            dve.wait_ge(h_lfree, K + 1)
                        else:
                            h = LEVELS[l - 1]
                            v = lambda x: x.rearrange("p (n t) -> p n t", n=NCH)
                            tt(v(tmp[:, 0:HALF]), v(ps[4 + l % 2][:]), bc(mask[:, l - 1].unsqueeze(1), [P, NCH, C // 2]), ALU.mult).then_inc(h_lfree, 1)
                            dve.wait_ge(h_lfree, K + (l + 1))
                            L(tt(odd(St, h), odd(St, h), tmp[:, 0:HALF].rearrange("p (b j) -> p b j", j=h), ALU.add))
                        if l == 7:
                            tt(qF[:], qs[:], Fd[:], ALU.mult).then_inc(h_qF, 1)
                    elif step == "KV":
                        dve.wait_ge(h_pe, i * 5 + 3 + ONE)
                        for n in range(NCH - 1):
                            kv = ps[4 + n // 4][:, (n % 4) * P:(n % 4 + 1) * P]
                            if n == 0:
                                L(V.tensor_copy(Sall[:, 1], kv))
                            else:
                                ins = stt(Sall[:, n + 1], Sall[:, n], Fd[:, n * C + C - 1:n * C + C], kv, ALU.mult, ALU.add)
                                L(ins) if n < NCH - 2 else ins.then_inc(h_S, 1)
                    elif step == "M":
                        dve.wait_ge(h_ev, i * 4 + 4 + ONE)
                        L(V.reciprocal(St[:], St[:]))
                        nw = chan[:, CV["nw"] + i:CV["nw"] + i + 1] if isinstance(i, int) else chan[:, bass.ds(i + CV["nw"], 1)]
                        for b in range(2):
                            ins = stt(tmp[:, b * HALF:(b + 1) * HALF], ps[6 + b][:], nw, St[:, b * HALF:(b + 1) * HALF], ALU.mult, ALU.mult)
                            N(ins)
                        ch.wait()
                        dve.wait_ge(h_q, i * 2 + 2)
                        tt(dyn(yA, i), tmp[:], dyn(yA, i), ALU.mult).then_inc(h_o, 1)
                    elif step[0] == "B":
                        b, k = use(step, last)
                        t = i * 2 + int(step[1])
                        mixin(int(step[1]), int(step[2]), i * 4 + (U_HL + k), (t, t), True)

            per = 1 + 1 + 7 + 6 + 3
            with dve.Fori(0, WT - 1) as i:
                ch.enter(i, per)
                head(i, NORMAL, False)
                ch.leave(WT - 1)
            head(WT - 1, LAST, True)
            for m, u in enumerate((U_GB, U_GA)):
                with dve.Fori(0, 4) as i:
                    for s in range(2):
                        for h in range(2):
                            mixin(s, h, i * 2 + (u + s), (i * 2 + s, i * 2 + (s + KD + KD * m)), False)
            tail_dve(dve, ch)


_OUTS = [((1, T, D), "float32")]


def _layout(i):
    f = lambda n: np.asarray(i[n])
    ch = lambda n, k: f(n)[0].reshape(k, P).T
    rows = lambda *names: np.ascontiguousarray(np.broadcast_to(np.stack([f(n)[0] for n in names]), (P, len(names), D)))
    pair = lambda x: x.reshape(GP, 2, NS, -1).transpose(1, 2, 0, 3).reshape(P, GP, -1)
    exp = np.empty((E + 1, P, NW), np.float32)
    for e, (w1, w3, w2) in enumerate([(f("sh_w1"), f("sh_w3"), f("sh_w2")), (f("exp_w1")[0], f("exp_w3")[0], f("exp_w2")[0])]):
        n = w1.shape[0]
        to = exp[:1] if e == 0 else exp[1:]
        hid = to[:, :, :KD * 2 * EH].reshape(n, P, KD, 2 * EH)
        hid[..., :EH] = w1.reshape(n, KD, P, EH).transpose(0, 2, 1, 3)
        hid[..., EH:] = w3.reshape(n, KD, P, EH).transpose(0, 2, 1, 3)
        to[:, :, :KD * 2 * EH] = hid.reshape(n, P, -1)
        to[:, :, KD * 2 * EH:] = w2.reshape(n, 2, P, D).transpose(0, 2, 1, 3).reshape(n, P, -1)
    x = f("x")[0]
    return {
        "x": x,
        "xT": x.T.reshape(KD, P, T).transpose(1, 0, 2),
        "w_in": f("w_in")[0].reshape(KD, P, -1, P).transpose(2, 1, 0, 3),
        "w_branch": f("w_branch")[0].reshape(3, WT, P, KD, P).transpose(0, 3, 2, 1, 4).reshape(3 * KD, P, WT, P),
        "w_out": f("w_out")[0].reshape(KD, P, D).transpose(1, 0, 2),
        "glu_w": f("s5_glu_w")[0].reshape(WT, P, W).transpose(1, 0, 2).reshape(P, WT * W),
        "rg_w": np.stack([f("rg_wa")[0], f("rg_wx")[0]]).transpose(2, 0, 1, 3).reshape(P, KD, P),
        "chan": np.concatenate([ch("hgrn_lb_logits", 4), ch("hgrn_norm_w", 4), ch("s5_glu_b", 4),
                                f("rg_conv_w")[0].reshape(4 * 4, P).T, ch("rg_conv_b", 4), ch("rg_ba", 4), ch("rg_bx", 4),
                                ch("rg_lambda", 4), ch("b_gate", 24)], axis=1),
        "s5p": np.concatenate([pair(f("s5_a_re")[0])[..., 0], pair(f("s5_a_im")[0])[..., 0],
                               pair(np.broadcast_to(f("s5_log_dt")[0][:, None], (G, NS)))[..., 0]], axis=1),
        "s5w": np.stack([pair(f("s5_b_re")[0]), pair(f("s5_b_im")[0]), pair(f("s5_c_re")[0].transpose(0, 2, 1)),
                         pair(f("s5_c_im")[0].transpose(0, 2, 1))], axis=1),
        "s5d": np.broadcast_to(f("s5_d")[0], (P, W)),
        "ln1": rows("ln1_g", "ln1_b"),
        "ln2": rows("ln2_g", "ln2_b"),
        "rb": np.broadcast_to(f("router_bias")[0], (P, E)),
        "router_w": f("router_w")[0].reshape(KD, P, E).transpose(1, 0, 2),
        "experts": exp,
    }


def kernel(**inputs):
    import concourse.bacc as bacc
    from concourse.bass_utils import run_bass_kernel_spmd

    nc = bacc.Bacc("TRN2", target_bir_lowering=False, num_devices=1)
    arrays = {f"in_{n}": np.ascontiguousarray(v) for n, v in _layout(inputs).items()}
    aps = {n[3:]: nc.dram_tensor(n, v.shape, mybir.dt.from_np(v.dtype), kind="ExternalInput").ap() for n, v in arrays.items()}
    out = nc.dram_tensor("out", (T, D), F32, kind="ExternalOutput").ap()
    build(nc, aps, out)
    r = run_bass_kernel_spmd(nc, [arrays], core_ids=[0])
    return r.results[0]["out"].reshape(1, T, D)
```

```python
from contextlib import ExitStack

import numpy as np

import concourse.bass as bass
from concourse import mybir

F32 = mybir.dt.float32
BF16 = mybir.dt.bfloat16
I32 = mybir.dt.int32
F32R = mybir.dt.float32r
ALU = mybir.AluOpType
ACT = mybir.ActivationFunctionType
AX = mybir.AxisListType.X

P = 128
D = 1024
T = 1024
KD = D // P
W = 512
WT = W // P
HALF = 512
C = 128
NCH = T // C
LEVELS = [1, 2, 4, 8, 16, 32, 64]
G, NS, CH = 32, 64, 16
GP = G // 2
HP = GP // 2
SC = 8
NM = T // SC
E, TOPK, NG = 64, 8, 8
EH = 256
NH = KD * 2 * EH
NW = NH + 2 * D
SHB = T // P
NBMAX = SHB + T * TOPK // P + E
NBT = NBMAX + 4
TRASH = P
NROW = T + TRASH
ALPHA = 2.0 ** 0.25
LN_EPS, RMS_EPS = 1e-5, 1e-6
BIG = 1e30
PI = float(np.pi)
PI_IN = float(np.nextafter(np.float32(np.pi), np.float32(0)))
TP1 = 6.28125
TP2 = float(np.array(int(np.float32(2 * np.pi - TP1).view(np.int32)) & ~0xFFF, np.int32).view(np.float32))
TP3 = float(np.float32(2 * np.pi - TP1 - TP2))

CV = {}
_o = 0
for _n, _k in (("lb", 4), ("nw", 4), ("glub", 4), ("convw", 16), ("convb", 4), ("ba", 4), ("bx", 4), ("lam", 4), ("bgate", 24)):
    CV[_n] = _o
    _o += _k
NCV = _o
RV = {"ln1g": 0, "ln1b": D, "ln2g": 2 * D, "ln2b": 3 * D, "rb": 4 * D}
NRV = 4 * D + E

(DT, TH, RE, SN, CS, ARE, AIM, NR, NI, QR, QI, DEN, T0, T1, CR, CI, U2R, U2I, U4R, U4I) = range(20)
RJ, UR, UI, PR, PIM, PRR, PIR = 20, 29, 38, 47, 56, 65, 73
NPT = 81

U_P1, U_SU, U_H0, U_HL, U_GB, U_GA, U_WO, U_RT = 0, 4, 6, 8, 22, 30, 38, 42
T_Q, T_F, T_V, T_G, T_SU, T_RG, T_RX, T_GATE = 0, 4, 8, 12, 16, 20, 24, 28


ONE = 1


class Chain:

    def __init__(self, eng, sem):
        self.eng, self.sem, self.base, self.n = eng, sem, 0, 0

    def add(self, ins):
        self.n += 1
        ins.then_inc(self.sem, 1)

    def wait(self):
        self.eng.wait_ge(self.sem, self.base + self.n)

    def link(self, ins):
        self.add(ins)
        self.wait()

    def enter(self, i, per, first=0):
        self.start, self.per = self.base + self.n - first * per, per
        self.base, self.n = i * per + self.start, 0

    def leave(self, count):
        assert self.n == self.per, (self.n, self.per)
        self.base, self.n = self.start + self.per * count, 0


def build(nc, a, out, dbg=None):
    ctx = ExitStack()
    with ctx:
        def sem(name):
            return ctx.enter_context(nc.semaphore(name))

        def sbx(stack, name, shape, dt=F32):
            return stack.enter_context(nc.sbuf_tensor(name, shape, dt))

        def sb(name, shape, dt=F32):
            return sbx(ctx, name, shape, dt)

        ps = [ctx.enter_context(nc.psum_tensor(f"ps{i}", [P, HALF], F32)) for i in range(8)]
        PB4 = ps[4:8]

        x1d = nc.dram_tensor("x1_rows", [NROW, D], F32, kind="Internal").ap()
        accd = nc.dram_tensor("ffn_rows", [NROW, D], F32, kind="Internal").ap()
        slotd = nc.dram_tensor("slot_table", [P * NBT, 2], I32, kind="Internal").ap()
        blockd = nc.dram_tensor("block_table", [2 * P, 4], I32, kind="Internal").ap()

        ident = sb("ident", [P, P])
        ones = sb("ones", [P, P])
        avg = sb("avg", [P, P])
        mask = sb("mask", [P, len(LEVELS), C // 2], BF16)
        diag = sb("diag", [P, C], BF16)
        ones_b = sb("ones_b", [P, P], BF16)
        before = sb("before", [P, P], BF16)
        chan = sb("chan", [P, NCV])
        sp4 = sb("sp4", [P, WT, 8])
        lb1 = sb("lb1", [P, 2, WT])
        eps = sb("eps", [P, 2])

        lay_a = ExitStack()
        ring = sbx(lay_a, "ring", [P, 6, KD, P])
        bring = sbx(lay_a, "bring", [P, 2, WT, P])
        xT = sbx(lay_a, "xT", [P, KD, T])
        u_tok = sbx(lay_a, "u_tok", [P, G, SC, CH])
        yC = sbx(lay_a, "yC", [P, WT, T])
        N4 = sbx(lay_a, "N4", [P, 4, T])
        rgt = N4
        fN, qN, gN, vN = (N4[:, n] for n in range(4))
        yB = u_tok[:, :, :, :].rearrange("p g s c -> p (g s c)").rearrange("p (c t) -> p c t", c=WT)
        yT = yB

        lay_1 = ExitStack()
        rgx = sbx(lay_1, "rgx", [P, WT, T])
        s5p = sbx(lay_1, "s5p", [P, 3 * GP])
        s5w = sbx(lay_1, "s5w", [P, 4, GP, CH])
        s5d = sbx(lay_1, "s5d", [P, W])
        pt = sbx(lay_1, "pt", [P, NPT, GP])
        pti = sbx(lay_1, "pti", [P, GP], I32)
        Bb = sbx(lay_1, "Bb", [P, 2, GP, CH])
        OutR = sbx(lay_1, "OutR", [P, HP, 9, CH])
        OutI = sbx(lay_1, "OutI", [P, HP, 9, CH])
        InR = sbx(lay_1, "InR", [P, HP, SC, CH])
        InI = sbx(lay_1, "InI", [P, HP, SC, CH])
        InT = sbx(lay_1, "InT", [P, 2, HP, P])
        ER = sbx(lay_1, "ER", [P, HP, NM])
        EI = sbx(lay_1, "EI", [P, HP, NM])
        R8 = sbx(lay_1, "R8", [P, HP, NM])
        Hs = sbx(lay_1, "Hs", [P, 2, HP, NM])
        TU = sbx(lay_1, "TU", [P, 4 * HP, P])
        Tg, uT = TU[:, 0:2 * HP, :], TU[:, 2 * HP:4 * HP, :]
        glut = TU[:, :, :].rearrange("p a b -> p (a b)").rearrange("p (j t) -> p j t", j=WT)
        xc = uT.rearrange("p (s a) m -> p s (a m)", s=2)
        Ksb = Hs[:, :, :, :].rearrange("p a b m -> p (a b) m")
        WR, WI = (InR[:, :, :, :].rearrange("p g s c -> p g (s c)"), InI[:, :, :, :].rearrange("p g s c -> p g (s c)"))
        ytok = rgx[:, :, :].rearrange("p a b -> p (a b)").rearrange("p (s w) -> p s w", s=SC)
        lay_1.close()

        lay_2 = ExitStack()
        mixT = sbx(lay_2, "mixT", [P, KD, T])
        yA = sbx(lay_2, "yA", [P, WT, T])
        sig = sbx(lay_2, "sig", [P, 2, HALF])
        lay_3 = ExitStack()
        Fd = sbx(lay_3, "Fd", [P, T])
        qs = sbx(lay_3, "qs", [P, T])
        kk = sbx(lay_3, "kk", [P, T])
        Gd = sbx(lay_3, "Gd", [P, T])
        qF = sbx(lay_3, "qF", [P, T])
        kG = sbx(lay_3, "kG", [P, T])
        St = sbx(lay_3, "St", [P, T])
        tmp = sbx(lay_3, "tmp", [P, T])
        vtok = sbx(lay_3, "vtok", [P, NCH, P])
        kGt = tmp[:, :].rearrange("p (n d) -> p n d", n=NCH)
        Sall = kG[:, :].rearrange("p (n d) -> p n d", n=NCH)
        lay_3.close()
        lay_4 = ExitStack()
        wout = sbx(lay_4, "wout", [P, KD, D])
        xr, x1 = N4[:, 0], N4[:, 1:3]
        x1T = N4[:, 3].rearrange("p (k t) -> p k t", k=KD)
        ln1 = sbx(lay_4, "ln1", [P, 2, D])
        bst = sbx(lay_4, "bst", [P, 2, 6])
        mv = sbx(lay_4, "mv", [P, 4])
        rwt = sbx(lay_4, "rwt", [P, KD, E])
        lay_4.close()
        lay_2.close()
        lay_a.close()

        lay_f = ExitStack()
        fr = sbx(lay_f, "fr", [P, KD, D])
        lay_f.close()
        lay_m = ExitStack()
        wts = sbx(lay_m, "wts", [P, 3, 2, NW], F32R)
        slt = sbx(lay_m, "slt", [P, NBT, 2], I32)
        i8 = sbx(lay_m, "i8", [P, 3, KD, 8], I32)
        tokw = sbx(lay_m, "tokw", [P, KD, 8, 2], I32)
        ec = sbx(lay_m, "ec", [P, 6, E + 1])
        eci = sbx(lay_m, "eci", [P, 3, E + 1], I32)
        bno = sbx(lay_m, "bno", [P, 2])
        boi = sbx(lay_m, "boi", [P, 2, 4], I32)
        btab = sbx(lay_m, "btab", [1, 2 * P, 4], I32)
        xg = sbx(lay_m, "xg", [P, 2, D])
        xgT = sbx(lay_m, "xgT", [P, 2, 2, KD, P], F32R)
        si = sbx(lay_m, "si", [P, 2, EH])
        hm = sbx(lay_m, "hm", [P, 2, EH])
        hTs = sbx(lay_m, "hTs", [P, 2, 2, P], F32R)
        yo = sbx(lay_m, "yo", [P, 2, D])
        ix = sbx(lay_m, "ix", [P, 2], I32)
        sx = sbx(lay_m, "sx", [P, 2], I32)
        wx = sbx(lay_m, "wx", [P, 2])
        ln2 = sbx(lay_m, "ln2", [P, 2, D])
        sltf = slt[:, :, :].bitcast(F32)
        fst = sbx(lay_m, "fst", [P, 2, 2, 6])
        fmv = sbx(lay_m, "fmv", [P, 2, 5])
        lay_m.close()

        lay_r = ExitStack()
        sbx(lay_r, "slots_above", [P, 120 * 1024 // 4])
        sc = sbx(lay_r, "sc", [P, KD, E])
        bi = sbx(lay_r, "bi", [P, KD, E])
        top2 = sbx(lay_r, "top2", [P, KD, NG, 8])
        gs = sbx(lay_r, "gs", [P, KD, NG])
        gr = sbx(lay_r, "gr", [P, 3, KD, NG])
        ma = sbx(lay_r, "ma", [P, KD, E])
        mr = sbx(lay_r, "mr", [P, KD, E])
        m8 = sbx(lay_r, "m8", [P, KD, 8])
        sel = sbx(lay_r, "sel", [P, KD, E])
        selb = sbx(lay_r, "selb", [P, KD, E], BF16)
        wt = sbx(lay_r, "wt", [P, KD, E])
        key = sbx(lay_r, "key", [P, KD, E])
        eq = sbx(lay_r, "eq", [P, KD, E])
        k8 = sbx(lay_r, "k8", [P, KD, 8])
        w8 = sbx(lay_r, "w8", [P, 8, KD])
        den = sbx(lay_r, "den", [P, KD])
        bcmp = sbx(lay_r, "bcmp", [P, 2, E + 1])
        bof = sbx(lay_r, "bof", [P, 2, 2])
        rb = sbx(lay_r, "rb", [P, E])
        lay_r.close()

        s_x = [sem(f"x_loaded{i}") for i in range(4)]
        s_par = sem("params_loaded")
        s_s5par = sem("s5_params_loaded")
        s_const = sem("constants_built")
        s_pool = sem("pool_chain")
        s_dve = sem("dve_chain")
        s_act = sem("act_chain")
        a_go = sem("act_waited")
        p_go = sem("pool_waited")
        w_full = [sem(f"w_full{i}") for i in range(6)]
        b_full = [sem(f"bw_full{i}") for i in range(2)]
        k_full = [sem(f"bank_full{i}") for i in range(4)]
        k_free = [sem(f"bank_free{i}") for i in range(4)]
        s_sp = sem("rg_rate_exp")
        s_rate = sem("rg_rate_ready")
        s_conv = sem("rg_conv_done")
        s_rgmm = sem("rg_gate_products")
        s_rgact = sem("rg_gates_done")
        s_rgsq = sem("rg_sqrt_done")
        s_rgy = sem("rg_tile_done")
        s_trig = sem("s5_trig_in")
        s_trigo = sem("s5_trig_out")
        s_tab = sem("s5_tables")
        s_pe5 = sem("s5_pe_steps")
        s_ev5 = sem("s5_evacuated")
        s_toep = sem("s5_toeplitz_placed")
        s_H = sem("s5_states_ready")
        s_y5 = sem("s5_y_tokens")
        s_gelu5 = sem("s5_gelu_done")
        s_glua = sem("s5_glu_gate")
        s_yB = sem("yB_done")
        h_q = sem("head_q_ready")
        h_k = sem("head_k_F_ready")
        h_F = sem("head_F_level")
        h_G = sem("head_G_level")
        h_qF = sem("head_qF_ready")
        h_kG = sem("head_kG_ready")
        h_lvl = sem("level_products")
        h_lfree = sem("level_bank_free")
        h_pe = sem("head_pe_steps")
        h_ev = sem("head_act_evacs")
        h_S = sem("states_ready")
        h_o = sem("head_output_done")
        g_mix = sem("gate_mixed")
        s_wo = sem("w_out_loaded")
        s_ln1 = sem("ln1_router_loaded")
        s_xr = sem("x_rows_loaded")
        s_xrf = sem("x_rows_used")
        s_var = sem("variance_ready")
        s_std = sem("deviation_ready")
        s_x1 = sem("x1_tile_ready")
        s_x1s = [sem(f"x1_tile_stored{i}") for i in range(2)]
        s_xtr = sem("x1_tile_turned")
        s_x1T = sem("x1T_ready")
        s_lg = sem("logits_ready")
        s_z = sem("zero_rows_ready")
        s_zd = sem("zero_rows_stored")
        s_xa = sem("residual_rows_ready")
        s_xas = sem("residual_rows_stored")
        s_sc_ = sem("scores_done")
        s_sel = sem("selection_ready")
        s_pos = sem("positions_counted")
        s_tw = sem("token_numbers")
        s_slt0 = sem("slot_table_default")
        s_slt1 = sem("slot_default_stored")
        s_adr = sem("slot_addresses")
        s_scat = sem("slots_scattered")
        s_slt = sem("slot_table_loaded")
        s_bt0 = sem("block_table_ready")
        s_bt1 = sem("block_table_stored")
        s_bt = sem("block_table_loaded")
        s_rb = sem("router_bias_loaded")
        w_h = [sem(f"expert_w13_in{i}") for i in range(3)]
        w_o = [sem(f"expert_w2_in{i}") for i in range(3)]
        s_wh = sem("w13_of_experts")
        s_wo2 = sem("w2_of_experts")
        e_hih = sem("w13_high_parts")
        e_loh = sem("w13_low_parts")
        e_hio = sem("w2_high_parts")
        e_loo = sem("w2_low_parts")
        e_Tl = sem("rowsT_low_ready")
        e_hTl = sem("hiddenT_low_ready")
        e_g = [sem(f"rows_gathered{i}") for i in range(2)]
        e_T = sem("rows_turned")
        e_Te = sem("rowsT_ready")
        e_H = sem("hidden_products")
        e_si = sem("silu_ready")
        e_hm = sem("hidden_ready")
        e_hT = sem("hidden_turned")
        e_hTe = sem("hiddenT_ready")
        e_Y = sem("output_products")
        e_wx = sem("row_weight_ready")
        e_ya = sem("output_half_act")
        e_yd = sem("output_half_dve")
        e_sc = sem("rows_adding")
        e_add = sem("rows_added")
        f_in = [sem(f"ffn_rows_loaded{i}") for i in range(KD)]
        f_var = sem("ffn_variance")
        f_std = sem("ffn_deviation")
        f_nb = sem("ffn_scale_ready")
        f_n = sem("ffn_normalised")
        f_g = sem("ffn_gain_done")
        f_y = sem("out_tile_ready")
        f_out = sem("out_tiles_stored")

        def counts(eng):
            eng.wait_ge(s_bt, 16)
            return eng.value_load(eci[0:1, 2, 0:1], min_val=(SHB + E) // 2, max_val=NBMAX // 2)

        def block_entry(eng, c, col, top):
            e = btab[0:1, c:c + 1, col:col + 1] if isinstance(c, int) else btab[0:1, bass.ds(c, 1), col:col + 1]
            return eng.value_load(e, min_val=0, max_val=top)

        def slot_cols(s, part, cols):
            return wts[:, s, part, cols] if isinstance(s, int) else wts[:, bass.ds(s, 1), part, cols].rearrange("p o n -> p (o n)")

        H13 = (slice(0, NH // 2), slice(NH // 2, NH))
        W2 = slice(NH, NW)

        def tail_sp(sp):
            sp.dma_start(ln1[:], a["ln1"]).then_inc(s_ln1, 16)
            sp.dma_start(rwt[:], a["router_w"]).then_inc(s_ln1, 16)
            sp.wait_ge(s_z, 1)
            zr = sig[:, :, :].rearrange("p a b -> p (a b)")
            sp.dma_start(x1d[T:NROW, :], zr).then_inc(s_zd, 16)

            def weights(slot, o, part):
                src = a["experts"][o] if isinstance(o, int) else a["experts"][bass.ds(o, 1)].rearrange("o p n -> (o p) n")
                for cols in ((W2,) if part else H13):
                    sp.dma_start(wts[:, slot, 0, cols].bitcast(F32), src[:, cols]).then_inc((w_h, w_o)[part][slot], 16)

            for t in range(KD):
                if t:
                    sp.wait_ge(s_xrf, t)
                sp.dma_start(xr, a["x"][t * P:(t + 1) * P, :]).then_inc(s_xr, 16)
                if t:
                    store_x1(sp, t - 1)
                if t == 0:
                    for o in range(2):
                        for part in range(2):
                            weights(o, o, part)
            store_x1(sp, KD - 1)
            for k in range(2):
                sp.wait_ge(s_x1s[k], 8 * KD)
            sp.wait_ge(s_lg, KD)
            sp.dma_start(rb[:], a["rb"]).then_inc(s_rb, 16)
            weights(2, 2, 0)
            sp.wait_ge(s_slt0, 3)
            sp.dma_start(slotd.rearrange("(p b) w -> p b w", b=NBT), slt[:]).then_inc(s_slt1, 16)
            sp.wait_ge(s_bt0, 1)
            sp.dma_start(blockd.rearrange("(k p) w -> p k w", k=2), boi[:]).then_inc(s_bt1, 16)
            sp.wait_ge(s_bt1, 16)
            sp.dma_start(btab[:], blockd.rearrange("(o b) w -> o b w", o=1)).then_inc(s_bt, 16)
            sp.wait_ge(s_xas, 16 * KD)

            def end_of(o):
                return sp.value_load(eci[0:1, 1, o:o + 1] if isinstance(o, int) else eci[0:1, 1, bass.ds(o, 1)],
                                     min_val=0, max_val=NBMAX)

            def announce(sems, slot, n, count):
                sp.wait_ge(sems[slot], n * (2 if sems is w_h else 1))
                sp.sem_inc(count, 1)

            weights(2, 2, 1)
            for o in range(2):
                announce(w_h, o, 16, s_wh)
            announce(w_o, 0, 16, s_wo2)
            sp.dma_start(ln2[:], a["ln2"]).then_inc(s_ln1, 16)
            sp.wait_ge(s_scat, 16 * KD * TOPK)
            sp.dma_start(slt[:, SHB:NBT], slotd.rearrange("(p b) w -> p b w", b=NBT)[:, SHB:NBT]).then_inc(s_slt, 16)
            sp.wait_ge(e_H, end_of(0))
            weights(0, 3, 0)
            announce(w_h, 2, 16, s_wh)
            announce(w_o, 1, 16, s_wo2)

            def next_weights(o, k, i):
                sp.wait_ge(e_H, end_of(o - 3))
                weights(k, o, 0)
                announce(w_h, (k + 2) % 3, i * 16 + (16 if k >= 1 else 0), s_wh)
                sp.wait_ge(e_Y, end_of(o - 4) + ONE)
                weights((k + 2) % 3, o - 1, 1)
                announce(w_o, (k + 1) % 3, i * 16 + (16 if k >= 2 else 0), s_wo2)

            for o in (4, 5):
                next_weights(o, o % 3, o // 3)
            with sp.Fori(2, 21) as i:
                for k in range(3):
                    next_weights(i * 3 + k, k, i)
            for o in (63, 64):
                next_weights(o, o % 3, o // 3)
            announce(w_h, 64 % 3, (64 // 3 + 1) * 16, s_wh)
            sp.wait_ge(e_Y, end_of(61) + ONE)
            weights(64 % 3, 64, 1)
            announce(w_o, 63 % 3, (63 // 3 + 1) * 16, s_wo2)
            announce(w_o, 64 % 3, (64 // 3 + 1) * 16, s_wo2)
            n = counts(sp)
            sp.wait_ge(e_sc, n * 32 + 16)
            for t in range(KD):
                sp.dma_start(fr[:, t], accd[t * P:(t + 1) * P, :]).then_inc(f_in[t], 16)
            for t in range(KD):
                store_out(sp, t)
            sp.wait_ge(f_out, 16 * KD)

        def store_x1(sp, t):
            sp.wait_ge(s_x1, t + 1)
            sp.dma_start(x1d[t * P:(t + 1) * P, :], x1[:, t % 2]).then_inc(s_x1s[t % 2], 16)
            sp.wait_ge(s_xa, t + 1)
            sp.dma_start(accd[t * P:(t + 1) * P, :], sig[:, :, :].rearrange("p a b -> p (a b)")).then_inc(s_xas, 16)

        def store_out(sp, t):
            sp.wait_ge(f_y, t + 1)
            sp.dma_start(out[t * P:(t + 1) * P, :], fr[:, t]).then_inc(f_out, 16)

        def tail_pool(pool, ch):
            g = nc.gpsimd
            pool.wait_ge(g_mix, 48 + ONE)
            g.memset(sig[:], 0.0).then_inc(s_z, 1)
            pool.wait_ge(s_z, 1)
            pool.dma_start(accd[T:NROW, :], sig[:, :, :].rearrange("p a b -> p (a b)")).then_inc(e_sc, 16)
            pool.wait_ge(s_lg, KD)
            g.iota(slt[:, 0:SHB, 0:1], pattern=[[P, SHB], [0, 1]], base=0, channel_multiplier=1).then_inc(s_slt0, 1)
            g.iota(slt[:, SHB:NBT, 0:1], pattern=[[0, NBT - SHB], [0, 1]], base=T, channel_multiplier=1).then_inc(s_slt0, 1)
            ch.add(g.memset(sltf[:, SHB:NBT, 1:2], 0.0))
            ch.wait()
            g.memset(sltf[:, 0:SHB, 1:2], 1.0).then_inc(s_slt0, 1)
            g.iota(bno[:, :], pattern=[[P, 2]], base=0, channel_multiplier=1, allow_small_or_imprecise_dtypes=True).then_inc(s_tw, 1)
            g.iota(tokw[:, :, :, 0:1], pattern=[[P, KD], [0, 8], [0, 1]], base=0, channel_multiplier=1).then_inc(s_tw, 1)
            pool.wait_ge(s_tw, 2)
            pool.wait_ge(s_slt1, 16)
            pool.wait_ge(s_adr, 1)
            for k in range(2):
                pool.wait_ge(s_x1s[k], 8 * KD)
            pool.wait_ge(s_zd, 16)
            pool.wait_ge(e_sc, 16)
            pool.wait_ge(s_xas, 16 * KD)

            def gather(k, c):
                pool.sem_inc(p_go, 1)
                ch.link(g.tensor_copy(ix[:, k:k + 1], slt[:, c, 0:1] if isinstance(c, int)
                                      else slt[:, bass.ds(c, 1), 0:1].rearrange("p o w -> p (o w)")))
                pool.sem_inc(p_go, 1)
                g.indirect_dma_start(out=xg[:, k, :], out_offset=None, in_=x1d,
                                     in_offset=bass.IndirectOffsetOnAxis(ap=ix[:, k:k + 1], axis=0)).then_inc(e_g[k], 16)

            def split2(o, s):
                pool.wait_ge(e_hio, o + 1)
                pool.sem_inc(p_go, 1)
                w, hi = slot_cols(s, 0, W2), slot_cols(s, 1, W2)
                g.tensor_tensor(w, w.bitcast(F32), hi.bitcast(F32), ALU.subtract).then_inc(e_loo, 1)

            def gather_after(c):
                pool.wait_ge(e_T, c - 1)
                pool.wait_ge(e_g[c % 2], 16 * (c // 2))
                gather(c % 2, c)

            def add_rows(b, u):
                pool.wait_ge(e_sc, b * 16 + 16)
                pool.sem_inc(e_add, 1)
                ch.link(g.tensor_copy(sx[:, u:u + 1], slt[:, b, 0:1] if isinstance(b, int)
                                      else slt[:, bass.ds(b, 1), 0:1].rearrange("p o w -> p (o w)")))
                pool.wait_ge(e_ya, b + (1 + ONE))
                pool.wait_ge(e_yd, b + (1 + ONE))
                pool.sem_inc(p_go, 1)
                g.indirect_dma_start(out=accd, out_offset=bass.IndirectOffsetOnAxis(ap=sx[:, u:u + 1], axis=0),
                                     in_=yo[:, u, :], in_offset=None, compute_op=ALU.add).then_inc(e_sc, 16)

            gather(0, 0)
            gather(1, 1)
            split2(0, 0)
            gather_after(2)
            entries = [(t, j) for t in range(KD) for j in range(TOPK)]
            for b in range(SHB):
                if b + 3 < SHB:
                    gather_after(b + 3)
                for t, j in entries[b * 11:(b + 1) * 11]:
                    g.indirect_dma_start(out=slotd, out_offset=bass.IndirectOffsetOnAxis(ap=i8[:, 2, t, j:j + 1], axis=0),
                                         in_=tokw[:, t, j, :], in_offset=None).then_inc(s_scat, 16)
                if b + 3 > SHB:
                    gather_after(b + 3)
                if b == SHB - 1:
                    split2(1, 1)
                add_rows(b, b % 2)
                if b + 3 == SHB:
                    pool.wait_ge(s_slt, 16)
                    gather_after(SHB)
            n = counts(pool)
            with pool.Fori(SHB // 2, n) as i:
                ch.enter(i, 4, SHB // 2)
                for u in range(2):
                    b = i * 2 + u
                    pool.wait_ge(e_T, i * 2 + (u + 2))
                    pool.wait_ge(e_g[1 - u], i * 16 + (16 + 16 * u))
                    gather(1 - u, i * 2 + (u + 3))
                    first = block_entry(pool, i * 2 + (u + 1), 2, 1)
                    with pool.If(first > 0):
                        split2(block_entry(pool, i * 2 + (u + 1), 0, E), block_entry(pool, i * 2 + (u + 1), 1, 2))
                    add_rows(b, u)
                ch.base = 0

            for t in range(KD):
                pool.wait_ge(f_g, t + 1)
                g.tensor_tensor(fr[:, t], fr[:, t], ln2[:, 1], ALU.add).then_inc(f_y, 1)

        def tail_pe(pe):
            mm, tr = nc.tensor.matmul, nc.tensor.transpose
            pe.wait_ge(s_wo, 16)
            pe.wait_ge(g_mix, 48 + ONE)
            pe.wait_ge(s_ln1, 32)
            def project_out(t, h):
                b = 2 * (t % 2) + h
                pe.wait_ge(k_free[b], U_WO + t // 2)
                for k in range(KD):
                    ins = mm(ps[b][:], mixT[:, k, t * P:(t + 1) * P], wout[:, k, h * HALF:(h + 1) * HALF],
                             start=k == 0, stop=k == KD - 1)
                ins.then_inc(k_full[b], 1)

            for t in range(KD + 1):
                if t < KD:
                    project_out(t, 0)
                if t >= 1:
                    pe.wait_ge(s_x1, t)
                    pe.wait_ge(s_x1T, t - 1)
                    for k in range(KD):
                        ins = tr(ps[4 + k // 4][:, (k % 4) * P:(k % 4 + 1) * P], x1[:, (t - 1) % 2, k * P:(k + 1) * P], ident[:])
                    ins.then_inc(s_xtr, 1)
                if t < KD:
                    project_out(t, 1)
                if t >= 1:
                    pe.wait_ge(s_x1T, t)
                    for k in range(KD):
                        ins = mm(ps[6][:, (t - 1) * E:t * E], x1T[:, k, :], rwt[:, k, :], start=k == 0, stop=k == KD - 1)
                    ins.then_inc(s_lg, 1)
            pe.wait_ge(s_sel, 1)
            for t in range(KD):
                o = ps[4][:, t * E:(t + 1) * E]
                ins = mm(o, before[:], selb[:, t], start=True, stop=t == 0)
                for t2 in range(t):
                    ins = mm(o, ones_b[:], selb[:, t2], start=False, stop=t2 == t - 1)
            for t in range(KD):
                ins = mm(ps[5][:, 0:E], ones_b[:], selb[:, t], start=t == 0, stop=t == KD - 1)
            ins.then_inc(s_pos, 1)

            n = counts(pe)

            def turn(k, c16, c):
                pe.wait_ge(e_g[k], c16)
                if not (isinstance(c, int) and c == 0):
                    pe.wait_ge(e_Te, c)
                    pe.wait_ge(e_Tl, c)
                for q in range(KD):
                    ins = tr(ps[q // 4][:, (q % 4) * P:(q % 4 + 1) * P], xg[:, k, q * P:(q + 1) * P], ident[:])
                ins.then_inc(e_T, 1)

            def product(o, left, s, c0, first, last):
                for n, (x, w) in enumerate(((1, 1), (1, 0), (0, 1))):
                    ins = mm(o, left(x), wts[:, bass.ds(s, 1), w, c0:c0 + HALF].rearrange("p o n -> p (o n)"),
                             start=first and n == 0, stop=last and n == 2)
                return ins

            def hidden(k, o, s, te, free):
                pe.wait_ge(e_Te, te)
                pe.wait_ge(e_Tl, te)
                if free is not None:
                    pe.wait_ge(e_hm, free + ONE)
                for q in range(KD):
                    if q % (KD // 2) == 0:
                        half = 1 + q // (KD // 2)
                        pe.wait_ge(e_hih, o * 2 + half)
                        pe.wait_ge(e_loh, o * 2 + half)
                    ins = product(ps[2 + k][:], lambda x: xgT[:, k, x, q, :], s, q * 2 * EH, q == 0, q == KD - 1)
                ins.then_inc(e_H, 1)

            turn(0, 16, 0)
            turn(1, 16, 1)
            hidden(0, block_entry(pe, 0, 0, E), block_entry(pe, 0, 1, 2), 1, None)
            with pe.Fori(0, n) as i:
                for u in range(2):
                    o1, s1, o0, s0 = (block_entry(pe, i * 2 + (u + n), *x) for n in (1, 0) for x in ((0, E), (1, 2)))
                    pe.wait_ge(e_hm, i * 2 + (u + 1) + ONE)
                    pe.wait_ge(e_hTe, i * 2 + u + ONE)
                    pe.wait_ge(e_hTl, i * 2 + u + ONE)
                    for q in range(2):
                        ins = tr(ps[4][:, q * P:(q + 1) * P], hm[:, u, q * P:(q + 1) * P], ident[:])
                    ins.then_inc(e_hT, 1)
                    hidden(1 - u, o1, s1, i * 2 + (u + 2), i * 2 + u)
                    turn(u, i * 16 + 32, i * 2 + (u + 2))
                    pe.wait_ge(e_hio, o0 + 1)
                    pe.wait_ge(e_loo, o0 + 1)
                    pe.wait_ge(e_hTe, i * 2 + (u + 1) + ONE)
                    pe.wait_ge(e_hTl, i * 2 + (u + 1) + ONE)
                    pe.wait_ge(e_ya, i * 2 + u + ONE)
                    pe.wait_ge(e_yd, i * 2 + u + ONE)
                    for h in range(2):
                        for q in range(2):
                            ins = product(ps[6 + h][:], lambda x: hTs[:, x, q, :], s0, NH + q * D + h * HALF, q == 0, q == 1)
                    ins.then_inc(e_Y, 1)

        def tail_act(act):
            A = nc.scalar.activation
            for t in range(KD + 1):
                if t >= 1:
                    act.wait_ge(s_x1, t)
                    act.wait_ge(s_zd, 16)
                    act.wait_ge(e_sc, 16)
                    if t >= 2:
                        act.wait_ge(s_xas, 16 * (t - 1))
                    A(sig[:, :, :].rearrange("p a b -> p (a b)"), x1[:, (t - 1) % 2], ACT.Copy, scale=ALPHA).then_inc(s_xa, 1)
                    act.wait_ge(s_xtr, t)
                    act.wait_ge(s_lg, t - 1)
                    for b in range(2):
                        ins = A(x1T[:, 4 * b:4 * b + 4, :].rearrange("p a b -> p (a b)"), ps[4 + b][:], ACT.Copy)
                    ins.then_inc(s_x1T, 1)
                if t < KD:
                    act.wait_ge(s_var, t + 1)
                    A(mv[:, 2:3], mv[:, 1:2], ACT.Sqrt, bias=eps[:, 0:1]).then_inc(s_std, 1)
            act.wait_ge(s_lg, KD)
            A(sc[:].rearrange("p a b -> p (a b)"), ps[6][:], ACT.Sigmoid).then_inc(s_sc_, 1)
            n = counts(act)

            def split13(o, s):
                act.wait_ge(s_wh, o + 1)
                act.sem_inc(a_go, 1)
                for cols in H13:
                    A(slot_cols(s, 1, cols), slot_cols(s, 0, cols).bitcast(F32), ACT.Copy).then_inc(e_hih, 1)

            def split2(o, s):
                act.wait_ge(s_wo2, o + 1)
                act.sem_inc(a_go, 1)
                A(slot_cols(s, 1, W2), slot_cols(s, 0, W2).bitcast(F32), ACT.Copy).then_inc(e_hio, 1)

            def rowsT(k, t, free):
                act.wait_ge(e_T, t)
                if free is not None:
                    act.wait_ge(e_H, free)
                for b in range(2):
                    ins = A(xgT[:, k, 1, 4 * b:4 * b + 4, :].rearrange("p a b -> p (a b)"), ps[b][:], ACT.Copy)
                ins.then_inc(e_Te, 1)

            def silu(k, h, free):
                act.wait_ge(e_H, h)
                if free is not None:
                    act.wait_ge(e_hm, free + ONE)
                A(si[:, k, :], ps[2 + k][:, 0:EH], ACT.Silu).then_inc(e_si, 1)

            split13(0, 0)
            split2(0, 0)
            rowsT(0, 1, None)
            rowsT(1, 2, None)
            silu(0, 1, None)
            with act.Fori(0, n) as i:
                for u in range(2):
                    act.wait_ge(e_hT, i * 2 + (u + 1) + ONE)
                    act.wait_ge(e_Y, i * 2 + u + ONE)
                    A(hTs[:, 1].rearrange("p a b -> p (a b)"), ps[4][:, 0:2 * P], ACT.Copy).then_inc(e_hTe, 1)
                    first = block_entry(act, i * 2 + (u + 2), 2, 1)
                    with act.If(first > 0):
                        split13(block_entry(act, i * 2 + (u + 2), 0, E), block_entry(act, i * 2 + (u + 2), 1, 2))
                    first = block_entry(act, i * 2 + (u + 1), 2, 1)
                    with act.If(first > 0):
                        split2(block_entry(act, i * 2 + (u + 1), 0, E), block_entry(act, i * 2 + (u + 1), 1, 2))
                    silu(1 - u, i * 2 + (u + 2), i * 2 + u)
                    rowsT(u, i * 2 + (u + 3), i * 2 + (u + 1))
                    act.wait_ge(e_Y, i * 2 + (u + 1) + ONE)
                    act.wait_ge(e_wx, i * 2 + (u + 1))
                    act.wait_ge(e_add, i * 2 + (u + 1))
                    A(yo[:, u, 0:HALF], ps[6][:], ACT.Copy, scale=wx[:, u:u + 1]).then_inc(e_ya, 1)
            for t in range(KD + 1):
                if t < KD:
                    m = fmv[:, t % 2]
                    act.wait_ge(f_var, t + 1)
                    A(m[:, 2:3], m[:, 1:2], ACT.Sqrt, bias=eps[:, 0:1]).then_inc(f_std, 1)
                if t >= 1:
                    m, x = fmv[:, (t - 1) % 2], fr[:, t - 1]
                    act.wait_ge(f_nb, t)
                    A(x, x, ACT.Identity, bias=m[:, 4:5], scale=m[:, 3:4]).then_inc(f_n, 1)

        def tail_dve(dve, ch):
            V = nc.vector
            tt, ts, stt = V.tensor_tensor, V.tensor_scalar, V.scalar_tensor_tensor
            L, N = ch.link, ch.add
            bc = lambda x, shape: x.broadcast_to(shape)

            def layernorm(x, st, m, gb, var, std, done, t):
                for h in range(2):
                    N(V.bn_stats(st[:, h, :], x[:, h * HALF:(h + 1) * HALF]))
                ch.wait()
                V.bn_aggr(m[:, 0:2], st[:, :, :].rearrange("p a b -> p (a b)")).then_inc(var, 1)
                dve.wait_ge(std, t + 1)
                L(V.reciprocal(m[:, 3:4], m[:, 2:3]))
                L(ts(x, x, m[:, 0:1], m[:, 3:4], ALU.subtract, ALU.mult))
                L(tt(x, x, gb[:, 0], ALU.mult))
                tt(x, x, gb[:, 1], ALU.add).then_inc(done, 1)

            dve.wait_ge(s_ln1, 32)
            for t in range(KD):
                dve.wait_ge(s_xr, 16 * (t + 1))
                if t >= 2:
                    dve.wait_ge(s_x1s[t % 2], 16 * (t // 2))
                    dve.wait_ge(s_xtr, t - 1)
                    dve.wait_ge(s_xa, t - 1)
                x = x1[:, t % 2]
                for h in range(2):
                    b = 2 * (t % 2) + h
                    dve.wait_ge(k_full[b], U_WO + t // 2 + 1)
                    cols = slice(h * HALF, (h + 1) * HALF)
                    stt(x[:, cols], xr[:, cols], ALPHA, ps[b][:], ALU.mult, ALU.add).then_inc(k_free[b], 1)
                    dve.wait_ge(k_free[b], U_WO + t // 2 + 1)
                dve.sem_inc(s_xrf, 1)
                layernorm(x, bst, mv, ln1, s_var, s_std, s_x1, t)
            dve.wait_ge(s_sc_, 1)
            dve.wait_ge(s_rb, 16)
            L(tt(bi[:], sc[:], bc(rb[:].unsqueeze(1), [P, KD, E]), ALU.add))
            for t in range(KD):
                for q in range(NG):
                    N(V.max(top2[:, t, q, :], bi[:, t, q * 8:(q + 1) * 8]))
            ch.wait()
            L(tt(gs[:], top2[:, :, :, 0], top2[:, :, :, 1], ALU.add))
            L(V.memset(gr[:, 0], 0.0))
            for q in range(NG):
                v = gs[:, :, q:q + 1]
                if q < NG - 1:
                    n = NG - 1 - q
                    L(tt(gr[:, 1, :, q + 1:], bc(v, [P, KD, n]), gs[:, :, q + 1:], ALU.is_ge))
                if q > 0:
                    L(tt(gr[:, 1, :, 0:q], bc(v, [P, KD, q]), gs[:, :, 0:q], ALU.is_gt))
                L(V.memset(gr[:, 1, :, q:q + 1], 0.0))
                L(tt(gr[:, 0], gr[:, 0], gr[:, 1], ALU.add))
            L(ts(gr[:, 1], gr[:, 0], 4.0, None, ALU.is_lt))
            L(ts(gr[:, 2], gr[:, 1], BIG, -BIG, ALU.mult, ALU.add))
            for t in range(KD):
                v4 = lambda x: x[:, t].rearrange("p (q e) -> p q e", q=NG)
                N(tt(v4(ma), v4(bi), bc(gr[:, 1, t].unsqueeze(2), [P, NG, 8]), ALU.mult))
            ch.wait()
            for t in range(KD):
                v4 = lambda x: x[:, t].rearrange("p (q e) -> p q e", q=NG)
                N(tt(v4(ma), v4(ma), bc(gr[:, 2, t].unsqueeze(2), [P, NG, 8]), ALU.add))
            ch.wait()
            for t in range(KD):
                N(V.max(m8[:, t, :], ma[:, t, :]))
            ch.wait()
            for t in range(KD):
                N(V.match_replace(out=mr[:, t, :], in_to_replace=m8[:, t, :], in_values=ma[:, t, :], imm_value=-3 * BIG))
            ch.wait()
            ts(selb[:], mr[:], -2 * BIG, None, ALU.is_lt).then_inc(s_sel, 1)
            L(ts(sel[:], mr[:], -2 * BIG, None, ALU.is_lt))
            L(tt(wt[:], sc[:], sel[:], ALU.mult))
            L(V.tensor_reduce(den[:], wt[:], AX, ALU.add))
            L(V.reciprocal(den[:], den[:]))
            L(ts(den[:], den[:], 2.5, None, ALU.mult))
            L(tt(wt[:], wt[:], bc(den[:].unsqueeze(2), [P, KD, E]), ALU.mult))
            dve.wait_ge(s_pos, 1)
            cI, cF, nb, end, beg = eci[:, 0, 0:E], ec[:, 0, 0:E], ec[:, 1, 0:E], ec[:, 2], ec[:, 3, 0:E]
            L(ts(cI, ps[5][:, 0:E], float(P - 1), None, ALU.add))
            L(ts(cI, cI, 7, None, ALU.logical_shift_right))
            L(ts(nb, cI, 1.0, None, ALU.max))
            L(V.memset(end[:, 0:1], float(SHB)))
            L(V.tensor_tensor_scan(end[:, 1:E + 1], ones[:, 0:E], nb, float(SHB), ALU.mult, ALU.add))
            L(tt(beg, end[:, 1:E + 1], nb, ALU.subtract))
            L(V.tensor_copy(eci[:, 1, :], end))
            dve.wait_ge(s_tw, 2)
            for k in range(2):
                N(ts(bcmp[:, k], end, bno[:, k:k + 1], None, ALU.is_le))
            ch.wait()
            L(V.tensor_reduce(bof[:, :, 0:1].rearrange("p k o -> p (k o)"), bcmp[:], AX, ALU.add))
            L(ts(bof[:, :, 0], bof[:, :, 0], float(E), None, ALU.min))
            L(V.tensor_copy(boi[:, :, 0], bof[:, :, 0]))
            L(ts(bof[:, :, 1], bof[:, :, 0], 171.0, None, ALU.mult))
            L(V.tensor_copy(boi[:, :, 1], bof[:, :, 1]))
            L(ts(boi[:, :, 1], boi[:, :, 1], 9, None, ALU.logical_shift_right))
            L(stt(bof[:, :, 1], boi[:, :, 1], -3.0, bof[:, :, 0], ALU.mult, ALU.add))
            L(V.tensor_copy(boi[:, :, 1], bof[:, :, 1]))
            for k in range(2):
                N(ts(bcmp[:, k], end, bno[:, k:k + 1], None, ALU.is_equal))
            ch.wait()
            L(V.tensor_reduce(bof[:, :, 1:2].rearrange("p k o -> p (k o)"), bcmp[:, :, 0:E], AX, ALU.add))
            L(V.tensor_copy(boi[:, :, 2], bof[:, :, 1]))
            L(V.memset(boi[:, :, 3:4], 0))
            L(ts(eci[:, 2, 0:1], end[:, E:E + 1], 1.0, None, ALU.add))
            ts(eci[:, 2, 0:1], eci[:, 2, 0:1], 1, None, ALU.logical_shift_right).then_inc(s_bt0, 1)
            L(ts(beg, beg, float(P), 1.0, ALU.mult, ALU.add))
            L(tt(key[:], ps[4][:].rearrange("p (t e) -> p t e", t=KD), bc(beg.unsqueeze(1), [P, KD, E]), ALU.add))
            L(tt(key[:], key[:], sel[:], ALU.mult))
            for t in range(KD):
                N(V.max(k8[:, t, :], key[:, t, :]))
            ch.wait()
            for j in range(TOPK):
                L(tt(eq[:], key[:], bc(k8[:, :, j:j + 1], [P, KD, E]), ALU.is_equal))
                L(tt(eq[:], eq[:], wt[:], ALU.mult))
                L(V.tensor_reduce(w8[:, j, :], eq[:], AX, ALU.add))
            L(V.tensor_copy(tokw[:, :, :, 1].bitcast(F32), w8[:].rearrange("p j t -> p t j")))
            L(ts(i8[:, 0], k8[:], -1.0, None, ALU.add))
            L(ts(i8[:, 1], i8[:, 0], P - 1, None, ALU.bitwise_and))
            L(ts(i8[:, 0], i8[:, 0], 7, None, ALU.logical_shift_right))
            stt(i8[:, 2], i8[:, 1], float(NBT), i8[:, 0], ALU.mult, ALU.add).then_inc(s_adr, 1)
            n = counts(dve)

            def hid(k, h, free):
                dve.wait_ge(e_si, h)
                if free is not None:
                    dve.wait_ge(e_hT, free + ONE)
                tt(hm[:, k, :], si[:, k, :], ps[2 + k][:, EH:2 * EH], ALU.mult).then_inc(e_hm, 1)

            def low(s, cols, done):
                w, hi = slot_cols(s, 0, cols), slot_cols(s, 1, cols).bitcast(F32)
                tt(w, w.bitcast(F32), hi, ALU.subtract).then_inc(done, 1)

            def split13(o, s, n):
                dve.wait_ge(e_hih, o * 2 + (n + 1))
                low(s, H13[n], e_loh)

            def rowsT_low(k, t):
                dve.wait_ge(e_Te, t)
                for b in range(2):
                    r = slice(4 * b, 4 * b + 4)
                    v = lambda x: xgT[:, k, x, r, :].rearrange("p a b -> p (a b)")
                    ins = tt(v(0), ps[b][:], v(1).bitcast(F32), ALU.subtract)
                ins.then_inc(e_Tl, 1)

            dve.wait_ge(s_slt0, 3)
            split13(0, 0, 0)
            split13(0, 0, 1)
            rowsT_low(0, 1)
            rowsT_low(1, 2)
            hid(0, 1, None)
            with dve.Fori(0, n) as i:
                for u in range(2):
                    first = block_entry(dve, i * 2 + (u + 2), 2, 1)
                    dve.wait_ge(e_ya, i * 2 + u + ONE)
                    dve.wait_ge(e_yd, i * 2 + u + ONE)
                    V.tensor_copy(wx[:, u:u + 1], sltf[:, bass.ds(i * 2 + u, 1), 1:2].rearrange("p o w -> p (o w)")).then_inc(e_wx, 1)
                    dve.wait_ge(e_hTe, i * 2 + (u + 1) + ONE)
                    h_ = lambda x: hTs[:, x].rearrange("p a b -> p (a b)")
                    tt(h_(0), ps[4][:, 0:2 * P], h_(1).bitcast(F32), ALU.subtract).then_inc(e_hTl, 1)
                    with dve.If(first > 0):
                        o, s = block_entry(dve, i * 2 + (u + 2), 0, E), block_entry(dve, i * 2 + (u + 2), 1, 2)
                        split13(o, s, 0)
                    hid(1 - u, i * 2 + (u + 2), i * 2 + u)
                    rowsT_low(u, i * 2 + (u + 3))
                    with dve.If(first > 0):
                        o, s = block_entry(dve, i * 2 + (u + 2), 0, E), block_entry(dve, i * 2 + (u + 2), 1, 2)
                        split13(o, s, 1)
                    dve.wait_ge(e_Y, i * 2 + (u + 1) + ONE)
                    dve.wait_ge(e_wx, i * 2 + (u + 1))
                    dve.wait_ge(e_add, i * 2 + (u + 1))
                    ts(yo[:, u, HALF:D], ps[7][:], wx[:, u:u + 1], None, ALU.mult).then_inc(e_yd, 1)
            dve.wait_ge(s_ln1, 48)
            for t in range(KD + 2):
                if t < KD:
                    dve.wait_ge(f_in[t], 16)
                    if t >= 2:
                        dve.wait_ge(f_n, t - 1)
                    for h in range(2):
                        N(V.bn_stats(fst[:, t % 2, h], fr[:, t, h * HALF:(h + 1) * HALF]))
                    ch.wait()
                    V.bn_aggr(fmv[:, t % 2, 0:2], fst[:, t % 2].rearrange("p a b -> p (a b)")).then_inc(f_var, 1)
                if 1 <= t <= KD:
                    m = fmv[:, (t - 1) % 2]
                    dve.wait_ge(f_std, t)
                    L(V.reciprocal(m[:, 3:4], m[:, 2:3]))
                    stt(m[:, 4:5], m[:, 0:1], -1.0, m[:, 3:4], ALU.mult, ALU.mult).then_inc(f_nb, 1)
                if t >= 2:
                    x = fr[:, t - 2]
                    dve.wait_ge(f_n, t - 1)
                    tt(x, x, ln2[:, 0], ALU.mult).then_inc(f_g, 1)

        def dyn(ap, i):
            if isinstance(i, int):
                return ap[:, i]
            x = ap[:, bass.ds(i, 1)]
            return x.rearrange("p o n -> p (o n)") if len(x.shape) == 3 else x.rearrange("p o a b -> p (o a) b")

        block = ctx.enter_context(nc.Block())

        @block.sync
        def _(sp):
            def load_w(slot, tile, bank, n):
                if n is not None:
                    sp.wait_ge(k_full[bank], n)
                src = a["w_in"][tile] if isinstance(tile, int) else a["w_in"][bass.ds(tile, 1)].rearrange("o p k c -> (o p) k c")
                sp.dma_start(ring[:, slot], src).then_inc(w_full[slot], 16)

            def load_b(slot, tile, n):
                if n is not None:
                    sp.wait_ge(k_full[3], n)
                src = a["w_branch"][tile] if isinstance(tile, int) else a["w_branch"][bass.ds(tile, 1)].rearrange("o p k c -> (o p) k c")
                sp.dma_start(bring[:, slot], src).then_inc(b_full[slot], 16)

            def load_gate(s, i, branch, n):
                load_w(4 + s, i * 2 + (T_GATE + KD * branch + s), 1, n)
                load_b(s, i * 2 + (KD * branch + s), n)

            load_w(0, T_RX, None, None)
            for q in range(4):
                sp.dma_start(xT[:, 2 * q:2 * q + 2], a["xT"][:, 2 * q:2 * q + 2]).then_inc(s_x[q], 16)
                if q == 0:
                    load_w(1, T_RX + 1, None, None)
            for s in (2, 3):
                load_w(s, T_RX + s, None, None)
            sp.dma_start(chan[:], a["chan"]).then_inc(s_par, 16)
            sp.dma_start(s5p[:], a["s5p"]).then_inc(s_s5par, 16)
            sp.dma_start(s5w[:], a["s5w"]).then_inc(s_s5par, 16)
            sp.dma_start(s5d[:], a["s5d"]).then_inc(s_s5par, 16)
            sp.dma_start(ring[:, 4], a["rg_w"]).then_inc(w_full[4], 16)
            for s in range(4):
                load_w(s, T_RG + s, 2 * (s % 2) + 1, s // 2 + 1)
            for s in range(4):
                load_w(s, T_SU + s, 2 * (s % 2) + 1, s // 2 + 3)
            for s, t in enumerate((T_F, T_Q, T_G, T_V)):
                load_w(s, t, 3, U_SU + 2)
            for half in range(2):
                sp.wait_ge(s_ev5, 3 * half + 3)
                for s in range(SC):
                    sp.dma_start(Tg[s * CH:(s + 1) * CH, :, s * CH:P], Ksb[0:CH, :, 0:P - s * CH]).then_inc(s_toep, 16)
                if half == 0:
                    sp.wait_ge(s_rgmm, WT)
                    sp.dma_start(ring[:, 4:6].rearrange("p a k c -> p (a k c)"), a["glu_w"]).then_inc(w_full[5], 16)
            sp.wait_ge(s_pe5, 18)
            for s in range(2):
                load_gate(s, 0, 2, None)
            for s, t in enumerate((T_F, T_Q, T_G, T_V)):
                load_w(s, t + 1, 2 * (s % 2) + 1, U_H0 + s // 2 + 1)
            with sp.Fori(1, WT - 1) as i:
                for s, t in enumerate((T_F, T_Q, T_G, T_V)):
                    load_w(s, i + (t + 1), 2 * (s % 2) + 1, i * 4 + (U_HL - 3 + s // 2))
                for s in range(2):
                    load_gate(s, i, 2, i * 4 + (U_HL - 1 + s))
            for s in range(2):
                load_gate(s, WT - 1, 2, (WT - 1) * 4 + (U_HL - 1 + s))
            for branch, u in ((1, U_GB), (0, U_GA)):
                with sp.Fori(0, 4) as i:
                    for s in range(2):
                        load_gate(s, i, branch, i * 2 + (u + s - 1))
            sp.wait_ge(h_o, WT + ONE)
            sp.dma_start(wout[:], a["w_out"]).then_inc(s_wo, 16)
            tail_sp(sp)

        @block.gpsimd
        def _(pool):
            ch = Chain(pool, s_pool)
            pool.sem_inc(h_kG, ONE)
            pool.sem_inc(e_add, 1)
            g = nc.gpsimd
            ch.add(g.memset(ident[:], 0.0))
            ch.add(g.memset(before[:], 1.0))
            ch.add(g.memset(ones[:], 1.0))
            ch.add(g.memset(avg[:], 1.0 / P))
            ch.add(g.memset(mask[:], 1.0))
            ch.add(g.memset(eps[:, 0:1], LN_EPS))
            ch.add(g.memset(eps[:, 1:2], RMS_EPS))
            ch.link(g.memset(Tg, 0.0))
            ch.add(g.affine_select(out=ident[:], in_=ident[:], compare_op=ALU.not_equal, fill=1.0, base=0,
                                   pattern=[[-1, P]], channel_multiplier=1))
            ch.add(g.affine_select(out=before[:], in_=before[:], compare_op=ALU.is_gt, fill=0.0, base=0,
                                   pattern=[[1, P]], channel_multiplier=-1))
            for n, h in enumerate(LEVELS):
                m = mask[:, n].rearrange("p (b j) -> p b j", j=h)
                nb = C // (2 * h)
                ch.wait()
                ch.link(g.affine_select(out=m, in_=m, compare_op=ALU.is_ge, fill=0.0, base=0,
                                        pattern=[[-2 * h, nb], [0, h]], channel_multiplier=1))
                ch.add(g.affine_select(out=m, in_=m, compare_op=ALU.is_ge, fill=0.0, base=h - 1,
                                       pattern=[[2 * h, nb], [0, h]], channel_multiplier=-1))
            ch.wait()
            ch.add(g.tensor_copy(ones_b[:], ones[:]))
            g.tensor_copy(diag[:], ident[:]).then_inc(s_const, 1)

            def head(i):
                pool.wait_ge(h_kG, i * 7 + ONE)
                pool.wait_ge(h_pe, i * 5 + ONE)
                pool.sem_inc(p_go, 1)
                ch.link(g.memset(Gd[:], 1.0))
                for n, h in enumerate(LEVELS):
                    Gv, Fv = (x[:, :].rearrange("p (b j) -> p b j", j=2 * h) for x in (Gd, Fd))
                    nb = T // (2 * h)
                    pool.wait_ge(h_F, i * 7 + (n + 1))
                    g.tensor_tensor(Gv[:, :, 0:h], Gv[:, :, 0:h], Fv[:, :, 2 * h - 1:2 * h].broadcast_to([P, nb, h]),
                                    ALU.mult).then_inc(h_G, 1)
                    pool.wait_ge(h_G, i * 7 + (n + 1))
                    pool.wait_ge(h_lvl, i * 8 + (n + 2))
                    if 0 < n < len(LEVELS) - 1:
                        kv, Gw, Kw = (x[:, :].rearrange("p (b j) -> p b j", j=4 * h)[:, :, 0:2 * h] for x in (kk, Gd, kG))
                        g.tensor_tensor(Kw, kv, Gw, ALU.mult).then_inc(h_kG, 1)
                    else:
                        g.tensor_tensor(kG[:], kk[:], Gd[:], ALU.mult).then_inc(h_kG, 1)
                    pool.wait_ge(h_kG, i * 7 + (n + 1) + ONE)

            pool.wait_ge(s_yB, WT)
            with pool.Fori(0, WT - 1) as i:
                ch.enter(i, 1)
                head(i)
                ch.leave(WT - 1)
            head(WT - 1)
            tail_pool(pool, ch)

        NORMAL = ("V f0 L0 f1 L1 q0 L2 q1 L3 g0 L4 g1 L5 v0 L6 v1 L7 G00 G01 KT B00 KV B01 G10 O G11 M B10 B11").split()
        LAST = "V L0 G00 L1 G01 L2 B00 L3 B01 L4 G10 L5 G11 L6 B10 L7 B11 KT KV O M".split()

        def use(step, last):
            kind, h = step[0], int(step[-1])
            if kind in "fq":
                return (0 if kind == "f" else 2) + h, 0
            if kind in "gv":
                return (0 if kind == "g" else 2) + h, 1
            return (0 if kind == "G" else 2) + h, (0 if last else 2) + int(step[1])

        @block.tensor
        def _(pe):
            mm, tr = nc.tensor.matmul, nc.tensor.transpose
            for one in (h_pe, e_hT, e_Y):
                pe.sem_inc(one, ONE)

            def claim(b, n):
                pe.wait_ge(k_free[b], n)

            def project(slot, nw, h, b, n):
                if h == 0:
                    pe.wait_ge(w_full[slot], nw)
                claim(b, n)
                for k in range(KD):
                    ins = mm(ps[b][:], ring[:, slot, k, :], xT[:, k, h * HALF:(h + 1) * HALF], start=k == 0, stop=k == KD - 1)
                ins.then_inc(k_full[b], 1)

            for q in range(4):
                pe.wait_ge(s_x[q], 16)
                for k in (2 * q, 2 * q + 1):
                    for t in range(2):
                        if k == 0:
                            pe.wait_ge(w_full[t], 16)
                        for h in range(2):
                            ins = mm(ps[2 * t + h][:], ring[:, t, k, :], xT[:, k, h * HALF:(h + 1) * HALF], start=k == 0, stop=k == KD - 1)
                            if k == KD - 1:
                                ins.then_inc(k_full[2 * t + h], 1)
            for t in range(2, 8):
                for h in range(2):
                    project(t % 4, 16 * (t // 4 + 1), h, 2 * (t % 2) + h, U_P1 + t // 2)

            pe.wait_ge(s_const, 1)
            rgw = ring[:, 4].rearrange("p (a j) c -> p a j c", a=2)
            for j in range(WT):
                for s in (2 * j, 2 * j + 1):
                    if s == 0:
                        for q in range(4):
                            pe.wait_ge(w_full[q], 48)
                    claim(s % 4, U_SU + s // 4)
                    for k in range(KD):
                        ins = mm(ps[s % 4][:], xT[:, k, s::SC], ring[:, 0:4, k, :], start=k == 0, stop=k == KD - 1)
                    ins.then_inc(k_full[s % 4], 1)
                pe.wait_ge(s_conv, j + 1)
                if j:
                    pe.wait_ge(s_rgact, 2 * j)
                else:
                    pe.wait_ge(w_full[4], 16)
                for m in range(2):
                    for h in range(2):
                        ins = mm(ps[4 + 2 * m + h][:], rgw[:, m, j, :], xc[:, j % 2, h * HALF:(h + 1) * HALF], start=True, stop=True)
                ins.then_inc(s_rgmm, 1)
            def by_rows(q):
                return PB4[2 * (q % 2) + q // 8][:, (q // 2 % 4) * P:(q // 2 % 4 + 1) * P]

            def s5_half(half):
                lo = 2 * HP * half
                if half:
                    pe.wait_ge(s_y5, 1)
                else:
                    pe.wait_ge(s_rgact, 2 * WT)
                    for q in range(4):
                        pe.wait_ge(k_free[q], U_SU + 2)
                for q in range(2 * HP):
                    ins = tr(PB4[q // 4][:, (q % 4) * P:(q % 4 + 1) * P], u_tok[:, lo + q].rearrange("p s c -> p (s c)"), ident[:])
                ins.then_inc(s_pe5, 1)
                yield
                pe.wait_ge(s_ev5, 3 * half + 1)
                pe.wait_ge(s_tab, half + 1)
                for part, src in ((0, InR), (1, InI)):
                    for q in range(HP):
                        ins = tr(PB4[2 * part + q // 4][:, (q % 4) * P:(q % 4 + 1) * P], src[:, q].rearrange("p s c -> p (s c)"), ident[:])
                ins.then_inc(s_pe5, 1)
                yield
                pe.wait_ge(s_ev5, 3 * half + 2)
                for q in range(2 * HP):
                    r = slice(NS * (q % 2), NS * (q % 2) + NS)
                    o = by_rows(q)[0:CH]
                    mm(o, Bb[r, 0, HP * half + q // 2, :], OutR[r, q // 2, 0:SC, :], start=True, stop=False)
                    ins = mm(o, Bb[r, 1, HP * half + q // 2, :], OutI[r, q // 2, 0:SC, :], start=False, stop=True)
                ins.then_inc(s_pe5, 1)
                yield
                pe.wait_ge(s_ev5, 3 * half + 3)
                for part in range(2):
                    for q in range(2 * HP):
                        o = PB4[2 * part + q // 8][NS * (q % 2):NS * (q % 2) + NS, (q // 2 % 4) * P:(q // 2 % 4 + 1) * P]
                        ins = mm(o, InT[:, part, q // 2, NS * (q % 2):NS * (q % 2) + NS], uT[:, q, :], start=True, stop=True)
                ins.then_inc(s_pe5, 1)
                yield
                pe.wait_ge(s_H, half + 1)
                pe.wait_ge(s_toep, 16 * SC * (half + 1))
                for q in range(2 * HP):
                    r = slice(NS * (q % 2), NS * (q % 2) + NS)
                    o = by_rows(q)
                    mm(o, uT[:, q, :], Tg[:, q, :], start=True, stop=False)
                    mm(o, Hs[r, 0, q // 2, :], OutR[r, q // 2, 1:SC + 1, :], start=False, stop=False)
                    ins = mm(o, Hs[r, 1, q // 2, :], OutI[r, q // 2, 1:SC + 1, :], start=False, stop=True)
                ins.then_inc(s_pe5, 1)
                yield

            def project_head(s):
                for h in range(2):
                    project(s, 64, h, 2 * (s % 2) + h, U_H0 + s // 2)

            halves = s5_half(0), s5_half(1)
            for _ in range(4):
                next(halves[0])
            project_head(0)
            project_head(1)
            next(halves[0])
            next(halves[1])
            project_head(2)
            for _ in range(3):
                next(halves[1])
            project_head(3)
            next(halves[1])
            for cj in range(WT):
                pe.wait_ge(s_gelu5, 2)
                if cj >= 2:
                    pe.wait_ge(s_ev5, 6 + cj - 1)
                else:
                    pe.wait_ge(s_y5, 2)
                for s in range(SC):
                    ins = tr(PB4[2 * (cj % 2) + s // 4][:, (s % 4) * P:(s % 4 + 1) * P], ytok[:, s, cj * P:(cj + 1) * P], ident[:])
                ins.then_inc(s_pe5, 1)
            glu = ring[:, 4:6].rearrange("p a k c -> p (a k c)").rearrange("p (k n) -> p k n", k=WT)
            pe.wait_ge(w_full[5], 16)
            pe.wait_ge(s_ev5, 10)
            for e in range(WT):
                if e >= 2:
                    pe.wait_ge(s_glua, e - 1)
                for h in range(2):
                    for k in range(WT):
                        ins = mm(PB4[2 * (e % 2) + h][:], glu[:, k, e * P:(e + 1) * P], yT[:, k, h * HALF:(h + 1) * HALF],
                                 start=k == 0, stop=k == WT - 1)
                ins.then_inc(s_pe5, 1)

            def gate(s, h, n, nw):
                if h == 0:
                    pe.wait_ge(w_full[4 + s], nw)
                claim(h, n)
                for k in range(KD):
                    ins = mm(ps[h][:], ring[:, 4 + s, k, :], xT[:, k, h * HALF:(h + 1) * HALF], start=k == 0, stop=k == KD - 1)
                ins.then_inc(k_full[h], 1)

            def branch(s, h, y, n, nb):
                if h == 0:
                    pe.wait_ge(b_full[s], nb)
                claim(2 + h, n)
                for k in range(WT):
                    ins = mm(ps[2 + h][:], bring[:, s, k, :], y[:, k, h * HALF:(h + 1) * HALF], start=k == 0, stop=k == WT - 1)
                ins.then_inc(k_full[2 + h], 1)

            def head(i, sched, last):
                for step in sched:
                    if step == "V":
                        pe.wait_ge(k_free[3], i * 4 + (U_HL - 2))
                        pe.wait_ge(h_ev, i * 4 + ONE)
                        for n in range(NCH):
                            ins = tr(ps[4 + n // 4][:, (n % 4) * P:(n % 4 + 1) * P], vN[:, n * P:(n + 1) * P], ident[:])
                        ins.then_inc(h_pe, 1)
                    elif step[0] == "L":
                        l = int(step[1])
                        if l == 0:
                            pe.wait_ge(h_ev, i * 4 + 1 + ONE)
                            pe.wait_ge(h_k, i + 1)
                            pe.wait_ge(h_q, i + 1)
                            for n in range(NCH):
                                ins = mm(ps[4 + n // 4][:, (n % 4) * P:(n % 4 + 1) * P], kk[:, n * P:(n + 1) * P], qs[:, n * P:(n + 1) * P],
                                         start=True, stop=True)
                        else:
                            pe.wait_ge(h_lfree, i * 8 + max(1, l - 1))
                            pe.wait_ge(h_qF, i * 8 + l + ONE)
                            if l > 1:
                                pe.wait_ge(h_kG, i * 7 + (l - 1) + ONE)
                            left = kk if l == 1 else kG
                            qc = qF[:, ((l - 1) % 2) * HALF:((l - 1) % 2 + 1) * HALF]
                            for n in range(NCH):
                                ins = mm(ps[4 + l % 2][:, n * 64:(n + 1) * 64], left[:, n * P:(n + 1) * P], qc[:, n * 64:(n + 1) * 64],
                                         start=True, stop=True)
                        ins.then_inc(h_lvl, 1)
                    elif step == "KT":
                        pe.wait_ge(h_lfree, i * 8 + 8)
                        pe.wait_ge(h_kG, i * 7 + 7 + ONE)
                        for n in range(NCH):
                            ins = tr(ps[4 + n // 4][:, (n % 4) * P:(n % 4 + 1) * P], kG[:, n * P:(n + 1) * P], ident[:])
                        ins.then_inc(h_pe, 1)
                    elif step == "KV":
                        pe.wait_ge(h_ev, i * 4 + 2 + ONE)
                        for n in range(NCH - 1):
                            ins = mm(ps[4 + n // 4][:, (n % 4) * P:(n % 4 + 1) * P], kGt[:, n, :], vtok[:, n, :], start=True, stop=True)
                        ins.then_inc(h_pe, 1)
                    elif step == "O":
                        pe.wait_ge(h_S, i + 1)
                        pe.wait_ge(h_qF, i * 8 + 8 + ONE)
                        pe.wait_ge(h_o, i + ONE)
                        for n in range(NCH):
                            o = ps[6 + n // 4][:, (n % 4) * P:(n % 4 + 1) * P]
                            ins = mm(o, vtok[:, n, :], St[:, n * P:(n + 1) * P], start=True, stop=n == 0)
                            if n:
                                ins = mm(o, Sall[:, n, :], qF[:, n * P:(n + 1) * P], start=False, stop=True)
                        ins.then_inc(h_pe, 1)
                    elif step == "M":
                        pe.wait_ge(h_ev, i * 4 + 3 + ONE)
                        for h in range(2):
                            ins = mm(ps[4 + h][:], avg[:], tmp[:, h * HALF:(h + 1) * HALF], start=True, stop=True)
                        ins.then_inc(h_pe, 1)
                    else:
                        b, k = use(step, last)
                        n = i * 4 + (U_HL + k)
                        if step[0] == "G":
                            gate(int(step[1]), int(step[2]), n, i * 16 + 32)
                        elif step[0] == "B":
                            branch(int(step[1]), int(step[2]), yC, n, i * 16 + 16)
                        else:
                            slot, h = "fqgv".index(step[0]), int(step[1])
                            project(slot, i * 16 + 80, h, b, n)

            pe.wait_ge(s_glua, WT)
            pe.wait_ge(k_free[3], U_HL)
            with pe.Fori(0, WT - 1) as i:
                head(i, NORMAL, False)
            head(WT - 1, LAST, True)
            for m, (y, u) in enumerate(((yB, U_GB), (yA, U_GA))):
                if m:
                    pe.wait_ge(h_o, WT + ONE)
                else:
                    pe.wait_ge(s_yB, WT)
                with pe.Fori(0, 4) as i:
                    for s in range(2):
                        for h in range(2):
                            gate(s, h, i * 2 + (u + s), i * 16 + 16 * (6 + 4 * m))
                        for h in range(2):
                            branch(s, h, y, i * 2 + (u + s), i * 16 + 16 * (5 + 4 * m))
            tail_pe(pe)

        @block.scalar
        def _(act):
            A = nc.scalar.activation
            ch = Chain(act, s_act)
            for one in (h_ev, e_ya, e_hTe):
                act.sem_inc(one, ONE)

            def evac(out, b, n, func=ACT.Copy, own=None, **kw):
                act.wait_ge(k_full[b], n + 1)
                if not isinstance(n, int):
                    act.sem_inc(a_go, 1)
                return A(out, ps[b][:], func, **kw).then_inc(k_free[b], 1)

            act.wait_ge(s_sp, 1)
            A(sp4[:, :, 1], sp4[:, :, 0], ACT.Exp, scale=-1.0).then_inc(s_rate, 1)
            act.wait_ge(s_s5par, 48)
            A(pt[:, DT], s5p[:, 2 * GP:3 * GP], ACT.Exp).then_inc(s_trigo, 1)
            act.wait_ge(s_trig, 1)
            A(pt[:, SN], pt[:, SN], ACT.Sin)
            A(pt[:, CS], pt[:, CS], ACT.Sin)
            for j in range(1, 9):
                ins = A(pt[:, RJ + j], pt[:, RE], ACT.Exp, scale=float(j))
            ins.then_inc(s_trigo, 1)
            for t in range(4):
                for h in range(2):
                    evac(rgx[:, t, h * HALF:(h + 1) * HALF], 2 * (t % 2) + h, U_P1 + t // 2)
            for t in range(4, 8):
                for h in range(2):
                    evac(yC[:, t - 4, h * HALF:(h + 1) * HALF], 2 * (t % 2) + h, U_P1 + t // 2, ACT.Gelu_apprx_tanh)
            for j in range(WT):
                for s in (2 * j, 2 * j + 1):
                    act.wait_ge(k_full[s % 4], U_SU + s // 4 + 1)
                    A(u_tok[:, :, s, :], ps[s % 4][:].rearrange("p (g c) -> p g c", g=G), ACT.Copy).then_inc(k_free[s % 4], 1)
                act.wait_ge(s_rgmm, j + 1)
                act.wait_ge(s_rgy, j)
                for h in range(2):
                    ins = A(rgt[:, 0, h * HALF:(h + 1) * HALF], PB4[h][:], ACT.Sigmoid, bias=chan[:, CV["ba"] + j:CV["ba"] + j + 1])
                ins.then_inc(s_rgact, 1)
                for h in range(2):
                    ins = A(rgt[:, 1, h * HALF:(h + 1) * HALF], PB4[2 + h][:], ACT.Sigmoid, bias=chan[:, CV["bx"] + j:CV["bx"] + j + 1])
                ins.then_inc(s_rgact, 1)
                act.wait_ge(s_rgact, 2 * j + 2)
                A(rgt[:, 2], rgt[:, 0], ACT.Tanh, scale=sp4[:, j, 7:8]).then_inc(s_rgsq, 1)
                act.wait_ge(s_rgsq, 2 * j + 1)
                A(rgt[:, 3], rgt[:, 2], ACT.Sqrt).then_inc(s_rgsq, 1)

            def s5_half(half):
                act.wait_ge(s_pe5, 5 * half + 1)
                act.wait_ge(s_rgy, WT)
                for q in range(4):
                    ins = A(uT[:, 4 * q:4 * q + 4, :].rearrange("p a b -> p (a b)"), PB4[q][:], ACT.Copy)
                ins.then_inc(s_ev5, 1)
                yield
                act.wait_ge(s_pe5, 5 * half + 2)
                for q in range(4):
                    ins = A(InT[:, q // 2, 4 * (q % 2):4 * (q % 2) + 4, :].rearrange("p a b -> p (a b)"), PB4[q][:], ACT.Copy)
                ins.then_inc(s_ev5, 1)
                yield
                act.wait_ge(s_pe5, 5 * half + 3)
                for q in range(4):
                    ins = A(Ksb[0:CH].rearrange("p (h a e) b -> p h e a b", h=2, e=2)[:, q % 2, q // 2],
                            PB4[q][0:CH, :].rearrange("p (a b) -> p a b", a=4), ACT.Copy)
                ins.then_inc(s_ev5, 1)
                yield

            def gelu5(half):
                for q in range(2):
                    g0 = 2 * HP * half + 8 * q
                    ins = A(ytok[:, :, g0 * CH:(g0 + 8) * CH].rearrange("p s (g c) -> p g s c", g=8), u_tok[:, g0:g0 + 8], ACT.Gelu_apprx_tanh)
                ins.then_inc(s_gelu5, 1)

            def head_evac(s, h, b, n, i):
                if i is not None:
                    act.wait_ge(*((h_F, i * 7 + 1), (h_q, i * 2 + 2), (h_q, i * 2 + 2), (h_pe, i * 5 + 1 + ONE))[s])
                evac((fN, qN, gN, vN)[s][:, h * HALF:(h + 1) * HALF], b, n, ACT.Sigmoid if s == 0 else ACT.Copy)

            def evac_head(s):
                for h in range(2):
                    head_evac(s, h, 2 * (s % 2) + h, U_H0 + s // 2, None)

            halves = s5_half(0), s5_half(1)
            for _ in range(3):
                next(halves[0])
            evac_head(0)
            evac_head(1)
            act.wait_ge(s_y5, 1)
            gelu5(0)
            next(halves[1])
            evac_head(2)
            for _ in range(2):
                next(halves[1])
            evac_head(3)
            act.wait_ge(s_y5, 2)
            gelu5(1)
            for cj in range(WT):
                act.wait_ge(s_pe5, 10 + cj + 1)
                yv = yT[:, cj, :].rearrange("p (m s) -> p s m", s=SC)
                for b in range(2):
                    ins = A(yv[:, 4 * b:4 * b + 4, :], PB4[2 * (cj % 2) + b][:].rearrange("p (s m) -> p s m", s=4), ACT.Copy)
                ins.then_inc(s_ev5, 1)
            for e in range(WT):
                act.wait_ge(s_pe5, 14 + e + 1)
                for h in range(2):
                    ins = A(glut[:, e, h * HALF:(h + 1) * HALF], PB4[2 * (e % 2) + h][:], ACT.Sigmoid,
                            bias=chan[:, CV["glub"] + e:CV["glub"] + e + 1])
                ins.then_inc(s_glua, 1)

            def gate(s, h, n, tile, branch):
                j, before = tile
                act.wait_ge(g_mix, before * 2 + ONE)
                evac(sig[:, h, :], h, n, ACT.Sigmoid, bias=chan[:, bass.ds(j + (CV["bgate"] + KD * branch), 1)]
                     if not isinstance(j, int) else chan[:, CV["bgate"] + KD * branch + j:CV["bgate"] + KD * branch + j + 1])

            def head(i, sched, last):
                for step in sched:
                    if step == "V":
                        act.wait_ge(k_free[2], i * 4 + U_HL)
                        act.wait_ge(k_free[3], i * 4 + U_HL)
                        act.wait_ge(k_free[1], i * 4 + U_HL)
                        act.wait_ge(k_free[0], i * 4 + U_HL)
                        act.wait_ge(h_qF, i * 8 + ONE)
                        act.sem_inc(a_go, 1)
                        A(qs[:], qN, ACT.Silu).then_inc(h_q, 1)
                        A(dyn(yA, i), gN, ACT.Silu).then_inc(h_q, 1)
                        act.wait_ge(h_pe, i * 5 + 1 + ONE)
                        for b in range(2):
                            ins = A(vtok[:, 4 * b:4 * b + 4, :].rearrange("p a b -> p (a b)"), ps[4 + b][:], ACT.Copy)
                        ins.then_inc(h_ev, 1)
                    elif step == "KT":
                        act.wait_ge(h_pe, i * 5 + 2 + ONE)
                        act.wait_ge(h_qF, i * 8 + 8 + ONE)
                        for b in range(2):
                            ins = A(tmp[:, b * HALF:(b + 1) * HALF], ps[4 + b][:], ACT.Copy)
                        ins.then_inc(h_ev, 1)
                    elif step == "O":
                        act.wait_ge(h_pe, i * 5 + 4 + ONE)
                        for b in range(2):
                            ins = A(tmp[:, b * HALF:(b + 1) * HALF], ps[6 + b][:], ACT.Square)
                        ins.then_inc(h_ev, 1)
                    elif step == "M":
                        act.wait_ge(h_pe, i * 5 + 5 + ONE)
                        for b in range(2):
                            ins = A(St[:, b * HALF:(b + 1) * HALF], ps[4 + b][:], ACT.Sqrt, bias=eps[:, 1:2])
                        ins.then_inc(h_ev, 1)
                    elif step[0] in "fqgv":
                        b, k = use(step, last)
                        head_evac("fqgv".index(step[0]), int(step[1]), b, i * 4 + (U_HL + k), i)
                    elif step[0] == "G":
                        b, k = use(step, last)
                        t = i * 2 + int(step[1])
                        gate(int(step[1]), int(step[2]), i * 4 + (U_HL + k), (t, t), 2)

            act.wait_ge(s_yB, WT)
            with act.Fori(0, WT - 1) as i:
                head(i, NORMAL, False)
            head(WT - 1, LAST, True)
            for m, (br, u) in enumerate(((1, U_GB), (0, U_GA))):
                with act.Fori(0, 4) as i:
                    for s in range(2):
                        for h in range(2):
                            gate(s, h, i * 2 + (u + s), (i * 2 + s, i * 2 + (s + KD + KD * m)), br)
            tail_act(act)

        @block.vector
        def _(dve):
            V = nc.vector
            tt, ts, stt = V.tensor_tensor, V.tensor_scalar, V.scalar_tensor_tensor
            ch = Chain(dve, s_dve)
            for one in (h_o, h_qF, g_mix, e_yd, e_hTl, e_hm):
                dve.sem_inc(one, ONE)
            L = ch.link
            N = ch.add

            dve.wait_ge(s_par, 16)
            lam = chan[:, CV["lam"]:CV["lam"] + WT]
            L(ts(sp4[:, :, 0], lam, -1.0, None, ALU.mult))
            N(ts(sp4[:, :, 7], sp4[:, :, 0], 0.0, None, ALU.max))
            tt(sp4[:, :, 0], sp4[:, :, 0], lam, ALU.max).then_inc(s_sp, 1)
            dve.wait_ge(s_rate, 1)
            z, w, w2, acc = (sp4[:, :, n] for n in (1, 2, 3, 4))
            L(ts(w, z, 2.0, None, ALU.add))
            L(V.reciprocal(w2, w))
            L(tt(w, z, w2, ALU.mult))
            L(tt(w2, w, w, ALU.mult))
            L(ts(acc, w2, 1.0 / 17, 1.0 / 15, ALU.mult, ALU.add))
            for n in (13, 11, 9, 7, 5, 3, 1):
                L(tt(acc, acc, w2, ALU.mult))
                L(ts(acc, acc, 1.0 / n, None, ALU.add))
            L(tt(acc, acc, w, ALU.mult))
            L(stt(acc, acc, 2.0, sp4[:, :, 7], ALU.mult, ALU.add))
            L(ts(sp4[:, :, 7], acc, 4.0, None, ALU.mult))
            lbl = chan[:, CV["lb"]:CV["lb"] + WT]
            L(tt(lb1[:, 0], lbl, lbl, ALU.subtract))
            L(ts(lb1[:, 0], lb1[:, 0], 1.0, None, ALU.add))
            L(tt(lb1[:, 0], lb1[:, 0], lb1[:, 0], ALU.subtract))
            L(ts(lb1[:, 1], lb1[:, 0], -1.0, 1.0, ALU.mult, ALU.add))

            p = lambda n: pt[:, n]
            dve.wait_ge(s_trigo, 1)
            are, aim = s5p[:, 0:GP], s5p[:, GP:2 * GP]
            N(tt(p(RE), are, p(DT), ALU.mult))
            L(tt(p(TH), aim, p(DT), ALU.mult))
            L(ts(p(T0), p(TH), float(1 / (2 * np.pi)), None, ALU.mult))
            L(V.tensor_copy(pti[:], p(T0)))
            L(V.tensor_copy(p(T0), pti[:]))
            L(stt(p(TH), p(T0), -TP1, p(TH), ALU.mult, ALU.add))
            L(stt(p(TH), p(T0), -TP2, p(TH), ALU.mult, ALU.add))
            L(stt(p(TH), p(T0), -TP3, p(TH), ALU.mult, ALU.add))
            L(ts(p(SN), p(TH), PI_IN, -PI_IN, ALU.min, ALU.max))
            L(ts(p(CS), p(SN), -1.0, None, ALU.mult))
            L(tt(p(CS), p(CS), p(SN), ALU.max))
            ts(p(CS), p(CS), -1.0, PI / 2, ALU.mult, ALU.add).then_inc(s_trig, 1)
            N(V.memset(p(UR), 1.0))
            N(V.memset(p(UI), 0.0))
            N(V.memset(p(RJ), 1.0))
            dve.wait_ge(s_trigo, 2)
            N(V.tensor_copy(p(UR + 1), p(CS)))
            L(V.tensor_copy(p(UI + 1), p(SN)))

            def bc(x, shape):
                return x.broadcast_to(shape)

            def cmul(outr, outi, ar, ai, br, bi, t, shape=None, first=None):
                N(tt(outr, ar, br, ALU.mult))
                L(tt(t, ai, bi, ALU.mult))
                L(tt(outr, outr, t, ALU.subtract))
                N(tt(outi, ar, bi, ALU.mult))
                L(tt(t, ai, br, ALU.mult))
                L(tt(outi, outi, t, ALU.add))

            scr = Hs[:, :, :, :].rearrange("p a b m -> p (a b m)")

            def pwr(dst, src, n, by):
                b3 = [P, n, GP]
                fr, fi = (bc(pt[:, x + by:x + by + 1, :], b3) for x in (UR, UI))
                cmul(pt[:, UR + dst:UR + dst + n], pt[:, UI + dst:UI + dst + n], pt[:, UR + src:UR + src + n],
                     pt[:, UI + src:UI + src + n], fr, fi, scr[:, 0:n * GP].rearrange("p (n g) -> p n g", n=n))

            pwr(2, 1, 1, 1)
            pwr(3, 1, 2, 2)
            pwr(5, 1, 4, 4)
            N(tt(pt[:, PR:PR + 9], pt[:, RJ:RJ + 9], pt[:, UR:UR + 9], ALU.mult))
            L(tt(pt[:, PIM:PIM + 9], pt[:, RJ:RJ + 9], pt[:, UI:UI + 9], ALU.mult))
            for s in range(SC):
                N(V.tensor_copy(p(PRR + s), p(PR + SC - 1 - s)))
                N(V.tensor_copy(p(PIR + s), p(PIM + SC - 1 - s)))
            N(ts(p(NR), p(PR + 1), -1.0, None, ALU.add))
            N(tt(p(T0), are, are, ALU.mult))
            L(tt(p(T1), aim, aim, ALU.mult))
            L(tt(p(DEN), p(T0), p(T1), ALU.add))
            N(V.reciprocal(p(DEN), p(DEN)))
            N(tt(p(QR), p(NR), are, ALU.mult))
            N(tt(p(T0), p(PIM + 1), aim, ALU.mult))
            N(tt(p(QI), p(PIM + 1), are, ALU.mult))
            L(tt(p(T1), p(NR), aim, ALU.mult))
            N(tt(p(QR), p(QR), p(T0), ALU.add))
            L(tt(p(QI), p(QI), p(T1), ALU.subtract))
            N(tt(p(QR), p(QR), p(DEN), ALU.mult))
            L(tt(p(QI), p(QI), p(DEN), ALU.mult))
            sh = [P, GP, CH]
            qr, qi = (bc(p(x).unsqueeze(2), sh) for x in (QR, QI))
            cmul(Bb[:, 0], Bb[:, 1], s5w[:, 0], s5w[:, 1], qr, qi, scr[:, 0:GP * CH].rearrange("p (g c) -> p g c", g=GP))

            def tables(half):
                gs = slice(HP * half, HP * half + HP)

                def view(x, n):
                    return pt[:, x:x + n, gs].rearrange("p j g -> p g j")

                sh = [P, HP, 9, CH]
                pr, pi = (bc(view(x, 9).unsqueeze(3), sh) for x in (PR, PIM))
                cr, ci = (bc(s5w[:, x, gs].unsqueeze(2), sh) for x in (2, 3))
                t = scr[:, 0:HP * 9 * CH].rearrange("p (g j c) -> p g j c", g=HP, j=9)
                for g in range(HP):
                    q = slice(g, g + 1)
                    N(tt(OutR[:, g], cr[:, g], pr[:, g], ALU.mult))
                    N(tt(t[:, g], ci[:, g], pi[:, g], ALU.mult))
                ch.wait()
                L(tt(OutR[:], OutR[:], t, ALU.subtract))
                for g in range(HP):
                    N(tt(OutI[:, g], cr[:, g], pi[:, g], ALU.mult))
                    N(tt(t[:, g], ci[:, g], pr[:, g], ALU.mult))
                ch.wait()
                L(stt(OutI[:].rearrange("p g j c -> p (g j c)"), OutI[:].rearrange("p g j c -> p (g j c)"), -1.0,
                      t.rearrange("p g j c -> p (g j c)"), ALU.mult, ALU.subtract))
                sh = [P, HP, SC, CH]
                pr, pi = (bc(view(x, SC).unsqueeze(3), sh) for x in (PRR, PIR))
                br, bi = (bc(Bb[:, x, gs].unsqueeze(2), sh) for x in (0, 1))
                t = scr[:, 0:HP * P].rearrange("p (g s c) -> p g s c", g=HP, s=SC)
                for o, (x0, x1), op in ((InR, (pr, pi), ALU.subtract), (InI, (pi, pr), ALU.add)):
                    for g in range(HP):
                        N(tt(o[:, g], br[:, g], x0[:, g], ALU.mult))
                        N(tt(t[:, g], bi[:, g], x1[:, g], ALU.mult))
                    ch.wait()
                    ins = tt(o[:], o[:], t, op)
                    L(ins) if o is InR else ins.then_inc(s_tab, 1)
                dve.wait_ge(s_tab, half + 1)
                N(V.memset(ER[:, :, 0:1], 1.0))
                N(V.memset(EI[:, :, 0:1], 0.0))
                L(V.tensor_copy(pt[:, CR:CR + 1, gs], pt[:, UR + 8:UR + 9, gs]))
                L(V.tensor_copy(pt[:, CI:CI + 1, gs], pt[:, UI + 8:UI + 9, gs]))
                n = 1
                while n < NM:
                    sh = [P, HP, n]
                    cr, ci = (bc(pt[:, x, gs].unsqueeze(2), sh) for x in (CR, CI))
                    cmul(ER[:, :, n:2 * n], EI[:, :, n:2 * n], ER[:, :, 0:n], EI[:, :, 0:n], cr, ci,
                         R8[:].rearrange("p g m -> p (g m)")[:, 0:HP * n].rearrange("p (g m) -> p g m", g=HP))
                    if 2 * n < NM:
                        a_, b_, c_ = (pt[:, x, gs] for x in (T0, CR, CI))
                        N(tt(pt[:, T1, gs], b_, c_, ALU.mult))
                        L(tt(a_, c_, c_, ALU.mult))
                        L(tt(b_, b_, b_, ALU.mult))
                        L(tt(b_, b_, a_, ALU.subtract))
                        L(ts(c_, pt[:, T1, gs], 2.0, None, ALU.mult))
                    n *= 2
                L(V.tensor_copy(R8[:], bc(pt[:, RJ + 8, gs].unsqueeze(2), [P, HP, NM])))
                L(V.memset(R8[:, :, 0:1], 0.0))

            tables(0)

            def conv(j):
                dve.wait_ge(k_free[2 * (j % 2) + 1], U_P1 + j // 2 + 1)
                dve.wait_ge(k_free[2 * (j % 2)], U_P1 + j // 2 + 1)
                if j >= 2:
                    dve.wait_ge(s_rgmm, j - 1)
                o = xc[:, j % 2]
                tap = lambda k: chan[:, CV["convw"] + 4 * k + j:CV["convw"] + 4 * k + j + 1]
                L(ts(o, rgx[:, j], tap(3), chan[:, CV["convb"] + j:CV["convb"] + j + 1], ALU.mult, ALU.add))
                for k in (2, 1, 0):
                    d = 3 - k
                    ins = stt(o[:, d:T], rgx[:, j, 0:T - d], tap(k), o[:, d:T], ALU.mult, ALU.add)
                    L(ins) if k else ins.then_inc(s_conv, 1)

            def recur(j):
                i_, s_, q_, r_ = rgt[:, 1], rgt[:, 2], rgt[:, 3], rgt[:, 0]
                dve.wait_ge(s_rgact, 2 * j + 2)
                dve.wait_ge(s_conv, j + 1)
                L(tt(i_, i_, xc[:, j % 2], ALU.mult))
                dve.wait_ge(s_rgsq, 2 * j + 2)
                L(ts(s_, s_, 1.0, None, ALU.add))
                L(V.reciprocal(r_, s_))
                L(stt(q_, q_, 2.0, r_, ALU.mult, ALU.mult))
                L(tt(i_, i_, q_, ALU.mult))
                L(ts(r_, r_, 2.0, -1.0, ALU.mult, ALU.add))
                L(V.tensor_tensor_scan(s_, r_, i_, 0.0, ALU.mult, ALU.add))
                dve.wait_ge(k_free[2 * (j % 2) + 1], U_P1 + 2 + j // 2 + 1)
                dve.wait_ge(k_free[2 * (j % 2)], U_P1 + 2 + j // 2 + 1)
                tt(yC[:, j], s_, yC[:, j], ALU.mult).then_inc(s_rgy, 1)
                dve.wait_ge(s_rgy, j + 1)

            conv(0)
            conv(1)
            for j in range(WT):
                recur(j)
                if j + 2 < WT:
                    conv(j + 2)

            def s5_half(half):
                dve.wait_ge(s_pe5, 5 * half + 4)
                for b in range(2):
                    gs = slice(4 * b, 4 * b + 4)
                    ir, ii = (PB4[2 * x + b][:].rearrange("p (g m) -> p g m", g=4)[:, :, 0:NM - 1] for x in range(2))
                    er, ei = ER[:, gs, 1:NM], EI[:, gs, 1:NM]
                    wr, wi = (x[:, gs, 1:NM] for x in (WR, WI))
                    dve.wait_ge(s_toep, 16 * SC * (half + 1))
                    t = Hs[:, 0, gs, 1:NM]
                    N(tt(wr, er, ir, ALU.mult))
                    L(tt(t, ei, ii, ALU.mult))
                    L(tt(wr, wr, t, ALU.add))
                    N(tt(wi, er, ii, ALU.mult))
                    L(tt(t, ei, ir, ALU.mult))
                    L(tt(wi, wi, t, ALU.subtract))
                N(V.memset(WR[:, :, 0:1], 0.0))
                L(V.memset(WI[:, :, 0:1], 0.0))
                r8 = R8[:].rearrange("p g m -> p (g m)")
                for w_ in (WR, WI):
                    f = w_.rearrange("p g m -> p (g m)")
                    L(V.tensor_tensor_scan(f, r8, f, 0.0, ALU.mult, ALU.add))
                hr, hi = Hs[:, 0], Hs[:, 1]
                N(tt(hr, ER[:], WR, ALU.mult))
                L(tt(R8[:], EI[:], WI, ALU.mult))
                L(tt(hr, hr, R8[:], ALU.subtract))
                N(tt(hi, ER[:], WI, ALU.mult))
                L(tt(R8[:], EI[:], WR, ALU.mult))
                tt(hi, hi, R8[:], ALU.add).then_inc(s_H, 1)
                g0 = 2 * HP * half
                d = s5d[:, :].rearrange("p (g c) -> p g c", g=G)
                L(tt(u_tok[:, g0:g0 + 2 * HP], u_tok[:, g0:g0 + 2 * HP], bc(d[:, g0:g0 + 2 * HP].unsqueeze(2), [P, 2 * HP, SC, CH]), ALU.mult))
                dve.wait_ge(s_pe5, 5 * half + 5)
                for b in range(4):
                    o = u_tok[:, g0:g0 + 2 * HP].rearrange("p (h a e) s c -> p h e a (s c)", h=2, e=2)[:, b % 2, b // 2]
                    ins = tt(o, o, PB4[b][:].rearrange("p (a n) -> p a n", a=4), ALU.add)
                    if b < 3:
                        N(ins)
                ins.then_inc(s_y5, 1)

            s5_half(0)
            tables(1)
            s5_half(1)
            dve.wait_ge(s_pe5, 18)
            for e in range(WT):
                dve.wait_ge(s_glua, e + 1)
                tt(yB[:, e], glut[:, e], yT[:, e], ALU.mult).then_inc(s_yB, 1)

            def mixin(s, h, n, tile, first):
                j, before = tile
                dve.wait_ge(g_mix, before * 2 + ONE)
                dve.wait_ge(k_full[2 + h], n + 1)
                dve.wait_ge(k_free[h], n + 1)
                o = mixT[:, :, h * HALF:(h + 1) * HALF]
                o = o[:, j] if isinstance(j, int) else o[:, bass.ds(j, 1)].rearrange("p o n -> p (o n)")
                if first:
                    tt(o, sig[:, h], ps[2 + h][:], ALU.mult).then_inc(g_mix, 1)
                    dve.wait_ge(g_mix, before * 2 + (h + 1) + ONE)
                    dve.sem_inc(k_free[2 + h], 1)
                else:
                    tt(sig[:, h], sig[:, h], ps[2 + h][:], ALU.mult).then_inc(k_free[2 + h], 1)
                    dve.wait_ge(k_free[2 + h], n + 1)
                    tt(o, o, sig[:, h], ALU.add).then_inc(g_mix, 1)

            odd = lambda x, h: x[:, :].rearrange("p (b j) -> p b j", j=2 * h)[:, :, h:2 * h]

            def head(i, sched, last):
                K = i * 8
                for step in sched:
                    if step == "V":
                        dve.wait_ge(k_free[0], i * 4 + U_HL)
                        dve.wait_ge(k_free[1], i * 4 + U_HL)
                        dve.wait_ge(h_kG, i * 7 + ONE)
                        dve.wait_ge(h_o, i + ONE)
                        sc = (lb1[:, 1], lb1[:, 0])
                        sc = [x[:, i:i + 1] if isinstance(i, int) else x[:, bass.ds(i, 1)] for x in sc]
                        ts(Fd[:], fN, sc[0], sc[1], ALU.mult, ALU.add).then_inc(h_F, 1)
                        dve.wait_ge(h_F, i * 7 + 1)
                        ts(kk[:], Fd[:], -1.0, 1.0, ALU.mult, ALU.add).then_inc(h_k, 1)
                        dve.wait_ge(h_q, i * 2 + 1)
                        tt(qF[:, 0:HALF].rearrange("p (b j) -> p b j", j=1), odd(qs, 1), odd(Fd, 1), ALU.mult).then_inc(h_qF, 1)
                        dve.wait_ge(h_qF, K + 1 + ONE)
                    elif step[0] == "L":
                        l = int(step[1])
                        if l < 7:
                            h = LEVELS[l]
                            Fv = Fd[:, :].rearrange("p (b j) -> p b j", j=2 * h)
                            dve.wait_ge(h_G, i * 7 + (l + 1))
                            ins = tt(Fv[:, :, h:], Fv[:, :, h:], bc(Fv[:, :, h - 1:h], [P, T // (2 * h), h]), ALU.mult)
                            if l < 6:
                                ins.then_inc(h_F, 1)
                                dve.wait_ge(h_F, i * 7 + (l + 2))
                                h2 = 2 * h
                                if l > 0:
                                    dve.wait_ge(h_lvl, K + (l + 1))
                                qc = qF[:, ((l + 1) % 2) * HALF:((l + 1) % 2 + 1) * HALF].rearrange("p (b j) -> p b j", j=h2)
                                tt(qc, odd(qs, h2), odd(Fd, h2), ALU.mult).then_inc(h_qF, 1)
                            else:
                                L(ins)
                        dve.wait_ge(h_lvl, K + (l + 1))
                        if l == 0:
                            for b in range(2):
                                v = lambda x: x.rearrange("p (n t) -> p n t", n=4)
                                ins = tt(v(St[:, b * HALF:(b + 1) * HALF]), v(ps[4 + b][:]), bc(diag[:, :].unsqueeze(1), [P, 4, C]), ALU.mult)
                                if b == 0:
                                    N(ins)
                            ins.then_inc(h_lfree, 1)
                            dve.wait_ge(h_lfree, K + 1)
                        else:
                            h = LEVELS[l - 1]
                            v = lambda x: x.rearrange("p (n t) -> p n t", n=NCH)
                            tt(v(tmp[:, 0:HALF]), v(ps[4 + l % 2][:]), bc(mask[:, l - 1].unsqueeze(1), [P, NCH, C // 2]), ALU.mult).then_inc(h_lfree, 1)
                            dve.wait_ge(h_lfree, K + (l + 1))
                            L(tt(odd(St, h), odd(St, h), tmp[:, 0:HALF].rearrange("p (b j) -> p b j", j=h), ALU.add))
                        if l == 7:
                            tt(qF[:], qs[:], Fd[:], ALU.mult).then_inc(h_qF, 1)
                    elif step == "KV":
                        dve.wait_ge(h_pe, i * 5 + 3 + ONE)
                        for n in range(NCH - 1):
                            kv = ps[4 + n // 4][:, (n % 4) * P:(n % 4 + 1) * P]
                            if n == 0:
                                L(V.tensor_copy(Sall[:, 1], kv))
                            else:
                                ins = stt(Sall[:, n + 1], Sall[:, n], Fd[:, n * C + C - 1:n * C + C], kv, ALU.mult, ALU.add)
                                L(ins) if n < NCH - 2 else ins.then_inc(h_S, 1)
                    elif step == "M":
                        dve.wait_ge(h_ev, i * 4 + 4 + ONE)
                        L(V.reciprocal(St[:], St[:]))
                        nw = chan[:, CV["nw"] + i:CV["nw"] + i + 1] if isinstance(i, int) else chan[:, bass.ds(i + CV["nw"], 1)]
                        for b in range(2):
                            ins = stt(tmp[:, b * HALF:(b + 1) * HALF], ps[6 + b][:], nw, St[:, b * HALF:(b + 1) * HALF], ALU.mult, ALU.mult)
                            N(ins)
                        ch.wait()
                        dve.wait_ge(h_q, i * 2 + 2)
                        tt(dyn(yA, i), tmp[:], dyn(yA, i), ALU.mult).then_inc(h_o, 1)
                    elif step[0] == "B":
                        b, k = use(step, last)
                        t = i * 2 + int(step[1])
                        mixin(int(step[1]), int(step[2]), i * 4 + (U_HL + k), (t, t), True)

            per = 1 + 1 + 7 + 6 + 3
            with dve.Fori(0, WT - 1) as i:
                ch.enter(i, per)
                head(i, NORMAL, False)
                ch.leave(WT - 1)
            head(WT - 1, LAST, True)
            for m, u in enumerate((U_GB, U_GA)):
                with dve.Fori(0, 4) as i:
                    for s in range(2):
                        for h in range(2):
                            mixin(s, h, i * 2 + (u + s), (i * 2 + s, i * 2 + (s + KD + KD * m)), False)
            tail_dve(dve, ch)


_OUTS = [((1, T, D), "float32")]


def _layout(i):
    f = lambda n: np.asarray(i[n])
    ch = lambda n, k: f(n)[0].reshape(k, P).T
    rows = lambda *names: np.ascontiguousarray(np.broadcast_to(np.stack([f(n)[0] for n in names]), (P, len(names), D)))
    pair = lambda x: x.reshape(GP, 2, NS, -1).transpose(1, 2, 0, 3).reshape(P, GP, -1)
    exp = np.empty((E + 1, P, NW), np.float32)
    for e, (w1, w3, w2) in enumerate([(f("sh_w1"), f("sh_w3"), f("sh_w2")), (f("exp_w1")[0], f("exp_w3")[0], f("exp_w2")[0])]):
        n = w1.shape[0]
        to = exp[:1] if e == 0 else exp[1:]
        hid = to[:, :, :KD * 2 * EH].reshape(n, P, KD, 2 * EH)
        hid[..., :EH] = w1.reshape(n, KD, P, EH).transpose(0, 2, 1, 3)
        hid[..., EH:] = w3.reshape(n, KD, P, EH).transpose(0, 2, 1, 3)
        to[:, :, :KD * 2 * EH] = hid.reshape(n, P, -1)
        to[:, :, KD * 2 * EH:] = w2.reshape(n, 2, P, D).transpose(0, 2, 1, 3).reshape(n, P, -1)
    x = f("x")[0]
    return {
        "x": x,
        "xT": x.T.reshape(KD, P, T).transpose(1, 0, 2),
        "w_in": f("w_in")[0].reshape(KD, P, -1, P).transpose(2, 1, 0, 3),
        "w_branch": f("w_branch")[0].reshape(3, WT, P, KD, P).transpose(0, 3, 2, 1, 4).reshape(3 * KD, P, WT, P),
        "w_out": f("w_out")[0].reshape(KD, P, D).transpose(1, 0, 2),
        "glu_w": f("s5_glu_w")[0].reshape(WT, P, W).transpose(1, 0, 2).reshape(P, WT * W),
        "rg_w": np.stack([f("rg_wa")[0], f("rg_wx")[0]]).transpose(2, 0, 1, 3).reshape(P, KD, P),
        "chan": np.concatenate([ch("hgrn_lb_logits", 4), ch("hgrn_norm_w", 4), ch("s5_glu_b", 4),
                                f("rg_conv_w")[0].reshape(4 * 4, P).T, ch("rg_conv_b", 4), ch("rg_ba", 4), ch("rg_bx", 4),
                                ch("rg_lambda", 4), ch("b_gate", 24)], axis=1),
        "s5p": np.concatenate([pair(f("s5_a_re")[0])[..., 0], pair(f("s5_a_im")[0])[..., 0],
                               pair(np.broadcast_to(f("s5_log_dt")[0][:, None], (G, NS)))[..., 0]], axis=1),
        "s5w": np.stack([pair(f("s5_b_re")[0]), pair(f("s5_b_im")[0]), pair(f("s5_c_re")[0].transpose(0, 2, 1)),
                         pair(f("s5_c_im")[0].transpose(0, 2, 1))], axis=1),
        "s5d": np.broadcast_to(f("s5_d")[0], (P, W)),
        "ln1": rows("ln1_g", "ln1_b"),
        "ln2": rows("ln2_g", "ln2_b"),
        "rb": np.broadcast_to(f("router_bias")[0], (P, E)),
        "router_w": f("router_w")[0].reshape(KD, P, E).transpose(1, 0, 2),
        "experts": exp,
    }


def kernel(**inputs):
    import concourse.bacc as bacc
    from concourse.bass_utils import run_bass_kernel_spmd

    nc = bacc.Bacc("TRN2", target_bir_lowering=False, num_devices=1)
    arrays = {f"in_{n}": np.ascontiguousarray(v) for n, v in _layout(inputs).items()}
    aps = {n[3:]: nc.dram_tensor(n, v.shape, mybir.dt.from_np(v.dtype), kind="ExternalInput").ap() for n, v in arrays.items()}
    out = nc.dram_tensor("out", (T, D), F32, kind="ExternalOutput").ap()
    build(nc, aps, out)
    r = run_bass_kernel_spmd(nc, [arrays], core_ids=[0])
    return r.results[0]["out"].reshape(1, T, D)
```
